# Optimizing a Trainium2 kernel written in Bass

```python
import math
import jax
import jax.numpy as jnp
from jax import lax
import numpy as np

D_MODEL = 2048
BATCH = 1
SEQ = 512
DEPTH = 1

D_MIX = D_MODEL
GROUP_W = D_MIX // 4

S5_W = GROUP_W
S5_CH = 16
S5_GROUPS = S5_W // S5_CH
S5_STATE = 64
S5_DT_MIN = 1e-3
S5_DT_MAX = 1e-1

LRU_W = GROUP_W
LRU_HEADS = 8
LRU_HEAD_DIM = LRU_W // LRU_HEADS
LRU_C = 8.0
CONV_K = 4

RW_W = GROUP_W
RW_HEAD_DIM = 64
RW_HEADS = RW_W // RW_HEAD_DIM
RW_DECAY_LORA = 32
RW_AAA_LORA = 32
RW_GATE_LORA = 96
RW_COLS = 3 * RW_W + RW_DECAY_LORA + RW_AAA_LORA + RW_GATE_LORA
RW_LN_EPS = 64e-5

SSD_W = GROUP_W
SSD_HEAD_DIM = 64
SSD_HEADS = SSD_W // SSD_HEAD_DIM
SSD_GROUPS = 2
SSD_STATE = 128
SSD_CHUNK = 128
SSD_XBC = SSD_W + 2 * SSD_GROUPS * SSD_STATE

IN_COLS = S5_W + 2 * LRU_W + RW_COLS + SSD_W + SSD_XBC + SSD_HEADS

MOE_GROUPS = 8
MOE_PER_GROUP = 8
MOE_EXPERTS = MOE_GROUPS * MOE_PER_GROUP
MOE_TOPK = 2
MOE_DFF = 384
MOE_BLOCK = 128

NORM_EPS = 1e-6

kernel_name = 'hybrid_s5_rglru_rwkv7_ssd_hmoe'

def rms_norm(x, g):
    xf = x.astype(jnp.float32)
    y = xf * lax.rsqrt(jnp.mean(xf * xf, axis=-1, keepdims=True) + NORM_EPS)
    return (y * g.astype(jnp.float32)).astype(x.dtype)

def _split(x, sizes):
    idx = np.cumsum(np.array(sizes))[:-1].tolist()
    return jnp.split(x, idx, axis=-1)

def causal_conv(x, w, b):
    k = w.shape[0]
    s = x.shape[1]
    xp = jnp.pad(x, ((0, 0), (k - 1, 0), (0, 0)))
    y = xp[:, 0:s] * w[0]
    for i in range(1, k):
        y = y + xp[:, i:i + s] * w[i]
    return y + b

def token_shift(x):
    return jnp.pad(x, ((0, 0), (1, 0), (0, 0)))[:, :-1]

def _complex_affine_combine(e1, e2):
    a1r, a1i, b1r, b1i = e1
    a2r, a2i, b2r, b2i = e2
    return (a2r * a1r - a2i * a1i,
            a2r * a1i + a2i * a1r,
            a2r * b1r - a2i * b1i + b2r,
            a2r * b1i + a2i * b1r + b2i)

def _affine_combine(e1, e2):
    a1, b1 = e1
    a2, b2 = e2
    return a1 * a2, a2 * b1 + b2

def s5_mixer(u, lam_re, lam_im, b_re, b_im, c_re, c_im, d_skip, log_dt, w_glu, b_glu, gain):
    f32 = jnp.float32
    bsz, s, _ = u.shape
    uf = u.astype(f32)
    dt = jnp.exp(log_dt.astype(f32))[:, None]
    lr, li = lam_re.astype(f32), lam_im.astype(f32)
    mag = jnp.exp(lr * dt)
    abar_re, abar_im = mag * jnp.cos(li * dt), mag * jnp.sin(li * dt)
    den = lr * lr + li * li
    q_re = ((abar_re - 1.0) * lr + abar_im * li) / den
    q_im = (abar_im * lr - (abar_re - 1.0) * li) / den
    br, bi = b_re.astype(f32), b_im.astype(f32)
    bbar_re = q_re[..., None] * br - q_im[..., None] * bi
    bbar_im = q_re[..., None] * bi + q_im[..., None] * br
    ug = uf.reshape(bsz, s, S5_GROUPS, S5_CH)
    bu_re = jnp.einsum('bsgh,gnh->bsgn', ug, bbar_re)
    bu_im = jnp.einsum('bsgh,gnh->bsgn', ug, bbar_im)
    a_re = jnp.broadcast_to(abar_re, bu_re.shape)
    a_im = jnp.broadcast_to(abar_im, bu_re.shape)
    _, _, st_re, st_im = lax.associative_scan(
        _complex_affine_combine, (a_re, a_im, bu_re, bu_im), axis=1)
    y = (jnp.einsum('bsgn,ghn->bsgh', st_re, c_re.astype(f32))
         - jnp.einsum('bsgn,ghn->bsgh', st_im, c_im.astype(f32)))
    y = y.reshape(bsz, s, S5_W) + d_skip.astype(f32) * uf
    y = jax.nn.gelu(y)
    y = y * jax.nn.sigmoid(y @ w_glu.astype(f32) + b_glu.astype(f32))
    return rms_norm(y, gain).astype(u.dtype)

def rglru_mixer(xb, gate, conv_w, conv_b, wa, ba, wx, bx, a_param, gain):
    f32 = jnp.float32
    bsz, s, _ = xb.shape
    xc = causal_conv(xb.astype(f32), conv_w.astype(f32), conv_b.astype(f32))
    xh = xc.reshape(bsz, s, LRU_HEADS, LRU_HEAD_DIM)
    r = jax.nn.sigmoid(jnp.einsum('bshi,hij->bshj', xh, wa.astype(f32)).reshape(bsz, s, LRU_W) + ba.astype(f32))
    i = jax.nn.sigmoid(jnp.einsum('bshi,hij->bshj', xh, wx.astype(f32)).reshape(bsz, s, LRU_W) + bx.astype(f32))
    log_a = -LRU_C * r * jax.nn.softplus(-a_param.astype(f32))
    a = jnp.exp(log_a)
    u = jnp.sqrt(-jnp.expm1(2.0 * log_a)) * (i * xc)
    _, hstate = lax.associative_scan(_affine_combine, (a, u), axis=1)
    y = hstate * jax.nn.gelu(gate.astype(f32))
    return rms_norm(y, gain).astype(xb.dtype)

def rwkv7_mixer(p, mu, w0, w2, a0, a2, g2, k_k, k_a, r_k, ln_w, ln_b):
    f32 = jnp.float32
    bsz, s, _ = p.shape
    pf = p.astype(f32)
    pf = pf + (token_shift(pf) - pf) * mu.astype(f32)
    r, k, v, xw, xa, xg = _split(pf, [RW_W, RW_W, RW_W, RW_DECAY_LORA, RW_AAA_LORA, RW_GATE_LORA])
    w_log = -jax.nn.softplus(-(w0.astype(f32) + jnp.tanh(xw) @ w2.astype(f32))) - 0.5
    decay = jnp.exp(-jnp.exp(w_log))
    a = jax.nn.sigmoid(a0.astype(f32) + xa @ a2.astype(f32))
    g = jax.nn.sigmoid(xg) @ g2.astype(f32)
    kk = (k * k_k.astype(f32)).reshape(bsz, s, RW_HEADS, RW_HEAD_DIM)
    kk = kk * lax.rsqrt(jnp.maximum(jnp.sum(kk * kk, axis=-1, keepdims=True), 1e-24))
    k = k * (1.0 + (a - 1.0) * k_a.astype(f32))

    def heads(t):
        return t.reshape(bsz, s, RW_HEADS, RW_HEAD_DIM)

    r_h, w_h, k_h, v_h, a_h = heads(r), heads(decay), heads(k), heads(v), heads(a)
    xs = tuple(jnp.moveaxis(t, 1, 0) for t in (r_h, w_h, k_h, v_h, kk, a_h))

    def step(state, inp):
        r_t, w_t, k_t, v_t, kk_t, a_t = inp
        sa = jnp.einsum('bhvk,bhk->bhv', state, -kk_t)
        state = (state * w_t[:, :, None, :]
                 + sa[..., None] * (kk_t * a_t)[:, :, None, :]
                 + v_t[..., None] * k_t[:, :, None, :])
        return state, jnp.einsum('bhvk,bhk->bhv', state, r_t)

    s0 = jnp.zeros((bsz, RW_HEADS, RW_HEAD_DIM, RW_HEAD_DIM), f32)
    _, o = lax.scan(step, s0, xs)
    o = jnp.moveaxis(o, 0, 1)
    mean = jnp.mean(o, axis=-1, keepdims=True)
    var = jnp.mean(jnp.square(o - mean), axis=-1, keepdims=True)
    o = ((o - mean) * lax.rsqrt(var + RW_LN_EPS)).reshape(bsz, s, RW_W)
    o = o * ln_w.astype(f32) + ln_b.astype(f32)
    bonus = jnp.sum(r_h * k_h * r_k.astype(f32), axis=-1, keepdims=True) * v_h
    y = (o + bonus.reshape(bsz, s, RW_W)) * g
    return y.astype(p.dtype)

def ssd_chunked(x, a, bmat, cmat):
    bsz, s, _, _ = x.shape
    nc, ln, hg = s // SSD_CHUNK, SSD_CHUNK, SSD_HEADS // SSD_GROUPS
    x = x.reshape(bsz, nc, ln, SSD_GROUPS, hg, SSD_HEAD_DIM)
    a = a.reshape(bsz, nc, ln, SSD_GROUPS, hg)
    bmat = bmat.reshape(bsz, nc, ln, SSD_GROUPS, SSD_STATE)
    cmat = cmat.reshape(bsz, nc, ln, SSD_GROUPS, SSD_STATE)
    a_cs = jnp.cumsum(a, axis=2)
    seg = a_cs[:, :, :, None] - a_cs[:, :, None, :]
    mask = jnp.tril(jnp.ones((ln, ln), dtype=bool))[None, None, :, :, None, None]
    decay = jnp.exp(jnp.where(mask, seg, -jnp.inf))
    scores = jnp.einsum('bclgn,bcsgn->bclsg', cmat, bmat)
    y_diag = jnp.einsum('bclsgh,bcsghp->bclghp', scores[..., None] * decay, x)
    decay_to_end = jnp.exp(a_cs[:, :, -1:] - a_cs)
    states = jnp.einsum('bclgn,bclghp->bcghpn', bmat, x * decay_to_end[..., None])
    chunk_decay = jnp.exp(a_cs[:, :, -1])

    def chunk_step(h, inp):
        st, dec = inp
        return h * dec[..., None, None] + st, h

    h0 = jnp.zeros((bsz, SSD_GROUPS, hg, SSD_HEAD_DIM, SSD_STATE), x.dtype)
    _, h_in = lax.scan(chunk_step, h0, (jnp.moveaxis(states, 1, 0), jnp.moveaxis(chunk_decay, 1, 0)))
    h_in = jnp.moveaxis(h_in, 0, 1)
    y_off = jnp.einsum('bclgn,bcghpn->bclghp', cmat, h_in) * jnp.exp(a_cs)[..., None]
    return (y_diag + y_off).reshape(bsz, s, SSD_HEADS, SSD_HEAD_DIM)

def ssd_mixer(z, xbc, dt_raw, conv_w, conv_b, dt_bias, a_log, d_skip, norm_w):
    f32 = jnp.float32
    bsz, s, _ = z.shape
    xbc = jax.nn.silu(causal_conv(xbc.astype(f32), conv_w.astype(f32), conv_b.astype(f32)))
    xs, bmat, cmat = _split(xbc, [SSD_W, SSD_GROUPS * SSD_STATE, SSD_GROUPS * SSD_STATE])
    xh = xs.reshape(bsz, s, SSD_HEADS, SSD_HEAD_DIM)
    dt = jax.nn.softplus(dt_raw.astype(f32) + dt_bias.astype(f32))
    a_coef = -jnp.exp(a_log.astype(f32))
    y = ssd_chunked(xh * dt[..., None], dt * a_coef,
                    bmat.reshape(bsz, s, SSD_GROUPS, SSD_STATE),
                    cmat.reshape(bsz, s, SSD_GROUPS, SSD_STATE))
    y = (y + xh * d_skip.astype(f32)[:, None]).reshape(bsz, s, SSD_W)
    y = rms_norm(y * jax.nn.silu(z.astype(f32)), norm_w)
    return y.astype(z.dtype)

def hier_moe(h, w_group, b_group, w_expert, b_expert, w1, w3, w2):
    bsz, s, d = h.shape
    n = bsz * s
    xt = h.reshape(n, d)
    g_logits = (xt @ w_group + b_group).astype(jnp.float32)
    g_probs = jax.nn.softmax(g_logits, axis=-1)
    g_idx = jnp.argmax(g_logits, axis=-1)
    g_gate = jnp.take_along_axis(g_probs, g_idx[:, None], axis=-1)
    e_logits = (xt @ w_expert + b_expert).astype(jnp.float32).reshape(n, MOE_GROUPS, MOE_PER_GROUP)
    e_logits = jnp.take_along_axis(e_logits, g_idx[:, None, None], axis=1)[:, 0]
    top_v, top_i = lax.top_k(e_logits, MOE_TOPK)
    gate = g_gate * jax.nn.softmax(top_v, axis=-1)
    expert_id = g_idx[:, None] * MOE_PER_GROUP + top_i
    na = n * MOE_TOPK
    eid = expert_id.reshape(na)
    tok = jnp.repeat(jnp.arange(n), MOE_TOPK)
    wgt = gate.reshape(na)
    order = jnp.argsort(eid)
    eid_s, tok_s, wgt_s = eid[order], tok[order], wgt[order]
    counts = jnp.bincount(eid, length=MOE_EXPERTS)
    starts = jnp.cumsum(counts) - counts
    padded = (counts + MOE_BLOCK - 1) // MOE_BLOCK * MOE_BLOCK
    pends = jnp.cumsum(padded)
    pstarts = pends - padded
    dest = pstarts[eid_s] + (jnp.arange(na) - starts[eid_s])
    cap = -(-(na + MOE_EXPERTS * (MOE_BLOCK - 1)) // MOE_BLOCK) * MOE_BLOCK
    nb = cap // MOE_BLOCK
    xpad = jnp.zeros((cap, d), h.dtype).at[dest].set(xt[tok_s])
    blk_e = jnp.minimum(jnp.searchsorted(pends, jnp.arange(nb) * MOE_BLOCK, side='right'), MOE_EXPERTS - 1)

    def block_ffn(args):
        xb, e = args
        return (jax.nn.silu(xb @ w1[e]) * (xb @ w3[e])) @ w2[e]

    ypad = lax.map(block_ffn, (xpad.reshape(nb, MOE_BLOCK, d), blk_e)).reshape(cap, d)
    y = jnp.zeros((n, d), h.dtype).at[tok_s].add(ypad[dest] * wgt_s[:, None].astype(h.dtype))
    return y.reshape(bsz, s, d)

def setup_inputs(seed: int = 0) -> dict:
    key = jax.random.key(seed)
    keys = iter(list(jax.random.split(key, 96)))
    f32 = jnp.float32
    L = DEPTH

    def nrm(shape, scale):
        return scale * jax.random.normal(next(keys), shape, f32)

    def unif(shape, lo, hi):
        return jax.random.uniform(next(keys), shape, f32, lo, hi)

    def gain(shape):
        return 1.0 + nrm(shape, 0.02)

    lru_a = unif((L, LRU_W), 0.9, 0.999) ** (1.0 / LRU_C)
    ssd_dt = jnp.exp(unif((L, SSD_HEADS), math.log(1e-3), math.log(1e-1)))
    return {
        'x': nrm((BATCH, SEQ, D_MODEL), 1.0),
        'norm_mix': gain((L, D_MODEL)),
        'w_in': nrm((L, D_MODEL, IN_COLS), D_MODEL ** -0.5),
        'w_out': nrm((L, D_MIX, D_MODEL), 0.5 * D_MIX ** -0.5),
        's5_lambda_re': -0.5 + nrm((L, S5_GROUPS, S5_STATE), 0.01),
        's5_lambda_im': jnp.broadcast_to(math.pi * jnp.arange(S5_STATE, dtype=f32), (L, S5_GROUPS, S5_STATE)),
        's5_b_re': nrm((L, S5_GROUPS, S5_STATE, S5_CH), (2 * S5_CH) ** -0.5),
        's5_b_im': nrm((L, S5_GROUPS, S5_STATE, S5_CH), (2 * S5_CH) ** -0.5),
        's5_c_re': nrm((L, S5_GROUPS, S5_CH, S5_STATE), 2.0 * S5_STATE ** -0.5),
        's5_c_im': nrm((L, S5_GROUPS, S5_CH, S5_STATE), 2.0 * S5_STATE ** -0.5),
        's5_d': nrm((L, S5_W), 0.5),
        's5_log_dt': unif((L, S5_GROUPS), math.log(S5_DT_MIN), math.log(S5_DT_MAX)),
        's5_w_glu': nrm((L, S5_W, S5_W), S5_W ** -0.5),
        's5_b_glu': nrm((L, S5_W), 0.01),
        's5_gain': gain((L, S5_W)),
        'lru_conv_w': nrm((L, CONV_K, LRU_W), CONV_K ** -0.5),
        'lru_conv_b': nrm((L, LRU_W), 0.01),
        'lru_wa': nrm((L, LRU_HEADS, LRU_HEAD_DIM, LRU_HEAD_DIM), LRU_HEAD_DIM ** -0.5),
        'lru_ba': nrm((L, LRU_W), 0.01),
        'lru_wx': nrm((L, LRU_HEADS, LRU_HEAD_DIM, LRU_HEAD_DIM), LRU_HEAD_DIM ** -0.5),
        'lru_bx': nrm((L, LRU_W), 0.01),
        'lru_a_param': jnp.log(lru_a) - jnp.log1p(-lru_a),
        'lru_gain': gain((L, LRU_W)),
        'rw_mu': unif((L, RW_COLS), 0.0, 1.0),
        'rw_w0': unif((L, RW_W), -6.0, 1.0),
        'rw_w2': nrm((L, RW_DECAY_LORA, RW_W), 0.1),
        'rw_a0': nrm((L, RW_W), 0.1),
        'rw_a2': nrm((L, RW_AAA_LORA, RW_W), 0.1),
        'rw_g2': nrm((L, RW_GATE_LORA, RW_W), RW_GATE_LORA ** -0.5),
        'rw_k_k': 0.85 + nrm((L, RW_W), 0.02),
        'rw_k_a': 1.0 + nrm((L, RW_W), 0.02),
        'rw_r_k': nrm((L, RW_HEADS, RW_HEAD_DIM), 0.1),
        'rw_ln_w': gain((L, RW_W)),
        'rw_ln_b': nrm((L, RW_W), 0.01),
        'ssd_conv_w': nrm((L, CONV_K, SSD_XBC), CONV_K ** -0.5),
        'ssd_conv_b': nrm((L, SSD_XBC), 0.01),
        'ssd_dt_bias': ssd_dt + jnp.log(-jnp.expm1(-ssd_dt)),
        'ssd_a_log': jnp.log(unif((L, SSD_HEADS), 1.0, 16.0)),
        'ssd_d': 1.0 + nrm((L, SSD_HEADS), 0.1),
        'ssd_norm_w': gain((L, SSD_W)),
        'norm_ffn': gain((L, D_MODEL)),
        'moe_w_group': nrm((L, D_MODEL, MOE_GROUPS), D_MODEL ** -0.5),
        'moe_b_group': nrm((L, MOE_GROUPS), 0.01),
        'moe_w_expert': nrm((L, D_MODEL, MOE_EXPERTS), D_MODEL ** -0.5),
        'moe_b_expert': nrm((L, MOE_EXPERTS), 0.01),
        'moe_w1': nrm((L, MOE_EXPERTS, D_MODEL, MOE_DFF), D_MODEL ** -0.5),
        'moe_w3': nrm((L, MOE_EXPERTS, D_MODEL, MOE_DFF), D_MODEL ** -0.5),
        'moe_w2': nrm((L, MOE_EXPERTS, MOE_DFF, D_MODEL), MOE_DFF ** -0.5),
        'norm_final': gain((D_MODEL,)),
    }

def reference(x, norm_mix, w_in, w_out,
              s5_lambda_re, s5_lambda_im, s5_b_re, s5_b_im, s5_c_re, s5_c_im,
              s5_d, s5_log_dt, s5_w_glu, s5_b_glu, s5_gain,
              lru_conv_w, lru_conv_b, lru_wa, lru_ba, lru_wx, lru_bx, lru_a_param, lru_gain,
              rw_mu, rw_w0, rw_w2, rw_a0, rw_a2, rw_g2, rw_k_k, rw_k_a, rw_r_k, rw_ln_w, rw_ln_b,
              ssd_conv_w, ssd_conv_b, ssd_dt_bias, ssd_a_log, ssd_d, ssd_norm_w,
              norm_ffn, moe_w_group, moe_b_group, moe_w_expert, moe_b_expert,
              moe_w1, moe_w3, moe_w2, norm_final):
    for l in range(DEPTH):
        h = rms_norm(x, norm_mix[l])
        proj = h @ w_in[l]
        u_s5, x_lru, g_lru, p_rw, z_ssd, xbc_ssd, dt_ssd = _split(
            proj, [S5_W, LRU_W, LRU_W, RW_COLS, SSD_W, SSD_XBC, SSD_HEADS])
        y_s5 = s5_mixer(u_s5, s5_lambda_re[l], s5_lambda_im[l], s5_b_re[l], s5_b_im[l],
                        s5_c_re[l], s5_c_im[l], s5_d[l], s5_log_dt[l],
                        s5_w_glu[l], s5_b_glu[l], s5_gain[l])
        y_lru = rglru_mixer(x_lru, g_lru, lru_conv_w[l], lru_conv_b[l], lru_wa[l], lru_ba[l],
                            lru_wx[l], lru_bx[l], lru_a_param[l], lru_gain[l])
        y_rw = rwkv7_mixer(p_rw, rw_mu[l], rw_w0[l], rw_w2[l], rw_a0[l], rw_a2[l], rw_g2[l],
                           rw_k_k[l], rw_k_a[l], rw_r_k[l], rw_ln_w[l], rw_ln_b[l])
        y_ssd = ssd_mixer(z_ssd, xbc_ssd, dt_ssd, ssd_conv_w[l], ssd_conv_b[l], ssd_dt_bias[l],
                          ssd_a_log[l], ssd_d[l], ssd_norm_w[l])
        mixed = jnp.concatenate([y_s5, y_lru, y_rw, y_ssd], axis=-1)
        x = x + (mixed @ w_out[l]).astype(x.dtype)
        h = rms_norm(x, norm_ffn[l])
        x = x + hier_moe(h, moe_w_group[l], moe_b_group[l], moe_w_expert[l], moe_b_expert[l],
                         moe_w1[l], moe_w3[l], moe_w2[l]).astype(x.dtype)
    return rms_norm(x, norm_final)


_drawn_inputs = setup_inputs


def setup_inputs(seed=0):
    import zlib

    import numpy as np

    out = dict(_drawn_inputs(seed))
    spreads = {}
    factors = {'s5_lambda_re': 8.0,
     's5_b_glu': 8.0,
     's5_gain': 5.408,
     'lru_ba': 8.0,
     'lru_bx': 8.0,
     'lru_gain': 4.277,
     'rw_w2': 5.21,
     'rw_a0': 5.195,
     'rw_k_k': 7.658,
     'rw_k_a': 5.877,
     'rw_ln_w': 8.0,
     'rw_ln_b': 8.0,
     'ssd_conv_b': 4.798,
     'ssd_d': 3.86,
     'ssd_norm_w': 5.519,
     'norm_ffn': 2.973,
     'moe_b_group': 4.711,
     'moe_b_expert': 6.864,
     'norm_final': 2.854}
    for name, (base, spread) in spreads.items():
        noise = np.random.default_rng([zlib.crc32(name.encode()), seed]).standard_normal(out[name].shape)
        drawn = base * np.exp(spread * noise) if base else spread * noise
        out[name] = jnp.asarray(drawn.astype(out[name].dtype))
    for name, factor in factors.items():
        out[name] = (out[name] * factor).astype(out[name].dtype)
    return out
```

```python
from contextlib import ExitStack

import concourse.bass as bass
from concourse import mybir

P = 128
F32 = mybir.dt.float32
I32 = mybir.dt.int32
ALU = mybir.AluOpType
ACT = mybir.ActivationFunctionType
AX = mybir.AxisListType.X

T = 512
D = 2048
NC = D // P
NTT = T // P
W = D // 4
WT = W // P
EPS = 1e-6
MAGIC = 1.5 * 2.0 ** 23

S5_G, S5_N, S5_H = 32, 64, 16
NPAIR = S5_G // 2
FINE, COARSE = 32, 16
RH, RD = 8, 64
LW, LA, LG = 32, 32, 96
RC = 64
NRC = T // RC
INV_SQRT_E = 0.6065306597126334
SH, SN, SC = 8, 128, 128
NSC = T // SC
NG, NPG, NE, FF = 8, 8, 64, 384
B = 64
NBLK = (2 * T + NE * (B - 1)) // B + 1
NROW = 4096
FC = FF // P

C_S5, C_XL, C_GL, C_R = 0, 512, 1024, 1536
C_LORA = C_R + 3 * W
C_XG = C_LORA + LW + LA
C_Z = C_XG + LG
C_XBC = C_Z + W
C_DT = C_XBC + 1024
IN_COLS = C_DT + SH


class Steps:

    def __init__(self, eng, sem):
        self.eng, self.sem, self.n = eng, sem, 0
        self.last = None

    def do(self, ins):
        ins.then_inc(self.sem, 1)
        self.n += 1
        self.last = (self.sem, self.n)

    def tell(self, ins, sem, value):
        ins.then_inc(sem, 1)
        self.last = (sem, value)

    def settle(self):
        self.eng.wait_ge(*self.last)


def param_rows():
    a, b = {}, {}
    n = 0
    for name, rows in (("s5_d", 4), ("s5_b_glu", 4), ("s5_gain", 4), ("lru_conv_w", 16), ("lru_conv_b", 4),
                       ("lru_ba", 4), ("lru_bx", 4), ("lru_a_param", 4), ("lru_gain", 4), ("rw_mu", 12),
                       ("rw_w0", 4), ("rw_a0", 4), ("rw_k_k", 4), ("rw_k_a", 4), ("rw_r_k", 4),
                       ("rw_ln_w", 4), ("rw_ln_b", 4), ("ssd_norm_w", 4)):
        a[name] = (n, rows)
        n += rows
    n = 0
    for name, rows in (("ssd_conv_w", 32), ("ssd_conv_b", 8), ("norm_mix", 16)):
        b[name] = (n, rows)
        n += rows
    return a, b


PA, PB = param_rows()
MU_LORA = 56


def build(nc, I, out):
    with ExitStack() as ctx:
        def sb(name, shape, dt=F32):
            return ctx.enter_context(nc.sbuf_tensor(name, shape, dt))

        def sem(name):
            return ctx.enter_context(nc.semaphore(name))

        big = sb("big", [P, 96, 512])
        hT = big[:, 0:16, :]
        ring = [big[:, 16 + 8 * i:24 + 8 * i, :].rearrange("p a n -> p (a n)").rearrange("p (k n) -> p k n", k=NC)
                for i in range(2)]
        proj = big[:, 32:70, :]
        U5, XL, GL = proj[:, 0:4, :], proj[:, 4:8, :], proj[:, 8:12, :]
        R_, K_, V_ = proj[:, 12:16, :], proj[:, 16:20, :], proj[:, 20:24, :]
        LO = proj[:, 24:26, :]
        Z_, XBC = proj[:, 26:30, :], proj[:, 30:38, :]
        xs = proj[:, 22:38, :].rearrange("p a n -> p (a n)").rearrange("p (i d) -> p i d", i=NTT)
        s5tab = proj[:, 20:24, :]
        rawB = proj[:, 16, :].rearrange("p (r g h) -> p r g h", r=2, g=NPAIR)
        dupC = proj[:, 18:20, :].rearrange("p r (q u n) -> p r q u n", q=WT, u=2)
        Gin = [proj[:, 12:16, :], big[:, 78:82, :]]
        ptmp = proj[:, 24:26, :]
        wk2 = big[:, 88:96, :]
        wk = big[:, 70:78, :]
        wglu = big[:, 78:82, :]
        lruW = big[:, 82:84, :].rearrange("p a (t c) -> p a t c", t=WT)
        loraW = big[:, 84:86, :]
        s5C = big[:, 86:88, :].rearrange("p r (g c) -> p r g c", g=NPAIR)
        s5G = big[:, 88:96, :].rearrange("p a n -> p (a n)").rearrange("p (r g c) -> p r g c", r=2, g=NPAIR)

        ident = sb("ident", [P, P])
        ones = sb("ones", [P, P])
        prmA, prmB, prmC = proj[:, 8, 0:P], proj[:, 8, P:2 * P], proj[0:48, 8, 2 * P:3 * P]
        colA = sb("colA", [P, P])
        colB = sb("colB", [P, P])
        colC = sb("colC", [P, 48])
        ldt = sb("ldt", [NPAIR, 2])
        st = sb("st", [P, 64])
        wdt = sb("wdt", [P, NC, SH])
        s5v = sb("s5v", [P, 16, NPAIR])
        misc = sb("misc", [P, 16])
        zero = sb("zero", [P, 1])
        halfpi = sb("halfpi", [P, 1])
        epsb = sb("epsb", [P, 1])
        tk = sb("tk", [P, FINE + COARSE])
        cosF, sinF = (proj[:, i:i + 2, :].rearrange("p a n -> p (a n)")[:, 0:NPAIR * (FINE + COARSE)]
                      .rearrange("p (g k) -> p g k", g=NPAIR) for i in (26, 28))
        lsp = sb("lsp", [P, 6, WT])
        ssdt = sb("ssdt", [P, NSC, SH])

        ps = [ctx.enter_context(nc.psum_tensor(f"ps{i}", [P, 512], F32)) for i in range(8)]

        def A(name, i=0):
            r, _ = PA[name]
            return colA[:, r + i:r + i + 1]

        def Bc(name, i=0):
            r, _ = PB[name]
            return colB[:, r + i:r + i + 1]

        KR = big[:, 40:48, :].rearrange("p (a j) n -> p a j n", a=2)
        XT_, XD, YT, XE = wk2[:, 0:4, :], wk2[:, 4:8, :], wk[:, 4:8, :], wk[:, 0:4, :]
        BT = big[:, 82:84, :].rearrange("p a n -> p (a n)").rearrange("p (c g n) -> p c g n", c=NSC, g=2)
        DM = big[:, 40:44, :].rearrange("p (u a) n -> p u (a n)", u=2).rearrange("p u (h l) -> p u h l", h=SH)
        SH_ = big[:, 86:88, :]
        BH, Gt, BV, Ot = big[:, 78:82, :], big[:, 92:96, :], big[:, 88:92, :], big[:, 20:24, :]
        moved = big[0:64, 0:20, :].rearrange("p (a j) n -> p a j n", a=5)
        rwb = [[24, 25, 26, 27, 29, 31, 62, 63, 64], [70, 71, 72, 73, 75, 77, 65, 66, 67]]

        def rb(c, k):
            i = rwb[c % 2][k]
            if k in (3, 4):
                return big[0:64, i:i + 2, :].rearrange("p a n -> p (a n)").rearrange("p (h a t) -> p h a t", h=RH, a=2)
            return big[0:64, i, :].rearrange("p (h t) -> p h t", h=RH)

        RHs, RY, RU = (big[0:64, i, :].rearrange("p (h t) -> p h t", h=RH) for i in (68, 69, 82))
        cbc = sb("cbc", [P, 4, SH])
        tri = sb("tri", [P, P])
        tris = sb("tris", [P, P])
        maskneg = sb("maskneg", [P, P])
        sds = sb("sds", [P, 8, NSC * SH])
        blk64 = sb("blk64", [P, P])
        rmask = sb("rmask", [64, 2, 64])
        emask = proj[0:64, 17, 0:448].rearrange("p (i t) -> p i t", i=7)
        lvm = sb("lvm", [64, 6, 64])
        wce = sb("wce", [P, WT, NRC])
        wco = sb("wco", [64, WT, NRC])

        sg, ra, kk, cum, cumx, wcum, winv, wprev = (big[:, 4 * i:4 * i + 4, :] for i in range(8))
        knr = wk[:, 4:8, :]

        mixed = [U5[:, q, :] for q in range(WT)] + [XL[:, q, :] for q in range(WT)] + [V_[:, q, :] for q in range(WT)] \
            + [Z_[:, q, :] for q in range(WT)]

        def wide(i, n=4):
            return big[:, i:i + n, :].rearrange("p a n -> p (a n)")

        x2 = [wide(4 * i) for i in range(NTT)]
        woslab = [big[:, 16:32, :], big[:, 62:78, :]]
        h2p = [wide(78 + 4 * i) for i in range(NTT)]
        gffn = wide(44)
        h2T = big[:, 16:32, :]
        wr = wide(40)[:, 0:NC * (NG + NE)].rearrange("p (c n) -> p c n", c=NC)
        W13 = [[wide(36 * k + 12 * r, 12).rearrange("p (c f) -> p c f", c=NC) for r in range(2)] for k in range(2)]
        W2 = [wide(36 * k + 24, 12).rearrange("p (c n) -> p c n", c=FC) for k in range(2)]
        xg = [wide(72 + 4 * k)[0:B, :] for k in range(2)]
        yb = [wide(80 + 4 * k)[0:B, :] for k in range(2)]
        xT = [wide(88 + 2 * k, 2).rearrange("p (c t) -> p c t", c=NC) for k in range(2)]
        hid = [big[:, 92 + k, 0:FC * B].rearrange("p (c t) -> p c t", c=FC) for k in range(2)]
        sil = [big[:, 92 + k, 256:256 + FC * B] for k in range(2)]
        rt = wide(62, 12)

        hd = nc.dram_tensor("h_rows", (T, D), F32, kind="Internal").ap()
        x2d = nc.dram_tensor("x2_rows", (T, D), F32, kind="Internal").ap()
        yd = nc.dram_tensor("y_rows", (2 * T, D), F32, kind="Internal").ap()
        tokd = nc.dram_tensor("tok_rows", (NBLK * B, 1), I32, kind="Internal").ap()

        def rv(i, *shape):
            n = 1
            for z in shape:
                n *= z
            v_ = rt[:, 320 * i:320 * i + n]
            names = "abc"[:len(shape)]
            return v_ if len(shape) == 1 else v_.rearrange("p (" + " ".join(names) + ") -> p " + " ".join(names),
                                                            **{k: z for k, z in zip(names, shape)})

        tokv = rt[:, 5700:5708].bitcast(I32).rearrange("p (k i) -> p k i", k=2)
        desti = rt[:, 5720:5728].bitcast(I32).rearrange("p (k i) -> p k i", k=2)
        tini = rt[0:NBLK, 5760:5760 + B].bitcast(I32)
        tabi = rt[0:NBLK, 5840:5840 + B].bitcast(I32)
        tabf = rt[0:NBLK, 5920:5920 + B]
        gate = sb("gate", [P, 2, NTT])
        idxg = sb("idxg", [B, NBLK + 2], I32)
        idxs = sb("idxs", [B, NBLK + 2], I32)
        rowi = sb("rowi", [1, P + 2], I32)
        gix, six = ([sb(f"{n}{k}", [B, 1], I32) for k in range(2)] for n in ("gix", "six"))

        fills, at = {}, {}

        def plan(name, bank):
            at[name] = (bank, fills.get(bank, 0))
            fills[bank] = fills.get(bank, 0) + 1

        plan("dt", 6)
        plan("cs", 7)
        for i in range(NTT):
            plan(("xt", i), 2 + i)
        for i in range(2):
            plan(("bt", i), 6 + i)
        for c in range(NSC):
            plan(("row", c, 0), 2)
            plan(("row", c, 1), 3)
            plan(("score", c), 4)
            plan(("state", c), 7)
            if c:
                plan(("off", c), 6)
            plan(("diag", c), 5)
        for q in range(WT):
            plan(("yt", q), 2 + q)
        plan("rms_s", 6)
        for q in range(WT):
            for r in range(3):
                plan(("lora", q, r), 2 + (3 * q + r) % 6)
        for q in range(WT):
            plan(("kn", q), 2 + q)
        for q in range(WT):
            plan(("bonus", q), 2 + (q + 4) % 6)
        LEV = 6
        for c0 in range(0, NRC, 2):
            for c in (c0, c0 + 1):
                for k in range(3):
                    plan(("tm", c, k), k)
                for k in range(4):
                    plan(("gram", c, k), 3 + k)
            for lv in range(LEV):
                for c in (c0, c0 + 1):
                    plan(("t", c, lv), 3 * (c % 2))
                for c in (c0, c0 + 1):
                    if lv and lv < LEV - 1:
                        plan(("u", c, lv), 3 * (c % 2) + 1)
                    if lv:
                        plan(("ut", c, lv), 3 * (c % 2) + 2)
            for c in (c0, c0 + 1):
                plan(("y", c), 6)
                plan(("un", c), 7)
                plan(("h", c), 0)
                plan(("o", c), 1)
        for q in range(WT):
            plan(("mean", q), 2 + q)
        for q in range(WT):
            plan(("var", q), 2 + q)

        for n in range(4 * NTT):
            plan(("out", n), n % 2)
        for m in range(4 * NTT):
            plan(("h2", m), 2 + m % 4)
        plan("logit", 6)
        plan("cum", 7)
        plan("row", 0)
        plan("tab", 1)

        x2_in, x2_ok, ssx_ok, msx_ok, rsx_ok = (sem(n) for n in ("x2_in", "x2_ok", "ssx_ok", "msx_ok", "rsx_ok"))
        wo_in = [sem("wo0_in"), sem("wo1_in")]
        gain_in, h2_ok, wr_in, spill = sem("gain_in"), sem("h2_ok"), sem("wr_in"), sem("spill")
        ri_ok, re_ok, oh_ok, bl_ok, dest_ok, rowi_ok = (sem(n) for n in ("ri_ok", "re_ok", "oh_ok", "bl_ok", "dest_ok", "rowi_ok"))
        tab_io, tabf_ok, idx_ok = (sem(n) for n in ("tab_io", "tabf_ok", "idx_ok"))
        w1_in, w2_in, xg_in, y_out = ([sem(f"{n}{k}") for k in range(2)] for n in ("w13_in", "w2_in", "xg_in", "y_out"))
        gcp_ok, y_ok = ([sem(f"{n}{k}") for k in range(2)] for n in ("gcp_ok", "y_ok"))
        xT_ok, xT2_ok, up_ok, down_ok, sil_ok, hid_ok, xz_ok = (
            sem(n) for n in ("xT_ok", "xT2_ok", "up_ok", "down_ok", "sil_ok", "hid_ok", "xz_ok"))
        fin_ok, fss_ok, frs_ok, fms_ok, out_ok = (
            sem(n) for n in ("fin_ok", "fss_ok", "frs_ok", "fms_ok", "out_ok"))
        full = [sem(f"bank{i}_full") for i in range(8)]
        free = [sem(f"bank{i}_free") for i in range(8)]
        cbc_in, dtx_ok, dte_ok, adt_ok = sem("cbc_in"), sem("dtx_ok"), sem("dte_ok"), sem("adt_ok")
        csd_ok, cse_ok = sem("csd_ok"), sem("cse_ok")
        sconv_ok, silu_ok, z_ok = sem("sconv_ok"), sem("silu_ok"), sem("z_ok")
        xe_ok, seg_ok, segx_ok = (sem(n) for n in ("xe_ok", "seg_ok", "segx_ok"))
        ssq2_ok = sem("ssq2_ok")
        mask_ok = sem("mask_ok")
        lo_ok, lot_ok, ksq_ok, kn_ok, knr_ok = (sem(n) for n in ("lo_ok", "lot_ok", "ksq_ok", "kn_ok", "knr_ok"))
        cum_ok, dec_ok, rk_ok, rw_ok, moved_in = (sem(n) for n in ("cum_ok", "dec_ok", "rk_ok", "rw_ok", "moved_in"))
        gram_ok, of_ok, x_ok = (sem(n) for n in ("gram_ok", "of_ok", "x_ok"))
        rh_ok, ro_ok, cen_ok = (sem(n) for n in ("rh_ok", "ro_ok", "cen_ok"))
        var_ok, rwy_ok = sem("var_ok"), sem("rwy_ok")
        x_in = [sem(f"x_in{i}") for i in range(NTT)]
        prm_in = sem("prm_in")
        s5_in = sem("s5_in")
        w_in_slot = [sem("slab0_in"), sem("slab1_in")]
        wdt_in = sem("wdt_in")
        wglu_in, lruw_in, lora_in = sem("wglu_in"), sem("lruw_in"), sem("lora_in")
        dve_s, act_s, pool_s = sem("dve_step"), sem("act_step"), sem("pool_step")
        const_ok = sem("const_ok")
        zero_ok = sem("zero_ok")
        ssq_ok = sem("ssq_ok")
        ms_ok, rs_ok = sem("ms_ok"), sem("rs_ok")
        h_ok = sem("h_ok")
        tr_ok, tr_used = sem("tr_ok"), sem("tr_used")
        prm_tr, prm_col = sem("prm_tr"), sem("prm_col")
        gin_zero, bbar_ok, gin_ok = sem("gin_zero"), sem("bbar_ok"), sem("gin_ok")
        g_tr, g_got = sem("g_tr"), sem("g_got")
        ldt_in, ldt_ok, s5_col = sem("ldt_in"), sem("ldt_ok"), sem("s5_col")
        dt_ok, lrdt_ok, mag_ok = sem("dt_ok"), sem("lrdt_ok"), sem("mag_ok")
        phase_ok, trig_ok = sem("phase_ok"), sem("trig_ok")
        tab_ok, tab_used = sem("tab_ok"), sem("tab_used")
        bu_ok, bu_used, st_ok, st_used = sem("bu_ok"), sem("bu_used"), sem("st_ok"), sem("st_used")
        y_used, gelu_ok = sem("y_used"), sem("gelu_ok")
        mm_ok, mm_used = sem("mm_ok"), sem("mm_used")
        sq_ok = sem("sq_ok")
        conv_ok, spa_ok, spe_ok = sem("conv_ok"), sem("spa_ok"), sem("spe_ok")
        sp_ok, ta_ok, m2_ok, m_ok = sem("sp_ok"), sem("ta_ok"), sem("m2_ok"), sem("m_ok")
        mix_ok = sem("mix_ok")
        proj_ok, proj_got = sem("proj_ok"), sem("proj_got")

        SW = 256
        slabs = [(C_S5 + SW * i, SW) for i in range(C_R // SW)] + [(C_Z + SW * i, SW) for i in range((C_DT - C_Z) // SW)] \
            + [(C_LORA, LW + LA + LG)] + [(C_R + SW * i, SW) for i in range(3 * W // SW)]
        tiles = []
        for s, (c0, wd) in enumerate(slabs):
            parts = [(0, P), (P, P)] if wd == SW else [(0, LW + LA), (LW + LA, LG)]
            for j, (c, w) in enumerate(parts):
                dest = c0 // P if c0 < C_LORA else (24 if c0 < C_Z else 26 + (c0 - C_Z) // P)
                tiles.append((s, c, w, dest + j))
        NT = len(tiles)
        proj_at = {d: n + 1 for n, (_, _, _, d) in enumerate(tiles)}

        U_GLU, U_RMS5, U_LRU, U_RMSL = 0, 4, 5, 13

        def ph(k):
            return wk[:, 2 * k:2 * k + 2, :].rearrange("p a n -> p (a n)")[:, 0:NPAIR * (FINE + COARSE)]\
                .rearrange("p (g k) -> p g k", g=NPAIR)

        def flat(x):
            return x.rearrange("p h t -> p (h t)")

        xtp_ok = sem("xtp_ok")
        fin_in = [sem("fin0_in"), sem("fin1_in")]
        passed = sem("passed")
        rbias = wide(94, 1)[:, 0:NG + NE]

        def wait_y_out(eng, r, k):
            if not isinstance(r, int) or r > 0:
                eng.wait_ge(y_out[k], 16 * r)

        def fbuf(i, j):
            return wide(12 * (i % 2) + 4 * j)

        gfin = wide(24)

        def OC(c, lv):
            return LEV * (c - c % 2) + 2 * lv + c % 2 + 1

        def XC(c, k):
            return (2 * LEV - 1) * (c - c % 2) + (4 * (k - 1) + 2 * (c % 2) + 2 if k < LEV else 4 * (LEV - 1) + c % 2 + 1)

        block = ctx.enter_context(nc.Block())

        @block.sync
        def _(sp):
            for i in range(NTT):
                sp.dma_start(xs[:, i, :], I["x"][0, P * i:P * (i + 1), :]).then_inc(x_in[i], 16)
            wv = I["w_in"][0].rearrange("(c p) n -> p c n", p=P)
            for s, (c0, wd) in enumerate(slabs):
                if s == 5:
                    sp.wait_ge(g_tr, 8)
                    sp.dma_start(wglu, I["s5_w_glu"][0].rearrange("(k p) n -> p k n", p=P)).then_inc(wglu_in, 16)
                if s >= 2:
                    sp.wait_ge(proj_ok, max(n + 1 for n, t in enumerate(tiles) if t[0] == s - 2))
                sp.dma_start(ring[s % 2][:, :, 0:wd], wv[:, :, c0:c0 + wd]).then_inc(w_in_slot[s % 2], 16)
            sp.wait_ge(rw_ok, 5)
            for a, src in enumerate((KR[:, 0], KR[:, 1], BH, K_, V_)):
                sp.dma_start(moved[:, a], src[64:128]).then_inc(moved_in, 16)
            sp.dma_start(wco[:], wce[64:128]).then_inc(moved_in, 16)
            sp.wait_ge(ro_ok, 2 * NRC)
            for i in range(NTT):
                sp.dma_start(x2[i], I["x"][0, P * i:P * (i + 1), :]).then_inc(x2_in, 16)
            wov = I["w_out"][0].rearrange("(c p) n -> p c n", p=P)
            sp.wait_ge(rwy_ok, WT)
            for n in range(4):
                if n >= 2:
                    b, i = at[("out", NTT * (n - 2) + 3)]
                    sp.wait_ge(full[b], i + 1)
                sp.dma_start(woslab[n % 2], wov[:, :, 512 * n:512 * n + 512]).then_inc(wo_in[n % 2], 16)
            for w, o in (("moe_w_group", 0), ("moe_w_expert", NG)):
                v_ = I[w][0].rearrange("(p c) n -> p c n", c=NC)
                sp.dma_start(wr[:, :, o:o + v_.shape[2]], v_).then_inc(wr_in, 16)
            for i in range(NTT):
                sp.wait_ge(x2_ok, 4 * NTT)
                sp.dma_start(x2d[P * i:P * i + P, :], x2[i]).then_inc(spill, 16)
                sp.wait_ge(h2_ok, i + 1)
                sp.dma_start(hd[P * i:P * i + P, :], h2p[i]).then_inc(spill, 16)
            sp.wait_ge(spill, 16 * 2 * NTT)
            sp.wait_ge(rowi_ok, 1)
            sp.wait_ge(idx_ok, 1)
            npairs = sp.value_load(rowi[0:1, P:P + 1], min_val=1, max_val=NBLK // 2)

            def load(r, k, first):
                e = sp.value_load(rowi[0:1, bass.ds(2 * r + k, 1)], min_val=0, max_val=NE - 1)
                if not first:
                    sp.wait_ge(up_ok, 2 * r + k - 1)
                for w, name in enumerate(("moe_w1", "moe_w3")):
                    sp.dma_start(W13[k][w], I[name][0][bass.ds(e, 1)].rearrange("e (p c) f -> p (e c) f", c=NC)).then_inc(w1_in[k], 16)
                if not first:
                    sp.wait_ge(down_ok, 8 * r + 4 * k - 4)
                sp.dma_start(W2[k], I["moe_w2"][0][bass.ds(e, 1)].rearrange("e (c p) n -> p (e c) n", p=P)).then_inc(w2_in[k], 16)

            load(0, 0, True)
            load(0, 1, True)
            with sp.Fori(1, NBLK // 2) as r:
                with sp.If(r < npairs):
                    load(r, 0, False)
                    load(r, 1, False)
            sp.wait_ge(y_out[0], npairs * 16)
            sp.wait_ge(y_out[1], npairs * 16)
            for i in range(NTT):
                if i >= 2:
                    sp.wait_ge(fin_ok, 4 * (i - 2) + 4)
                    sp.dma_start(out[0, P * (i - 2):P * (i - 1), :], fbuf(i, 0)).then_inc(out_ok, 16)
                    sp.wait_ge(out_ok, 16 * (i - 1))
                for j, src in enumerate((x2d[P * i:P * i + P, :], yd[P * i:P * i + P, :], yd[T + P * i:T + P * i + P, :])):
                    sp.dma_start(fbuf(i, j), src).then_inc(fin_in[i % 2], 16)
            for i in range(NTT - 2, NTT):
                sp.wait_ge(fin_ok, 4 * i + 4)
                sp.dma_start(out[0, P * i:P * i + P, :], fbuf(i, 0)).then_inc(out_ok, 16)
            sp.wait_ge(out_ok, 16 * NTT)

        @block.gpsimd
        def _(pool):
            g = Steps(pool, pool_s)
            g.do(nc.gpsimd.memset(ident[:], 0.0))
            nc.gpsimd.memset(ones[:], 1.0)
            nc.gpsimd.memset(zero[:], 0.0)
            nc.gpsimd.memset(halfpi[:], 1.5707963267948966)
            nc.gpsimd.memset(misc[:, :], 0.0)
            nc.gpsimd.memset(prmA, 0.0)
            nc.gpsimd.memset(prmB, 0.0).then_inc(zero_ok, 1)
            nc.gpsimd.memset(lruW, 0.0).then_inc(zero_ok, 1)
            nc.gpsimd.memset(epsb[:], EPS)
            nc.gpsimd.iota(tk[:, 0:FINE], pattern=[[1, FINE]], base=0, channel_multiplier=0,
                           allow_small_or_imprecise_dtypes=True)
            nc.gpsimd.iota(tk[:, FINE:], pattern=[[FINE, COARSE]], base=0, channel_multiplier=0,
                           allow_small_or_imprecise_dtypes=True)
            nc.gpsimd.memset(s5C, 0.0)
            nc.gpsimd.memset(Gin[0], 0.0)
            nc.gpsimd.memset(Gin[1], 0.0).then_inc(gin_zero, 1)
            pool.wait_ge(gin_zero, 1)
            nc.gpsimd.affine_select(out=ident[:], in_=ident[:], compare_op=ALU.not_equal, fill=1.0, base=0,
                                    pattern=[[-1, P]], channel_multiplier=1).then_inc(const_ok, 1)
            nc.gpsimd.memset(tri[:], 1.0)
            nc.gpsimd.memset(maskneg[:], 0.0)
            nc.gpsimd.memset(rmask[:], 1.0)
            nc.gpsimd.memset(emask[:], 1.0)
            nc.gpsimd.memset(blk64[:], 0.0)
            g.do(nc.gpsimd.memset(misc[:, :], 0.0))
            g.settle()
            ge = ALU.is_ge
            g.do(nc.gpsimd.affine_select(out=tri[:], in_=tri[:], compare_op=ge, fill=0.0, base=0, pattern=[[1, P]], channel_multiplier=-1))
            g.do(nc.gpsimd.affine_select(out=maskneg[:], in_=maskneg[:], compare_op=ge, fill=-1e9, base=0, pattern=[[1, P]], channel_multiplier=-1))
            g.do(nc.gpsimd.affine_select(out=rmask[:, 0], in_=rmask[:, 0], compare_op=ge, fill=0.0, base=-1, pattern=[[1, 64]], channel_multiplier=-1))
            g.do(nc.gpsimd.affine_select(out=rmask[:, 1], in_=rmask[:, 1], compare_op=ge, fill=0.0, base=0, pattern=[[1, 64]], channel_multiplier=-1))
            g.do(nc.gpsimd.memset(blk64[0:64, 0:64], 1.0))
            g.settle()
            g.do(nc.gpsimd.memset(blk64[64:128, 64:128], 1.0))
            g.settle()
            for i in range(7):
                m = 2 ** i
                e = emask[:, i].rearrange("p (b m) -> p b m", m=m)
                g.do(nc.gpsimd.affine_select(out=e, in_=e, compare_op=ge, fill=0.0, base=0, pattern=[[-m, 64 // m], [0, m]], channel_multiplier=1))
                g.settle()
                g.do(nc.gpsimd.affine_select(out=e, in_=e, compare_op=ge, fill=0.0, base=m - 1, pattern=[[m, 64 // m], [0, m]], channel_multiplier=-1))
                g.settle()
            g.do(nc.gpsimd.tensor_tensor(tris[:], tri[:], ident[:], ALU.subtract))
            g.do(nc.gpsimd.tensor_tensor(lvm[:], emask[:, 1:7], emask[:, 0:6], ALU.subtract))
            g.settle()
            g.tell(nc.gpsimd.tensor_tensor(lvm[:], lvm[:], rmask[:, 0:1].to_broadcast([64, 6, 64]), ALU.mult), mask_ok, 1)
            g.settle()
            pool.wait_ge(bbar_ok, 1)
            for r in range(2):
                gv = Gin[r].rearrange("p a (b c) -> p a b c", b=4)
                bb = wk[:, r, 0:256].rearrange("p (a b h) -> p a b h", a=WT, b=4)
                for b in range(4):
                    for u in range(2):
                        last = nc.gpsimd.tensor_copy(gv[64 * u:64 * u + 64, :, b, 32 * b + 16 * u:32 * b + 16 * u + 16],
                                                     bb[64 * u:64 * u + 64, :, b, :])
            last.then_inc(gin_ok, 1)
            pool.wait_ge(gin_ok, 1)
            pool.wait_ge(trig_ok, 1)
            pool.wait_ge(tr_ok, NTT * 4)
            for p in range(NPAIR):
                fine = [m[:, p, 0:FINE].unsqueeze(1).to_broadcast([P, COARSE, FINE]) for m in (cosF, sinF)]
                coarse = [m[:, p, FINE:].unsqueeze(2).to_broadcast([P, COARSE, FINE]) for m in (cosF, sinF)]
                cosT, sinT = (s5tab[:, 2 * (p % 2) + r, :].rearrange("p (a b) -> p a b", a=COARSE) for r in range(2))
                t0, t1 = (ptmp[:, r, :].rearrange("p (a b) -> p a b", a=COARSE) for r in range(2))
                if p >= 2:
                    pool.wait_ge(tab_used, p - 1)
                g.do(nc.gpsimd.tensor_tensor(t0, coarse[0], fine[0], ALU.mult))
                g.do(nc.gpsimd.tensor_tensor(t1, coarse[1], fine[1], ALU.mult))
                g.settle()
                g.do(nc.gpsimd.tensor_tensor(cosT, t0, t1, ALU.subtract))
                g.settle()
                g.do(nc.gpsimd.tensor_tensor(t0, coarse[1], fine[0], ALU.mult))
                g.do(nc.gpsimd.tensor_tensor(t1, coarse[0], fine[1], ALU.mult))
                g.settle()
                g.tell(nc.gpsimd.tensor_tensor(sinT, t0, t1, ALU.add), tab_ok, p + 1)
                g.settle()
            for c0 in range(0, NRC, 2):
                for lv in range(LEV):
                    for c in (c0, c0 + 1):
                        if lv == 0:
                            pool.wait_ge(gram_ok, 4 * c + 4)
                        else:
                            b, i = at[("t", c, lv - 1)]
                            pool.wait_ge(full[b], i + 1)
                            if lv == 1:
                                pool.wait_ge(x_ok, XC(c, 1))
                        if c >= 2 and lv == 0:
                            pool.wait_ge(ro_ok, 2 * (c - 1))
                        g.tell(nc.gpsimd.tensor_tensor(rb(c, 8), rb(c, 3)[:, :, 0, :], lvm[:, lv:lv + 1, :].to_broadcast([64, RH, 64]),
                                                       ALU.mult), of_ok, OC(c, lv))

            b, i = at[("out", 4 * NTT - 1)]
            pool.wait_ge(free[b], i + 1)
            pool.wait_ge(full[at["logit"][0]], at["logit"][1] + 1)
            fl = dict(allow_small_or_imprecise_dtypes=True)
            nc.gpsimd.iota(rv(0, 8), pattern=[[1, 8]], base=0, channel_multiplier=0, **fl)
            nc.gpsimd.iota(rv(1, NE), pattern=[[1, NE]], base=0, channel_multiplier=0, **fl)
            nc.gpsimd.iota(rv(2, 8), pattern=[[B, 8]], base=0, channel_multiplier=0, **fl)
            nc.gpsimd.iota(rv(3, 1), pattern=[[0, 1]], base=0, channel_multiplier=1, **fl)
            nc.gpsimd.iota(tokv, pattern=[[T, 2], [P, NTT]], base=0, channel_multiplier=1)
            nc.gpsimd.memset(tini, NROW)
            g.tell(nc.gpsimd.memset(rv(0, 320)[:, 8:9], 0.0), ri_ok, 1)
            g.settle()
            pool.dma_start(tokd.rearrange("(b r) o -> b (r o)", r=B), tini).then_inc(tab_io, 16)
            pool.wait_ge(dest_ok, 1)
            pool.wait_ge(tab_io, 16)
            for k in range(2):
                for i in range(NTT):
                    nc.gpsimd.indirect_dma_start(tokd, bass.IndirectOffsetOnAxis(ap=desti[:, k, i:i + 1], axis=0),
                                                 tokv[:, k, i:i + 1], None).then_inc(tab_io, 16)
                    pool.wait_ge(tab_io, 16 * (NTT * k + i + 2))
            pool.dma_start(tabi, tokd.rearrange("(b r) o -> b (r o)", r=B)).then_inc(tab_io, 16)
            pool.wait_ge(spill, 16 * 2 * NTT)
            pool.wait_ge(idx_ok, 1)
            pool.wait_ge(rowi_ok, 1)
            npairs = pool.value_load(rowi[0:1, P:P + 1], min_val=1, max_val=NBLK // 2)
            for k in range(2):
                g.tell(nc.gpsimd.memset(xg[k], 0.0), xz_ok, k + 1)
            g.settle()

            def gather(r, k, first):
                if not first:
                    pool.wait_ge(xtp_ok, 4 * (r - 1) + 2 * k + 2)
                    pool.sem_inc(passed, 1)
                nc.gpsimd.tensor_copy(gix[k][:], idxg[:, bass.ds(2 * r + k, 1)]).then_inc(gcp_ok[k], 1)
                pool.wait_ge(gcp_ok[k], 1 if first else 2 * r)
                pool.sem_inc(passed, 1)
                nc.gpsimd.indirect_dma_start(xg[k], None, hd, bass.IndirectOffsetOnAxis(ap=gix[k][:, 0:1], axis=0),
                                             bounds_check=T - 1, oob_is_err=False).then_inc(xg_in[k], 16)

            def scatter(r, k):
                pool.wait_ge(y_ok[k], 4 * r + 4)
                pool.sem_inc(passed, 1)
                nc.gpsimd.tensor_copy(six[k][:], idxs[:, bass.ds(2 * r + k, 1)]).then_inc(gcp_ok[k], 1)
                pool.wait_ge(gcp_ok[k], 2 * r + 3)
                pool.sem_inc(passed, 1)
                nc.gpsimd.indirect_dma_start(yd, bass.IndirectOffsetOnAxis(ap=six[k][:, 0:1], axis=0), yb[k], None,
                                             bounds_check=2 * T - 1, oob_is_err=False).then_inc(y_out[k], 16)

            gather(0, 0, True)
            gather(0, 1, True)

            def pair(r):
                for k in range(2):
                    gather(r + 1, k, False)
                    scatter(r, k)

            pair(0)
            with pool.Fori(1, NBLK // 2) as r:
                with pool.If(r < npairs):
                    pair(r)

        @block.scalar
        def _(act):
            a = Steps(act, act_s)
            act.wait_ge(zero_ok, 1)
            for tab, dst in ((PA, prmA), (PB, prmB)):
                for name, (r, n) in tab.items():
                    src = I[name]
                    flat = src.rearrange(" ".join("abcd"[:len(src.shape)]) + " -> (" + " ".join("abcd"[:len(src.shape)]) + ")")
                    if name == "rw_mu":
                        flat = flat[0:3 * W]
                    act.dma_start(dst[r:r + n, :], flat.rearrange("(r c) -> r c", c=P)).then_inc(prm_in, 16)
            mu = I["rw_mu"]
            act.dma_start(prmB[MU_LORA:MU_LORA + 1, 0:LW + LA], mu[:, 3 * W:3 * W + LW + LA]).then_inc(prm_in, 16)
            act.dma_start(prmB[MU_LORA + 1:MU_LORA + 2, 0:LG], mu[:, 3 * W + LW + LA:]).then_inc(prm_in, 16)
            act.dma_start(wdt[:], I["w_in"][0].rearrange("(c p) n -> p c n", p=P)[:, :, C_DT:]).then_inc(wdt_in, 16)
            act.dma_start(ldt[:], I["s5_log_dt"][0].rearrange("(g u) -> g u", u=2)).then_inc(ldt_in, 16)
            act.dma_start(prmC[16:32, :], I["s5_lambda_re"][0].rearrange("(g u) n -> g (u n)", u=2)).then_inc(s5_in, 16)
            act.dma_start(prmC[32:48, :], I["s5_lambda_im"][0].rearrange("(g u) n -> g (u n)", u=2)).then_inc(s5_in, 16)
            for r, w in enumerate(("s5_b_re", "s5_b_im")):
                act.dma_start(rawB[:, r], I[w][0].rearrange("(g u) n h -> (u n) g h", u=2)).then_inc(s5_in, 16)
            for r, w in enumerate(("s5_c_re", "s5_c_im")):
                for u in range(2):
                    act.dma_start(dupC[:, r, :, u, :], I[w][0].rearrange("(q g) h n -> (g h) q n", q=WT)).then_inc(s5_in, 16)
            for k, w in enumerate(("ssd_dt_bias", "ssd_a_log", "ssd_d")):
                act.dma_start(cbc[:, k, :], I[w].to_broadcast([P, SH])).then_inc(cbc_in, 16)
            act.dma_start(loraW[0:LW, 0, :], I["rw_w2"][0]).then_inc(lora_in, 16)
            act.dma_start(loraW[LW:LW + LA, 0, :], I["rw_a2"][0]).then_inc(lora_in, 16)
            act.dma_start(loraW[0:LG, 1, :], I["rw_g2"][0]).then_inc(lora_in, 16)
            act.wait_ge(zero_ok, 2)
            for r, w in enumerate(("lru_wa", "lru_wx")):
                wv = I[w][0].rearrange("(t u) i j -> u i t j", u=2)
                for u in range(2):
                    act.dma_start(lruW[64 * u:64 * u + 64, r, :, 64 * u:64 * u + 64], wv[u]).then_inc(lruw_in, 16)
            for i in range(NTT):
                act.wait_ge(x_in[i], 16)
                nc.scalar.activation(hT[:, 0:4, :].rearrange("p a n -> p (a n)"), xs[:, i, :], ACT.Square,
                                     accum_out=st[:, i:i + 1]).then_inc(ssq_ok, 1)
                act.wait_ge(ssq_ok, i + 1)
            act.wait_ge(ms_ok, 1)
            nc.scalar.activation(st[:, 8:12], st[:, 4:8], ACT.Sqrt).then_inc(rs_ok, 1)
            act.wait_ge(s5_col, 1)
            nc.scalar.activation(s5v[:, 0, :], colC[:, 0:16], ACT.Exp).then_inc(dt_ok, 1)
            act.wait_ge(lrdt_ok, 1)
            nc.scalar.activation(s5v[:, 2, :], s5v[:, 1, :], ACT.Exp).then_inc(mag_ok, 1)
            act.wait_ge(phase_ok, 2)
            nc.scalar.activation(sinF, ph(2), ACT.Sin, scale=6.283185)
            nc.scalar.activation(cosF, ph(3), ACT.Sin, scale=6.283185).then_inc(trig_ok, 1)
            act.wait_ge(spa_ok, 1)
            nc.scalar.activation(lsp[:, 1, :], lsp[:, 0, :], ACT.Exp, scale=-1.0).then_inc(spe_ok, 1)
            def s5_setup():
                for n in range(8):
                    act.wait_ge(g_tr, n + 1)
                    nc.scalar.activation(s5G.rearrange("p r g c -> p (r g c)")[:, 512 * n:512 * n + 512], ps[2 + n % 4][:], ACT.Copy).then_inc(g_got, 1)
                for r in range(2):
                    act.wait_ge(g_tr, 9 + r)
                    for u in range(2):
                        src = ps[2 + r][64 * u:64 * u + 64, :].rearrange("p (g u h) -> p g u h", u=2, h=S5_H)[:, :, u, :]
                        last = nc.scalar.activation(s5C[64 * u:64 * u + 64, r, :, 16 * u:16 * u + 16], src, ACT.Copy,
                                                    scale=1.0 - 2.0 * r)
                    last.then_inc(g_got, 1)

            def proj_out(n):
                s, c, wd, d = tiles[n]
                act.wait_ge(proj_ok, n + 1)
                nc.scalar.activation(proj[0:wd, d, :], ps[n % 2][0:wd, :], ACT.Copy).then_inc(proj_got, 1)

            def use(u, out, func, **kw):
                act.wait_ge(mm_ok, u + 1)
                nc.scalar.activation(out, ps[2 + u % 4][:], func, **kw).then_inc(mm_used, 1)

            def s5_glu():
                act.wait_ge(y_used, WT)
                nc.scalar.activation(U5, U5, ACT.Gelu_apprx_tanh).then_inc(gelu_ok, 1)
                for q in range(WT):
                    use(U_GLU + q, wk2[:, q, :], ACT.Sigmoid, bias=A("s5_b_glu", q))

            def lru_gates():
                for q in range(WT):
                    use(U_LRU + 2 * q, XL[:, q, :], ACT.Sigmoid, bias=A("lru_ba", q))
                    use(U_LRU + 2 * q + 1, wk[:, 4 + q, :], ACT.Sigmoid, bias=A("lru_bx", q))
                act.wait_ge(sp_ok, 1)
                act.wait_ge(mm_used, U_LRU + 8)
                for q in range(WT):
                    nc.scalar.activation(wk2[:, 4 + q, :], XL[:, q, :], ACT.Tanh, scale=lsp[:, 4, q:q + 1]).then_inc(ta_ok, 1)
                act.wait_ge(ta_ok, 4)
                for q in range(WT):
                    nc.scalar.activation(XL[:, q, :], XL[:, q, :], ACT.Exp, scale=lsp[:, 5, q:q + 1]).then_inc(ta_ok, 1)
                act.wait_ge(m2_ok, 1)
                nc.scalar.activation(wk2[:, 4:8, :], wk2[:, 4:8, :], ACT.Sqrt).then_inc(m_ok, 1)
                nc.scalar.activation(GL, GL, ACT.Gelu_apprx_tanh).then_inc(m_ok, 1)

            def rms(u, scratch):
                use(u, scratch, ACT.Sqrt, bias=epsb[:], scale=1.0 / W)

            def take(name, out, func=ACT.Copy, part=slice(0, P), cols=slice(0, 512), **kw):
                b, i = at[name]
                act.wait_ge(full[b], i + 1)
                nc.scalar.activation(out, ps[b][part, cols], func, **kw).then_inc(free[b], 1)

            def ssd_small():
                act.wait_ge(dtx_ok, 1)
                nc.scalar.activation(sds[:, 1, :], sds[:, 0, :], ACT.Exp, scale=-1.0).then_inc(dte_ok, 1)
                act.wait_ge(cbc_in, 48)
                nc.scalar.activation(cbc[:, 3, :], cbc[:, 1, :], ACT.Exp).then_inc(dte_ok, 1)
                act.wait_ge(csd_ok, 1)
                nc.scalar.activation(sds[:, 4:7, :], sds[:, 4:7, :], ACT.Exp).then_inc(cse_ok, 1)

            def ssd_silu():
                for j in range(8):
                    act.wait_ge(sconv_ok, j + 1)
                    nc.scalar.activation(XBC[:, j, :], wk[:, j % 4, :], ACT.Silu).then_inc(silu_ok, 1)
                nc.scalar.activation(Z_, Z_, ACT.Silu).then_inc(z_ok, 1)

            def ssd_tokens():
                for i in range(NTT):
                    take(("xt", i), XT_[:, i, :])
                for i in range(2):
                    take(("bt", i), BT.rearrange("p c g n -> p (c g n)")[:, 512 * i:512 * i + 512])

            def ssd_exp(c):
                act.wait_ge(seg_ok, c + 1)
                nc.scalar.activation(DM[:, c % 2], DM[:, c % 2], ACT.Exp).then_inc(segx_ok, 1)

            for n in range(NT):
                proj_out(n)
                if n == 3:
                    s5_setup()
                if n == 12:
                    s5_glu()
                if n == 14:
                    rms(U_RMS5, wk2[:, 0, :])
                if n == 15:
                    lru_gates()
                if n == 18:
                    rms(U_RMSL, wk2[:, 0, :])
                if n == 25:
                    ssd_small()
                    ssd_silu()
                if n == 27:
                    ssd_tokens()
                if n >= 28 and n % 2 == 0 and n < 28 + 2 * NSC:
                    ssd_exp((n - 28) // 2)
            b, i = at["rms_s"]
            act.wait_ge(full[b], i + 1)
            nc.scalar.activation(wk[:, 0, :], ps[b][:], ACT.Sqrt, bias=epsb[:], scale=1.0 / W).then_inc(free[b], 1)

            act.wait_ge(lo_ok, 2)
            nc.scalar.activation(LO[0:LW, 0, :], LO[0:LW, 0, :], ACT.Tanh).then_inc(lot_ok, 1)
            nc.scalar.activation(LO[0:LG, 1, :], LO[0:LG, 1, :], ACT.Sigmoid).then_inc(lot_ok, 1)
            act.wait_ge(mix_ok, 12)
            for q in range(WT):
                take(("lora", q, 0), sg[:, q, :], ACT.Sigmoid, bias=A("rw_w0", q))
                take(("lora", q, 1), ra[:, q, :], ACT.Sigmoid, bias=A("rw_a0", q))
                take(("lora", q, 2), Gt[:, q, :])
            act.wait_ge(kn_ok, WT)
            nc.scalar.activation(knr, knr, ACT.Sqrt).then_inc(knr_ok, 1)
            KAP = INV_SQRT_E
            act.wait_ge(cum_ok, 2)
            nc.scalar.activation(wcum, cum, ACT.Exp, scale=-KAP).then_inc(dec_ok, 1)
            nc.scalar.activation(winv, cum, ACT.Exp, scale=KAP).then_inc(dec_ok, 1)
            nc.scalar.activation(wprev, cumx, ACT.Exp, scale=-KAP).then_inc(dec_ok, 1)
            lo = slice(0, 64)

            def flat(x):
                return x.rearrange("p h t -> p (h t)")

            for c0 in range(0, NRC, 2):
                for c in (c0, c0 + 1):
                    if c >= 2:
                        act.wait_ge(ro_ok, 2 * (c - 1))
                    for k in range(3):
                        b, i = at[("tm", c, k)]
                        act.wait_ge(full[b], i + 1)
                        nc.scalar.activation(flat(rb(c, k)), ps[b][lo, :], ACT.Copy).then_inc(free[b], 1)
                for lv in range(LEV):
                    for c in (c0, c0 + 1):
                        b, i = at[("t", c, lv)]
                        if lv:
                            act.wait_ge(full[b], i + 1)
                            nc.scalar.activation(flat(rb(c, 7)), ps[b][lo, :], ACT.Copy).then_inc(free[b], 1)
                for c in (c0, c0 + 1):
                    take(("y", c), flat(RY), part=lo)
                    take(("un", c), flat(RU), part=lo, scale=-1.0)
                    b, i = at[("o", c)]
                    act.wait_ge(full[b], i + 1)
                    pv = ps[b][lo, :].rearrange("p (j o t) -> p o j t", o=2, t=RC)
                    nc.scalar.activation(Ot[0:64, :, RC * c:RC * c + RC], pv[:, 0], ACT.Copy).then_inc(ro_ok, 1)
                    nc.scalar.activation(Ot[64:128, :, RC * c:RC * c + RC], pv[:, 1], ACT.Copy).then_inc(free[b], 1)
                    act.wait_ge(free[b], i + 1)
                    nc.scalar.activation(misc[:, 4:5], misc[:, 5:6], ACT.Copy).then_inc(ro_ok, 1)
            act.wait_ge(var_ok, WT)
            nc.scalar.activation(wk[:, 0:4, :], wk[:, 0:4, :], ACT.Sqrt).then_inc(var_ok, 1)
            act.dma_start(gffn, I["norm_ffn"].to_broadcast([P, D])).then_inc(gain_in, 16)
            for i in range(NTT):
                act.wait_ge(x2_ok, 4 * NTT)
                nc.scalar.activation(h2p[i], x2[i], ACT.Square, accum_out=st[:, 16 + i:17 + i]).then_inc(ssx_ok, 1)
            act.wait_ge(msx_ok, 1)
            nc.scalar.activation(st[:, 24:28], st[:, 20:24], ACT.Sqrt).then_inc(rsx_ok, 1)
            for m in range(4 * NTT):
                i, c4 = divmod(m, 4)
                b, n = at[("h2", m)]
                act.wait_ge(full[b], n + 1)
                nc.scalar.activation(h2T[:, 4 * c4:4 * c4 + 4, P * i:P * i + P], ps[b][:].rearrange("p (a n) -> p a n", a=4),
                                     ACT.Copy).then_inc(free[b], 1)
            act.dma_start(rbias[:, 0:NG], I["moe_b_group"].to_broadcast([P, NG])).then_inc(cbc_in, 16)
            act.dma_start(rbias[:, NG:], I["moe_b_expert"].to_broadcast([P, NE])).then_inc(cbc_in, 16)
            act.wait_ge(re_ok, 1)
            nc.scalar.activation(rv(6, NTT, NG), rv(6, NTT, NG), ACT.Exp).then_inc(re_ok, 1)
            act.wait_ge(re_ok, 3)
            nc.scalar.activation(gate[:, 1, :], gate[:, 1, :], ACT.Exp).then_inc(re_ok, 1)
            act.wait_ge(idx_ok, 1)
            act.wait_ge(rowi_ok, 1)
            act.wait_ge(spill, 16 * 2 * NTT)
            npairs = act.value_load(rowi[0:1, P:P + 1], min_val=1, max_val=NBLK // 2)

            def columns(r, k):
                act.wait_ge(xtp_ok, 4 * r + 2 * k + 1)
                nc.scalar.activation(xT[k][:, 0:8, :].rearrange("p c t -> p (c t)"), ps[0][:], ACT.Copy).then_inc(xT_ok, 1)

            def block_(r, k, nr, nk):
                act.wait_ge(up_ok, 2 * r + k + 1)
                nc.scalar.activation(sil[k], ps[2 + k][:, 0:FC * B], ACT.Silu).then_inc(sil_ok, 1)
                columns(nr, nk)
                for n in (0, 2):
                    act.wait_ge(down_ok, 8 * r + 4 * k + n + 1)
                    if n == 0 and k is not None:
                        wait_y_out(act, r, k)
                    nc.scalar.activation(yb[k][:, 512 * n:512 * n + 512], ps[4 + n][0:B, :], ACT.Copy).then_inc(y_ok[k], 1)

            columns(0, 0)
            block_(0, 0, 0, 1)
            block_(0, 1, 1, 0)
            with act.Fori(1, NBLK // 2) as r:
                with act.If(r < npairs):
                    block_(r, 0, r, 1)
                    block_(r, 1, r + 1, 0)
            act.dma_start(gfin, I["norm_final"].rearrange("(a d) -> a d", a=1).to_broadcast([P, D])).then_inc(gain_in, 16)
            for i in range(NTT):
                act.wait_ge(fin_ok, 4 * i + 1)
                nc.scalar.activation(fbuf(i, 1), fbuf(i, 0), ACT.Square, accum_out=st[:, 32 + i:33 + i]).then_inc(fss_ok, 1)
                act.wait_ge(fms_ok, i + 1)
                nc.scalar.activation(st[:, 40 + i:41 + i], st[:, 36 + i:37 + i], ACT.Sqrt).then_inc(frs_ok, 1)

        NPRM = 16 * (len(PA) + len(PB) + 2)

        @block.vector
        def _(dve):
            v = Steps(dve, dve_s)
            dve.wait_ge(ssq_ok, NTT)
            v.do(nc.vector.tensor_scalar(st[:, 12:16], st[:, 0:4], 1.0 / D, EPS, ALU.mult, ALU.add))
            v.settle()
            v.tell(nc.vector.reciprocal(st[:, 4:8], st[:, 12:16]), ms_ok, 1)
            dve.wait_ge(rs_ok, 1)
            for i in range(NTT):
                v.tell(nc.vector.tensor_scalar(xs[:, i, :], xs[:, i, :], st[:, 8 + i:9 + i], None, ALU.mult), h_ok, i + 1)
            dve.wait_ge(prm_tr, 1)
            nc.vector.tensor_copy(colA[:], ps[6][:, 0:128])
            nc.vector.tensor_copy(colB[:], ps[6][:, 128:256]).then_inc(prm_col, 1)
            dve.wait_ge(prm_col, 1)
            dve.wait_ge(ldt_in, 16)
            v.tell(nc.vector.tensor_copy(prmC[0:16, :].rearrange("p (u n) -> p u n", u=2),
                                         ldt[:].unsqueeze(2).to_broadcast([NPAIR, 2, S5_N])), ldt_ok, 1)
            dve.wait_ge(prm_tr, 2)
            v.tell(nc.vector.tensor_copy(colC[:], ps[7][:, 0:48]), s5_col, 1)
            v.settle()
            lr, li = colC[:, 16:32], colC[:, 32:48]
            ap4 = colA[:, PA["lru_a_param"][0]:PA["lru_a_param"][0] + WT]
            v.do(nc.vector.tensor_scalar(lsp[:, 2, :], ap4, -1.0, None, ALU.mult))
            v.settle()
            v.tell(nc.vector.tensor_tensor(lsp[:, 0, :], ap4, lsp[:, 2, :], ALU.max), spa_ok, 1)
            for m in range(NTT * 4):
                i, c4 = divmod(m, 4)
                dve.wait_ge(tr_ok, m + 1)
                g0 = PB["norm_mix"][0] + 4 * c4
                nc.vector.tensor_tensor(
                    hT[:, 4 * c4:4 * c4 + 4, P * i:P * (i + 1)], ps[2 + m % 4][:].rearrange("p (a n) -> p a n", a=4),
                    colB[:, g0:g0 + 4].to_broadcast([P, 4, P]), ALU.mult).then_inc(tr_used, 1)

            def op(out, a, b, o):
                v.do(nc.vector.tensor_tensor(out, a, b, o))

            def sc(out, a, s1, s2=None, o0=ALU.mult, o1=None):
                if s2 is None:
                    v.do(nc.vector.tensor_scalar(out, a, s1, None, o0))
                else:
                    v.do(nc.vector.tensor_scalar(out, a, s1, s2, o0, o1))

            MUL, ADD, SUB = ALU.mult, ALU.add, ALU.subtract
            S = [s5v[:, i, :] for i in range(16)]
            dve.wait_ge(dt_ok, 1)
            op(S[3], li, S[0], MUL)
            v.tell(nc.vector.tensor_tensor(S[1], lr, S[0], MUL), lrdt_ok, 1)
            v.settle()
            sc(S[4], S[3], 0.15915494309189535)
            v.settle()
            sc(S[5], S[4], MAGIC, MAGIC, ADD, SUB)
            v.settle()
            op(S[4], S[4], S[5], SUB)
            v.settle()
            sc(S[5], S[4], 16384.0, MAGIC, MUL, ADD)
            v.settle()
            sc(S[6], S[5], MAGIC, 1.0 / 16384.0, SUB, MUL)
            v.settle()
            op(S[7], S[4], S[6], SUB)
            v.settle()
            shp = [P, NPAIR, FINE + COARSE]
            tkb = tk[:].unsqueeze(1).to_broadcast(shp)
            op(ph(0), tkb, S[6].unsqueeze(2).to_broadcast(shp), MUL)
            op(ph(2), tkb, S[7].unsqueeze(2).to_broadcast(shp), MUL)
            v.settle()
            sc(ph(1), ph(0), MAGIC, MAGIC, ADD, SUB)
            v.settle()
            op(ph(0), ph(0), ph(1), SUB)
            v.settle()
            op(ph(0), ph(0), ph(2), ADD)
            v.settle()
            sc(ph(1), ph(0), MAGIC, MAGIC, ADD, SUB)
            v.settle()
            v.tell(nc.vector.tensor_tensor(ph(2), ph(0), ph(1), SUB), phase_ok, 1)
            v.settle()
            sc(ph(0), ph(0), 0.25, None, ADD)
            v.settle()
            sc(ph(1), ph(0), MAGIC, MAGIC, ADD, SUB)
            v.settle()
            v.tell(nc.vector.tensor_tensor(ph(3), ph(0), ph(1), SUB), phase_ok, 2)
            dve.wait_ge(trig_ok, 1)
            dve.wait_ge(mag_ok, 1)
            op(S[8], S[2], cosF[:, :, 1], MUL)
            op(S[9], S[2], sinF[:, :, 1], MUL)
            op(S[10], lr, lr, MUL)
            op(S[11], li, li, MUL)
            v.settle()
            sc(S[8], S[8], -1.0, None, ADD)
            op(S[10], S[10], S[11], ADD)
            v.settle()
            v.do(nc.vector.reciprocal(S[10], S[10]))
            op(S[11], S[8], lr, MUL)
            op(S[12], S[9], li, MUL)
            op(S[13], S[9], lr, MUL)
            op(S[14], S[8], li, MUL)
            v.settle()
            op(S[11], S[11], S[12], ADD)
            op(S[13], S[13], S[14], SUB)
            v.settle()
            op(S[11], S[11], S[10], MUL)
            op(S[13], S[13], S[10], MUL)
            v.settle()
            dve.wait_ge(s5_in, 16 * 8)
            w4 = [wk[:, r, 0:256].rearrange("p (g h) -> p g h", g=NPAIR) for r in range(4)]
            qre, qim = (S[i].unsqueeze(2).to_broadcast([P, NPAIR, S5_H]) for i in (11, 13))
            op(w4[0], rawB[:, 0], qre, MUL)
            op(w4[2], rawB[:, 1], qim, MUL)
            op(w4[1], rawB[:, 1], qre, MUL)
            op(w4[3], rawB[:, 0], qim, MUL)
            v.settle()
            op(w4[0], w4[0], w4[2], SUB)
            v.tell(nc.vector.tensor_tensor(w4[1], w4[1], w4[3], ADD), bbar_ok, 1)
            dve.wait_ge(spe_ok, 1)

            def log1p(out, e, s, s2):
                sc(out, e, 2.0, None, ADD)
                v.settle()
                v.do(nc.vector.reciprocal(out, out))
                v.settle()
                op(s, e, out, MUL)
                v.settle()
                op(s2, s, s, MUL)
                v.settle()
                sc(out, s2, 2.0 / 17, 2.0 / 15, MUL, ADD)
                for k in (13, 11, 9, 7, 5, 3, 1):
                    v.settle()
                    op(out, out, s2, MUL)
                    v.settle()
                    sc(out, out, 2.0 / k, None, ADD)
                v.settle()
                op(out, out, s, MUL)
                v.settle()

            log1p(lsp[:, 3, :], lsp[:, 1, :], lsp[:, 4, :], lsp[:, 5, :])
            v.do(nc.vector.scalar_tensor_tensor(out=lsp[:, 0, :], in0=lsp[:, 2, :], scalar=0.0, in1=lsp[:, 3, :],
                                                op0=ALU.max, op1=ALU.add))
            v.settle()
            sc(lsp[:, 4, :], lsp[:, 0, :], 8.0)
            v.tell(nc.vector.tensor_scalar(lsp[:, 5, :], lsp[:, 0, :], -8.0, None, MUL), sp_ok, 1)
            dve.wait_ge(gin_ok, 1)

            def s5_pair(p):
                bre, bim = ps[2 + 2 * (p % 2)][:], ps[3 + 2 * (p % 2)][:]
                cosT, sinT = s5tab[:, 2 * (p % 2), :], s5tab[:, 2 * (p % 2) + 1, :]
                k = [wk[:, i, :] for i in range(4)]
                xr, xi = wk[:, 4 + 2 * (p % 2), :], wk[:, 5 + 2 * (p % 2), :]
                dve.wait_ge(bu_ok, p + 1)
                dve.wait_ge(tab_ok, p + 1)
                v.settle()
                op(k[0], bre, cosT, MUL)
                op(k[1], bim, sinT, MUL)
                op(k[2], bim, cosT, MUL)
                v.tell(nc.vector.tensor_tensor(k[3], bre, sinT, MUL), bu_used, p + 1)
                v.settle()
                op(k[0], k[0], k[1], ADD)
                op(k[2], k[2], k[3], SUB)
                v.settle()
                mag = s5v[:, 2, p:p + 1].to_broadcast([P, T])
                v.do(nc.vector.tensor_tensor_scan(k[1], mag, k[0], 0.0, MUL, ADD))
                v.do(nc.vector.tensor_tensor_scan(k[3], mag, k[2], 0.0, MUL, ADD))
                v.settle()
                op(k[0], cosT, k[1], MUL)
                op(k[2], sinT, k[3], MUL)
                v.settle()
                if p >= 2:
                    dve.wait_ge(st_used, p - 1)
                op(xr, k[0], k[2], SUB)
                v.settle()
                op(k[0], sinT, k[1], MUL)
                v.tell(nc.vector.tensor_tensor(k[2], cosT, k[3], MUL), tab_used, p + 1)
                v.settle()
                v.tell(nc.vector.tensor_tensor(xi, k[0], k[2], ADD), st_ok, p + 1)

            def s5_y(q):
                dve.wait_ge(st_used, 4 * q + 4)
                v.tell(nc.vector.scalar_tensor_tensor(out=U5[:, q, :], in0=U5[:, q, :], scalar=A("s5_d", q),
                                                      in1=ps[6][:], op0=MUL, op1=ADD), y_used, q + 1)

            for p in range(NPAIR):
                s5_pair(p)
                if p % 4 == 0 and p:
                    s5_y(p // 4 - 1)
            s5_y(WT - 1)
            v.settle()
            dve.wait_ge(proj_got, proj_at[7])

            def conv(out, src, name, q, rows, at):
                conv_to(conv_ok, out, src, name, q, rows, at)

            def conv_to(done, out, src, name, q, rows, at):
                col = (A if name == "lru" else Bc)
                v.do(nc.vector.tensor_scalar(out, src, col(name + "_conv_w", 3 * rows + q), col(name + "_conv_b", q), MUL, ADD))
                for sh in (1, 2, 3):
                    v.settle()
                    ins = nc.vector.scalar_tensor_tensor(out=out[:, sh:], in0=src[:, 0:T - sh],
                                                         scalar=col(name + "_conv_w", (3 - sh) * rows + q),
                                                         in1=out[:, sh:], op0=MUL, op1=ADD)
                    if sh < 3:
                        v.do(ins)
                    else:
                        v.tell(ins, done, at)

            dve.wait_ge(st_used, NPAIR)
            for q in range(WT):
                conv(wk[:, q, :], XL[:, q, :], "lru", q, WT, q + 1)
            v.settle()

            def rms(x, sq, scratch, u, k, gain):
                v.tell(nc.vector.tensor_tensor(sq, x, x, MUL), sq_ok, k + 1)
                dve.wait_ge(mm_used, u + 1)
                v.do(nc.vector.reciprocal(scratch, scratch))
                v.settle()
                for q in range(WT):
                    v.tell(nc.vector.scalar_tensor_tensor(out=x[:, q, :], in0=x[:, q, :], scalar=gain(q), in1=scratch,
                                                          op0=MUL, op1=MUL), mix_ok, WT * k + q + 1)

            dve.wait_ge(mm_used, U_GLU + WT)
            op(U5, U5, wk2[:, 0:4, :], MUL)
            v.settle()
            rms(U5, wk2[:, 4:8, :], wk2[:, 0, :], U_RMS5, 0, lambda q: A("s5_gain", q))
            v.settle()
            dve.wait_ge(mm_used, U_LRU + 8)
            op(wk[:, 0:4, :], wk[:, 0:4, :], wk[:, 4:8, :], MUL)
            v.settle()
            dve.wait_ge(ta_ok, 4)
            sc(wk[:, 4:8, :], wk2[:, 4:8, :], 1.0, None, ADD)
            v.settle()
            v.do(nc.vector.reciprocal(wk[:, 4:8, :], wk[:, 4:8, :]))
            v.settle()
            v.tell(nc.vector.scalar_tensor_tensor(out=wk2[:, 4:8, :], in0=wk2[:, 4:8, :], scalar=2.0, in1=wk[:, 4:8, :],
                                                  op0=MUL, op1=MUL), m2_ok, 1)
            dve.wait_ge(m_ok, 1)
            op(wk[:, 0:4, :], wk[:, 0:4, :], wk2[:, 4:8, :], MUL)
            v.settle()
            dve.wait_ge(ta_ok, 8)
            for q in range(WT):
                v.do(nc.vector.tensor_tensor_scan(wk[:, 4 + q, :], XL[:, q, :], wk[:, q, :], 0.0, MUL, ADD))
            v.settle()
            dve.wait_ge(m_ok, 2)
            op(XL, wk[:, 4:8, :], GL, MUL)
            v.settle()
            rms(XL, wk[:, 0:4, :], wk2[:, 0, :], U_RMSL, 1, lambda q: A("lru_gain", q))
            v.settle()

            def got(name):
                b, i = at[name]
                dve.wait_ge(full[b], i + 1)
                return ps[b], (free[b], i + 1)

            dve.wait_ge(cbc_in, 48)
            bias4, a4, d4 = (cbc[:, k:k + 1, :].to_broadcast([P, NSC, SH]) for k in (0, 3, 2))
            sd = [sds[:, k, :].rearrange("p (c h) -> p c h", h=SH) for k in range(8)]
            src, done = got("dt")
            v.tell(nc.vector.tensor_tensor(sd[2], src[:, 0:NSC * SH].rearrange("p (c h) -> p c h", h=SH), bias4, ADD), *done)
            v.settle()
            sc(sd[3], sd[2], -1.0)
            v.settle()
            v.tell(nc.vector.tensor_tensor(sd[0], sd[2], sd[3], ALU.max), dtx_ok, 1)
            dve.wait_ge(dte_ok, 2)
            log1p(sds[:, 3, :], sds[:, 1, :], sds[:, 4, :], sds[:, 5, :])
            v.do(nc.vector.scalar_tensor_tensor(out=sds[:, 2, :], in0=sds[:, 2, :], scalar=0.0, in1=sds[:, 3, :], op0=ALU.max, op1=ADD))
            v.settle()
            op(sd[3], sd[2], a4, MUL)
            v.settle()
            v.tell(nc.vector.tensor_scalar(sds[:, 3, :], sds[:, 3, :], -1.0, None, MUL), adt_ok, 1)
            src, done = got("cs")
            v.settle()
            v.do(nc.vector.tensor_copy(sds[:, 7, :], src[:, 0:32]))
            v.do(nc.vector.tensor_copy(sds[:, 6, :], src[:, 32:64]))
            v.tell(nc.vector.tensor_copy(sds[:, 4, :], src[:, 0:32]), *done)
            v.settle()
            v.tell(nc.vector.tensor_tensor(sds[:, 5, :], sds[:, 6, :], sds[:, 7, :], SUB), csd_ok, 1)
            for j in range(8):
                dve.wait_ge(proj_got, proj_at[30 + j])
                if j >= 4:
                    dve.wait_ge(silu_ok, j - 3)
                v.settle()
                conv_to(sconv_ok, wk[:, j % 4, :], XBC[:, j, :], "ssd", j, 8, j + 1)
            dve.wait_ge(cse_ok, 1)
            hs = [P, NSC, SH, 64]

            def heads(x):
                return x.rearrange("p c (h d) -> p c h d", h=SH)

            b, i = at[("xt", 3)]
            dve.wait_ge(free[b], i + 1)
            for c in range(NSC):
                op(XD[:, c, :].rearrange("p (h d) -> p h d", h=SH), XT_[:, c, :].rearrange("p (h d) -> p h d", h=SH),
                   sd[2][:, c].unsqueeze(2).to_broadcast([P, SH, 64]), MUL)
            v.settle()
            dve.wait_ge(silu_ok, 8)
            for c in range(NSC):
                v.tell(nc.vector.tensor_tensor(XE[:, c, :].rearrange("p (h d) -> p h d", h=SH), XD[:, c, :].rearrange("p (h d) -> p h d", h=SH),
                                               sd[5][:, c].unsqueeze(2).to_broadcast([P, SH, 64]), MUL), xe_ok, c + 1)
            for c in range(NSC):
                dm = DM[:, c % 2]
                if c >= 2:
                    b, i = at[("diag", c - 2)]
                    dve.wait_ge(full[b], i + 1)
                for k in range(2):
                    src, done = got(("row", c, k))
                    v.tell(nc.vector.tensor_tensor(dm[:, 4 * k:4 * k + 4], src[:].rearrange("p (h l) -> p h l", h=4),
                                                   sd[7][:, c, 4 * k:4 * k + 4].unsqueeze(2).to_broadcast([P, 4, P]), SUB), *done)
                    v.settle()
                v.tell(nc.vector.tensor_copy(misc[:, 6:7], misc[:, 7:8]), seg_ok, c + 1)
                src, done = got(("state", c))
                if c == 0:
                    v.tell(nc.vector.tensor_copy(SH_[:, 0, :], src[:]), *done)
                    v.settle()
                elif c < NSC - 1:
                    op(SH_[:, c % 2, :].rearrange("p (h d) -> p h d", h=SH), SH_[:, (c - 1) % 2, :].rearrange("p (h d) -> p h d", h=SH),
                       sd[6][:, c].unsqueeze(2).to_broadcast([P, SH, 64]), MUL)
                    v.settle()
                    v.tell(nc.vector.tensor_tensor(SH_[:, c % 2, :], SH_[:, c % 2, :], src[:], ADD), *done)
                    v.settle()
                else:
                    v.tell(nc.vector.tensor_copy(misc[:, 8:9], src[:, 0:1]), *done)
                    v.settle()
                dve.wait_ge(segx_ok, c + 1)
                src, done = got(("score", c))
                for k in range(2):
                    x = nc.vector.tensor_tensor(dm[:, 4 * k:4 * k + 4], dm[:, 4 * k:4 * k + 4],
                                                src[:, 128 * k:128 * k + 128].unsqueeze(1).to_broadcast([P, 4, P]), MUL)
                    if k:
                        v.tell(x, *done)
                v.settle()
                yt = YT[:, c, :].rearrange("p (h d) -> p h d", h=SH)
                op(yt, XT_[:, c, :].rearrange("p (h d) -> p h d", h=SH), cbc[:, 2, :].unsqueeze(2).to_broadcast([P, SH, 64]), MUL)
                v.settle()
                if c:
                    src, done = got(("off", c))
                    v.tell(nc.vector.tensor_tensor(XD[:, c - 1, :].rearrange("p (h d) -> p h d", h=SH), src[:].rearrange("p (h d) -> p h d", h=SH),
                                                   sd[4][:, c].unsqueeze(2).to_broadcast([P, SH, 64]), MUL), *done)
                    v.settle()
                    op(YT[:, c, :], YT[:, c, :], XD[:, c - 1, :], ADD)
                    v.settle()
                src, done = got(("diag", c))
                v.tell(nc.vector.tensor_tensor(YT[:, c, :], YT[:, c, :], src[:], ADD), *done)
                v.settle()
            dve.wait_ge(z_ok, 1)
            for q in range(WT):
                src, done = got(("yt", q))
                v.tell(nc.vector.tensor_tensor(Z_[:, q, :], Z_[:, q, :], src[:], MUL), *done)
                v.settle()
            v.tell(nc.vector.tensor_tensor(wk2[:, 4:8, :], Z_, Z_, MUL), ssq2_ok, 1)
            b, i = at["rms_s"]
            dve.wait_ge(free[b], i + 1)
            v.do(nc.vector.reciprocal(wk[:, 0, :], wk[:, 0, :]))
            v.settle()
            for q in range(WT):
                v.tell(nc.vector.scalar_tensor_tensor(out=Z_[:, q, :], in0=Z_[:, q, :], scalar=A("ssd_norm_w", q), in1=wk[:, 0, :],
                                                      op0=MUL, op1=MUL), mix_ok, 9 + q)

            dve.wait_ge(proj_got, NT)
            v.settle()

            def shift(x, d, mus):
                n = x.shape[1]
                op(d[:, :, 1:], x[:, :, 0:T - 1], x[:, :, 1:], SUB)
                sc(d[:, :, 0:1], x[:, :, 0:1], -1.0)
                v.settle()
                for k in range(n):
                    v.do(nc.vector.scalar_tensor_tensor(out=x[:, k, :], in0=d[:, k, :], scalar=mus(k), in1=x[:, k, :], op0=MUL, op1=ADD))
                v.settle()

            for k, (rows, wd) in enumerate(((LW + LA, 0), (LG, 1))):
                shift(LO[0:rows, k:k + 1, :], wk[0:rows, k:k + 1, :], lambda _: colB[0:rows, MU_LORA + k:MU_LORA + k + 1])
                v.tell(nc.vector.tensor_copy(misc[:, 6:7], misc[:, 7:8]), lo_ok, k + 1)
                v.settle()
            for a, x in enumerate((R_, K_, V_)):
                shift(x, wk[:, 4 * (a % 2):4 * (a % 2) + 4, :], lambda k: A("rw_mu", 4 * a + k))
            dve.wait_ge(proj_ok, NT)
            for q in range(WT):
                sc(kk[:, q, :], K_[:, q, :], A("rw_k_k", q))
            v.settle()
            v.tell(nc.vector.tensor_tensor(wprev, kk, kk, MUL), ksq_ok, 1)
            b, i = at[("lora", 3, 1)]
            dve.wait_ge(free[b], i + 1)
            b, i = at[("lora", 3, 0)]
            dve.wait_ge(free[b], i + 1)
            v.settle()
            for q in range(WT):
                sc(cumx[:, q, :], ra[:, q, :], -1.0, A("rw_k_a", q), ADD, MUL)
            v.settle()
            v.do(nc.vector.scalar_tensor_tensor(out=K_, in0=cumx, scalar=1.0, in1=K_, op0=ADD, op1=MUL))
            v.settle()
            for q in range(WT):
                v.do(nc.vector.scalar_tensor_tensor(out=wcum[:, q, :], in0=R_[:, q, :], scalar=A("rw_r_k", q), in1=K_[:, q, :], op0=MUL, op1=MUL))
            v.settle()
            v.tell(nc.vector.tensor_copy(misc[:, 6:7], misc[:, 7:8]), rk_ok, 1)
            v.settle()
            v.do(nc.vector.memset(wk[:, 0, :], 1.0))
            v.settle()
            v.do(nc.vector.memset(wk[:, 0, :].rearrange("p (c t) -> p c t", t=RC)[:, :, 0:1], 0.0))
            v.settle()
            for q in range(WT):
                v.do(nc.vector.tensor_tensor_scan(cum[:, q, :], wk[:, 0, :], sg[:, q, :], 0.0, MUL, ADD))
            v.settle()
            v.tell(nc.vector.tensor_tensor(cumx, cum, sg, SUB), cum_ok, 1)
            for q in range(WT):
                src, done = got(("kn", q))
                v.do(nc.vector.tensor_scalar(knr[:, q, :], src[:], 1e-24, None, ALU.max))
                v.settle()
                v.tell(nc.vector.tensor_copy(misc[:, 6:7], misc[:, 7:8]), *done)
                v.settle()
            v.do(nc.vector.reciprocal(knr, knr))
            v.settle()
            for q in range(WT):
                v.tell(nc.vector.tensor_copy(misc[:, 6:7], misc[:, 7:8]), kn_ok, q + 1)
                v.settle()
            for q in range(WT):
                src, done = got(("bonus", q))
                v.tell(nc.vector.tensor_tensor(BV[:, q, :], V_[:, q, :], src[:], MUL), *done)
                v.settle()
            v.tell(nc.vector.tensor_copy(misc[:, 6:7], misc[:, 7:8]), cum_ok, 2)
            dve.wait_ge(knr_ok, 1)
            op(kk, kk, knr, MUL)
            v.settle()
            op(ra, ra, kk, MUL)
            dve.wait_ge(dec_ok, 3)
            v.tell(nc.vector.tensor_copy(wce[:], wcum.rearrange("p j (c t) -> p j c t", t=RC)[:, :, :, RC - 1]), rw_ok, 1)
            v.settle()
            v.tell(nc.vector.tensor_tensor(KR[:, 0], kk, wprev, MUL), rw_ok, 2)
            v.tell(nc.vector.tensor_tensor(R_, R_, wcum, MUL), rw_ok, 3)
            v.tell(nc.vector.tensor_tensor(BH, ra, winv, MUL), rw_ok, 4)
            v.tell(nc.vector.tensor_tensor(K_, K_, winv, MUL), rw_ok, 5)
            v.settle()
            v.do(nc.vector.memset(flat(RHs), 0.0))
            v.settle()
            lo = slice(0, 64)
            I8 = ident[0:64, 0:64].unsqueeze(1).to_broadcast([64, RH, 64])
            dve.wait_ge(moved_in, 96)
            for c0 in range(0, NRC, 2):
                for c in (c0, c0 + 1):
                    if c >= 2:
                        dve.wait_ge(ro_ok, 2 * (c - 1))
                    for k in range(4):
                        src, done = got(("gram", c, k))
                        dst = rb(c, 3 + k // 2)[:, 4 * (k % 2):4 * (k % 2) + 4]
                        v.tell(nc.vector.tensor_tensor(dst.rearrange("p h a t -> p h (a t)"), src[lo, :].rearrange("p (h u) -> p h u", h=4),
                                                       rmask[:].rearrange("p a t -> p (a t)").unsqueeze(1).to_broadcast([64, 4, P]), MUL), *done)
                        v.settle()
                        v.tell(nc.vector.tensor_copy(misc[:, 6:7], misc[:, 7:8]), gram_ok, 4 * c + k + 1)
                        v.settle()
                for lv in range(LEV):
                    for c in (c0, c0 + 1):
                        X, XT = rb(c, 5), rb(c, 6)
                        n = XC(c, lv + 1)
                        if lv == 0:
                            src, done = got(("t", c, 0))
                            v.tell(nc.vector.tensor_tensor(X, I8, src[lo, :].rearrange("p (h t) -> p h t", h=RH), SUB), *done)
                            v.settle()
                            v.tell(nc.vector.tensor_copy(misc[:, 6:7], misc[:, 7:8]), x_ok, n - 1)
                            v.settle()
                            dve.wait_ge(of_ok, OC(c, 0))
                            v.tell(nc.vector.tensor_tensor(XT, I8, rb(c, 8), SUB), x_ok, n)
                            v.settle()
                        else:
                            if lv < LEV - 1:
                                src, done = got(("u", c, lv))
                                v.tell(nc.vector.tensor_tensor(flat(X), flat(X), src[lo, :], SUB), *done)
                                v.settle()
                                v.tell(nc.vector.tensor_copy(misc[:, 6:7], misc[:, 7:8]), x_ok, n - 1)
                                v.settle()
                            src, done = got(("ut", c, lv))
                            v.tell(nc.vector.tensor_tensor(flat(XT), flat(XT), src[lo, :], SUB), *done)
                            v.settle()
                            v.tell(nc.vector.tensor_copy(misc[:, 6:7], misc[:, 7:8]), x_ok, n)
                            v.settle()
                for c in (c0, c0 + 1):
                    src, done = got(("h", c))
                    b, i = at[("o", c)]
                    dve.wait_ge(full[b], i + 1)
                    v.tell(nc.vector.tensor_tensor(flat(RHs), flat(RHs), src[lo, :], ADD), *done)
                    v.settle()
                    hv = RHs.rearrange("p (j o) v -> p o j v", o=2)
                    v.do(nc.vector.tensor_tensor(hv[:, 0], hv[:, 0], wce[0:64, :, c].unsqueeze(2).to_broadcast([64, WT, 64]), MUL))
                    v.tell(nc.vector.tensor_tensor(hv[:, 1], hv[:, 1], wco[:, :, c].unsqueeze(2).to_broadcast([64, WT, 64]), MUL), rh_ok, c + 1)
                    v.settle()
            dve.wait_ge(ro_ok, 2 * NRC)
            for q in range(WT):
                src, done = got(("mean", q))
                v.tell(nc.vector.scalar_tensor_tensor(out=Ot[:, q, :], in0=src[:], scalar=-1.0 / RD, in1=Ot[:, q, :], op0=MUL, op1=ADD), *done)
                v.settle()
                v.tell(nc.vector.tensor_tensor(wk[:, 4 + q, :], Ot[:, q, :], Ot[:, q, :], MUL), cen_ok, q + 1)
                v.settle()
            for q in range(WT):
                src, done = got(("var", q))
                v.tell(nc.vector.tensor_scalar(wk[:, q, :], src[:], 1.0 / RD, 64e-5, MUL, ADD), *done)
                v.settle()
            for q in range(WT):
                v.tell(nc.vector.reciprocal(wk[:, q, :], wk[:, q, :]), var_ok, q + 1)
                v.settle()
            dve.wait_ge(var_ok, WT + 1)
            op(Ot, Ot, wk[:, 0:4, :], MUL)
            v.settle()
            for q in range(WT):
                sc(Ot[:, q, :], Ot[:, q, :], A("rw_ln_w", q), A("rw_ln_b", q), MUL, ADD)
            v.settle()
            op(Ot, Ot, BV, ADD)
            v.settle()
            for q in range(WT):
                v.tell(nc.vector.tensor_tensor(V_[:, q, :], Ot[:, q, :], Gt[:, q, :], MUL), rwy_ok, q + 1)

            for n in range(4 * NTT):
                ncol, i = divmod(n, NTT)
                src, done = got(("out", n))
                dve.wait_ge(x2_in, 16 * NTT)
                xc = x2[i][:, 512 * ncol:512 * ncol + 512]
                v.tell(nc.vector.tensor_tensor(xc, xc, src[:], ADD), *done)
                v.settle()
                v.tell(nc.vector.tensor_copy(misc[:, 6:7], misc[:, 7:8]), x2_ok, n + 1)
                v.settle()
            dve.wait_ge(ssx_ok, NTT)
            sc(st[:, 28:32], st[:, 16:20], 1.0 / D, EPS, MUL, ADD)
            v.settle()
            v.tell(nc.vector.reciprocal(st[:, 20:24], st[:, 28:32]), msx_ok, 1)
            dve.wait_ge(rsx_ok, 1)
            dve.wait_ge(gain_in, 16)
            v.settle()
            for i in range(NTT):
                v.tell(nc.vector.scalar_tensor_tensor(
                    out=h2p[i].rearrange("t (c p) -> t p c", p=P), in0=x2[i].rearrange("t (p c) -> t p c", c=NC),
                    scalar=st[:, 24 + i:25 + i], in1=gffn.rearrange("t (p c) -> t p c", c=NC), op0=MUL, op1=MUL), h2_ok, i + 1)

            def red(out, x, o):
                v.do(nc.vector.tensor_reduce(out=out, in_=x, op=o, axis=AX))

            def bc(x, n):
                return x.unsqueeze(2).to_broadcast([P, NTT, n])

            def first(idx, x, m, t):
                op(t, x, bc(m, 8), ALU.is_equal)
                v.settle()
                sc(t, t, -8.0, 8.0, MUL, ADD)
                v.settle()
                op(t, t, i8, ADD)
                v.settle()
                red(idx, t, ALU.min)
                v.settle()

            src, done = got("logit")
            dve.wait_ge(cbc_in, 80)
            dve.wait_ge(ri_ok, 1)
            L = rv(4, NTT, NG + NE)
            v.tell(nc.vector.tensor_tensor(L, src[:, 0:NTT * (NG + NE)].rearrange("p (i n) -> p i n", i=NTT),
                                           rbias.unsqueeze(1).to_broadcast([P, NTT, NG + NE]), ADD), *done)
            v.settle()
            i8 = rv(0, 8).unsqueeze(1).to_broadcast([P, NTT, 8])
            gl, el = L[:, :, 0:NG], L[:, :, NG:]
            t8, es, oh = rv(5, NTT, 8), rv(7, NTT, 8), rv(8, NTT, 8)
            sm = [rt[:, 5600 + 4 * j:5604 + 4 * j] for j in range(12)]
            gm, gi, gs, m1, i1, m2, i2, e1, e2 = sm[:9]
            red(gm, gl, ALU.max)
            v.settle()
            v.tell(nc.vector.tensor_tensor(rv(6, NTT, NG), gl, bc(gm, 8), SUB), re_ok, 1)
            first(gi, gl, gm, t8)
            dve.wait_ge(re_ok, 2)
            red(gs, rv(6, NTT, NG), ADD)
            v.settle()
            v.do(nc.vector.reciprocal(gs, gs))
            op(oh, i8, bc(gi, 8), ALU.is_equal)
            v.settle()
            sel = rv(9, NTT, NG, NPG)
            for i in range(NTT):
                op(sel[:, i], el[:, i].rearrange("p (g j) -> p g j", g=NG), oh[:, i].unsqueeze(2).to_broadcast([P, NG, NPG]), MUL)
            v.settle()
            for i in range(NTT):
                red(es[:, i], sel[:, i].rearrange("p g j -> p j g"), ADD)
            v.settle()
            red(m1, es, ALU.max)
            v.settle()
            first(i1, es, m1, t8)
            op(oh, i8, bc(i1, 8), ALU.is_equal)
            v.settle()
            v.do(nc.vector.scalar_tensor_tensor(out=es, in0=oh, scalar=-1e30, in1=es, op0=MUL, op1=ADD))
            v.settle()
            red(m2, es, ALU.max)
            v.settle()
            first(i2, es, m2, t8)
            v.tell(nc.vector.tensor_tensor(gate[:, 1, :], m2, m1, SUB), re_ok, 3)
            v.do(nc.vector.scalar_tensor_tensor(out=e1, in0=gi, scalar=8.0, in1=i1, op0=MUL, op1=ADD))
            v.do(nc.vector.scalar_tensor_tensor(out=e2, in0=gi, scalar=8.0, in1=i2, op0=MUL, op1=ADD))
            v.settle()
            i64 = rv(1, NE).unsqueeze(1).to_broadcast([P, NTT, NE])
            op(rv(10, NTT, NE), i64, bc(e1, NE), ALU.is_equal)
            op(rv(11, NTT, NE), i64, bc(e2, NE), ALU.is_equal)
            v.settle()
            v.tell(nc.vector.tensor_tensor(rv(12, NTT, NE), rv(10, NTT, NE), rv(11, NTT, NE), ADD), oh_ok, 1)
            dve.wait_ge(re_ok, 4)
            sc(gate[:, 0, :], gate[:, 1, :], 1.0, None, ADD)
            v.settle()
            v.do(nc.vector.reciprocal(gate[:, 0, :], gate[:, 0, :]))
            v.settle()
            op(gate[:, 0, :], gate[:, 0, :], gs, MUL)
            v.settle()
            op(gate[:, 1, :], gate[:, 1, :], gate[:, 0, :], MUL)
            src, done = got("cum")
            v.settle()
            v.do(nc.vector.tensor_copy(rv(13, 320), src[:, 0:320]))
            v.settle()
            cnt = rv(13, 320)[:, 256:320]
            c8 = rt[:, 320 * 14:320 * 14 + 512].rearrange("p (e j) -> p e j", e=NE)
            op(c8, cnt.unsqueeze(2).to_broadcast([P, NE, 8]), rv(2, 8).unsqueeze(1).to_broadcast([P, NE, 8]), ALU.is_gt)
            v.settle()
            nb, pend, pst = (rv(7, 320)[:, 32 + 64 * j:96 + 64 * j] for j in range(3))
            red(nb, c8, ADD)
            v.do(nc.vector.memset(rv(8, 320)[:, 64:128], 1.0))
            v.settle()
            v.do(nc.vector.tensor_tensor_scan(pend, rv(8, 320)[:, 64:128], nb, 0.0, MUL, ADD))
            v.settle()
            op(pst, pend, nb, SUB)
            sc(rv(9, NE), pend, rv(3, 1), None, ALU.is_le)
            v.settle()
            red(rv(3, 320)[:, 1:2], rv(9, NE), ADD)
            sc(pst, pst, float(B))
            v.settle()
            sc(rv(3, 320)[:, 1:2], rv(3, 320)[:, 1:2], float(NE - 1), None, ALU.min)
            v.settle()
            v.tell(nc.vector.tensor_copy(rv(3, 320)[:, 2:3], rv(3, 320)[:, 1:2]), bl_ok, 1)
            place = rv(13, 320)[:, 0:256].rearrange("p (i e) -> p i e", i=NTT)
            op(place, place, pst.unsqueeze(1).to_broadcast([P, NTT, NE]), ADD)
            v.settle()
            for k in range(2):
                op(rv(10 + k, NTT, NE), rv(10 + k, NTT, NE), place, MUL)
                v.settle()
                red(sm[9 + k], rv(10 + k, NTT, NE), ADD)
                v.settle()
                v.do(nc.vector.tensor_copy(desti[:, k, :], sm[9 + k]))
            v.settle()
            v.tell(nc.vector.tensor_copy(misc[:, 6:7], misc[:, 7:8]), dest_ok, 1)
            v.settle()
            src, done = got("row")
            v.do(nc.vector.tensor_copy(rowi[0:1, 0:P], src[0:1, 0:P]))
            v.settle()
            v.tell(nc.vector.tensor_copy(misc[:, 6:7], misc[:, 7:8]), *done)
            sc(sm[11][0:1, 0:1], pend[0:1, NE - 1:NE], 0.5, 0.25, MUL, ADD)
            v.settle()
            sc(sm[11][0:1, 1:2], sm[11][0:1, 0:1], MAGIC, MAGIC, ADD, SUB)
            v.settle()
            v.tell(nc.vector.tensor_copy(rowi[0:1, P:P + 1], sm[11][0:1, 1:2]), rowi_ok, 1)
            dve.wait_ge(tab_io, 16 * (2 * NTT + 2))
            v.tell(nc.vector.tensor_copy(tabf, tabi), tabf_ok, 1)
            src, done = got("tab")
            v.settle()
            v.do(nc.vector.memset(idxg[:, NBLK:NBLK + 2], NROW))
            v.do(nc.vector.tensor_copy(idxs[:, 0:NBLK], src[0:B, 0:NBLK]))
            sc(rt[0:B, 320:320 + NBLK], src[0:B, 0:NBLK], T - 0.5, -float(T), ALU.is_gt, MUL)
            v.settle()
            v.tell(nc.vector.tensor_tensor(rt[0:B, 640:640 + NBLK], rt[0:B, 320:320 + NBLK], src[0:B, 0:NBLK], ADD), *done)
            v.settle()
            v.tell(nc.vector.tensor_copy(idxg[:, 0:NBLK], rt[0:B, 640:640 + NBLK]), idx_ok, 1)
            v.settle()

            dve.wait_ge(spill, 16 * 2 * NTT)
            dve.wait_ge(rowi_ok, 1)
            npairs = dve.value_load(rowi[0:1, P:P + 1], min_val=1, max_val=NBLK // 2)

            def columns(r, k):
                dve.wait_ge(xtp_ok, 4 * r + 2 * k + 2)
                nc.vector.tensor_copy(xT[k][:, 8:16, :].rearrange("p c t -> p (c t)"), ps[1][:]).then_inc(xT2_ok, 1)

            def block_(r, k, nr, nk):
                dve.wait_ge(sil_ok, 2 * r + k + 1)
                nc.vector.tensor_tensor(hid[k].rearrange("p c t -> p (c t)"), sil[k], ps[2 + k][:, FC * B:2 * FC * B], MUL).then_inc(hid_ok, 1)
                columns(nr, nk)
                for n in (1, 3):
                    dve.wait_ge(down_ok, 8 * r + 4 * k + n + 1)
                    if n == 1:
                        wait_y_out(dve, r, k)
                    nc.vector.tensor_copy(yb[k][:, 512 * n:512 * n + 512], ps[4 + n][0:B, :]).then_inc(y_ok[k], 1)

            columns(0, 0)
            block_(0, 0, 0, 1)
            block_(0, 1, 1, 0)
            with dve.Fori(1, NBLK // 2) as r:
                with dve.If(r < npairs):
                    block_(r, 0, r, 1)
                    block_(r, 1, r + 1, 0)
            dve.wait_ge(gain_in, 32)
            for i in range(NTT):
                xf, y0, y1 = (fbuf(i, j) for j in range(3))
                dve.wait_ge(fin_in[i % 2], 48 * (i // 2 + 1))
                v.settle()
                v.do(nc.vector.scalar_tensor_tensor(out=xf, in0=y0, scalar=gate[:, 0, i:i + 1], in1=xf, op0=MUL, op1=ADD))
                v.settle()
                v.tell(nc.vector.scalar_tensor_tensor(out=xf, in0=y1, scalar=gate[:, 1, i:i + 1], in1=xf, op0=MUL, op1=ADD), fin_ok, 4 * i + 1)
                dve.wait_ge(fss_ok, i + 1)
                v.settle()
                v.tell(nc.vector.tensor_scalar(st[:, 44 + i:45 + i], st[:, 32 + i:33 + i], 1.0 / D, EPS, MUL, ADD), fin_ok, 4 * i + 2)
                v.settle()
                v.tell(nc.vector.reciprocal(st[:, 36 + i:37 + i], st[:, 44 + i:45 + i]), fms_ok, i + 1)
                dve.wait_ge(frs_ok, i + 1)
                v.tell(nc.vector.tensor_scalar(xf, xf, st[:, 40 + i:41 + i], None, MUL), fin_ok, 4 * i + 3)
                v.settle()
                v.tell(nc.vector.tensor_tensor(xf, xf, gfin, MUL), fin_ok, 4 * i + 4)

        @block.tensor
        def _(pe):
            pe.wait_ge(const_ok, 1)
            pe.wait_ge(prm_in, NPRM)
            nc.tensor.transpose(ps[6][:, 0:128], prmA, ident[:])
            nc.tensor.transpose(ps[6][:, 128:256], prmB, ident[:]).then_inc(prm_tr, 1)
            pe.wait_ge(ldt_ok, 1)
            pe.wait_ge(s5_in, 16 * 8)
            nc.tensor.transpose(ps[7][:, 0:48], prmC, ident[0:48, 0:48]).then_inc(prm_tr, 1)
            for m in range(NTT * 4):
                i, c4 = divmod(m, 4)
                if c4 == 0:
                    pe.wait_ge(h_ok, i + 1)
                if m >= 4:
                    pe.wait_ge(tr_used, m - 3)
                for j in range(4):
                    c = 4 * c4 + j
                    last = nc.tensor.transpose(ps[2 + m % 4][:, P * j:P * (j + 1)], xs[:, i, P * c:P * (c + 1)], ident[:])
                last.then_inc(tr_ok, 1)
            pe.wait_ge(tr_used, NTT * 4)

            def s5_setup():
                pe.wait_ge(gin_ok, 1)
                for n in range(8):
                    if n >= 4:
                        pe.wait_ge(g_got, n - 3)
                    for j in range(4):
                        last = nc.tensor.transpose(ps[2 + n % 4][:, P * j:P * j + P],
                                                   Gin[n // 4][:, n % 4, P * j:P * j + P], ident[:])
                    last.then_inc(g_tr, 1)
                for r in range(2):
                    pe.wait_ge(g_got, 5 + r)
                    for q in range(WT):
                        last = nc.tensor.transpose(ps[2 + r][:, P * q:P * q + P],
                                                   dupC[:, r, q].rearrange("p u n -> p (u n)"), ident[:])
                    last.then_inc(g_tr, 1)
                pe.wait_ge(g_got, 10)

            def s5_in_mm(p):
                if p >= 2:
                    pe.wait_ge(bu_used, p - 1)
                if p % 4 == 0:
                    pe.wait_ge(proj_got, p // 4 + 1)
                for r in range(2):
                    last = nc.tensor.matmul(ps[2 + 2 * (p % 2) + r][:], s5G[:, r, p, :], U5[:, p // 4, :], start=True, stop=True)
                last.then_inc(bu_ok, 1)

            def s5_out_mm(p):
                pe.wait_ge(st_ok, p + 1)
                if p % 4 == 0 and p:
                    pe.wait_ge(y_used, p // 4)
                o = ps[6][32 * (p % 4):32 * (p % 4) + 32, :]
                for r in range(2):
                    last = nc.tensor.matmul(o, s5C[:, r, p, :], wk[:, 4 + 2 * (p % 2) + r, :], start=(r == 0), stop=(r == 1))
                last.then_inc(st_used, 1)

            def bank(u):
                if u >= 4:
                    pe.wait_ge(mm_used, u - 3)
                return ps[2 + u % 4][:]

            def s5_glu():
                pe.wait_ge(gelu_ok, 1)
                pe.wait_ge(wglu_in, 16)
                for q in range(WT):
                    o = bank(U_GLU + q)
                    for k in range(WT):
                        last = nc.tensor.matmul(o, wglu[:, k, P * q:P * q + P], U5[:, k, :], start=(k == 0), stop=(k == WT - 1))
                    last.then_inc(mm_ok, 1)

            def rms(u, k, sq):
                pe.wait_ge(sq_ok, k + 1)
                o = bank(u)
                for q in range(WT):
                    last = nc.tensor.matmul(o, ones[:], sq[:, q, :], start=(q == 0), stop=(q == WT - 1))
                last.then_inc(mm_ok, 1)

            def lru_gates():
                pe.wait_ge(conv_ok, WT)
                pe.wait_ge(lruw_in, 64)
                for q in range(WT):
                    for r in range(2):
                        o = bank(U_LRU + 2 * q + r)
                        nc.tensor.matmul(o, lruW[:, r, q, :], wk[:, q, :], start=True, stop=True).then_inc(mm_ok, 1)

            def fill(name):
                b, i = at[name]
                if i:
                    pe.wait_ge(free[b], i)
                return ps[b], full[b]

            def ssd_dt():
                pe.wait_ge(wdt_in, 16)
                pe.wait_ge(mm_used, U_RMSL + 1)
                o, done = fill("dt")
                for i in range(NTT):
                    for k in range(NC):
                        last = nc.tensor.matmul(o[:, SH * i:SH * (i + 1)], hT[:, k, P * i:P * (i + 1)], wdt[:, k, :],
                                                start=(k == 0), stop=(k == NC - 1))
                last.then_inc(done, 1)

            def ssd_cs():
                pe.wait_ge(adt_ok, 1)
                pe.wait_ge(mask_ok, 1)
                o, done = fill("cs")
                nc.tensor.matmul(o[:, 0:32], tri[:], sds[:, 3, :], start=True, stop=True)
                nc.tensor.matmul(o[:, 32:64], ones[:], sds[:, 3, :], start=True, stop=True).then_inc(done, 1)

            def ssd_tokens():
                pe.wait_ge(silu_ok, 8)
                for i in range(NTT):
                    o, done = fill(("xt", i))
                    for q in range(WT):
                        last = nc.tensor.transpose(o[:, P * q:P * q + P], XBC[:, q, P * i:P * i + P], ident[:])
                    last.then_inc(done, 1)
                for i in range(2):
                    o, done = fill(("bt", i))
                    for j in range(4):
                        c, g = 2 * i + j // 2, j % 2
                        last = nc.tensor.transpose(o[:, P * j:P * j + P], XBC[:, 4 + g, P * c:P * c + P], ident[:])
                    last.then_inc(done, 1)

            def ssd_chunk(c):
                cols = slice(P * c, P * c + P)
                for k in range(2):
                    o, done = fill(("row", c, k))
                    for j in range(4):
                        h = 4 * k + j
                        nc.tensor.matmul(o[:, P * j:P * j + P], sds[:, 3, SH * c + h:SH * c + h + 1].to_broadcast([P, P]), tri[:],
                                         start=True, stop=False)
                        last = nc.tensor.matmul(o[:, P * j:P * j + P], ident[:], maskneg[:], start=False, stop=True)
                    last.then_inc(done, 1)
                o, done = fill(("score", c))
                for g in range(2):
                    last = nc.tensor.matmul(o[:, P * g:P * g + P], XBC[:, 4 + g, cols], XBC[:, 6 + g, cols], start=True, stop=True)
                last.then_inc(done, 1)
                pe.wait_ge(xe_ok, c + 1)
                for i in range(2):
                    b, n = at[("bt", i)]
                    pe.wait_ge(free[b], n + 1)
                o, done = fill(("state", c))
                for g in range(2):
                    last = nc.tensor.matmul(o[:, 256 * g:256 * g + 256], BT[:, c, g, :], XE[:, c, 256 * g:256 * g + 256], start=True, stop=True)
                last.then_inc(done, 1)
                if c:
                    b, n = at[("state", c - 1)]
                    pe.wait_ge(free[b], n + 1)
                    o, done = fill(("off", c))
                    for g in range(2):
                        last = nc.tensor.matmul(o[:, 256 * g:256 * g + 256], XBC[:, 6 + g, cols], SH_[:, (c - 1) % 2, 256 * g:256 * g + 256],
                                                start=True, stop=True)
                    last.then_inc(done, 1)
                b, n = at[("score", c)]
                pe.wait_ge(free[b], n + 1)
                o, done = fill(("diag", c))
                for h in range(SH):
                    last = nc.tensor.matmul(o[:, 64 * h:64 * h + 64], DM[:, c % 2, h, :], XD[:, c, 64 * h:64 * h + 64], start=True, stop=True)
                last.then_inc(done, 1)

            def ssd_out():
                b, n = at[("diag", NSC - 1)]
                pe.wait_ge(free[b], n + 1)
                for q in range(WT):
                    o, done = fill(("yt", q))
                    for c in range(NSC):
                        last = nc.tensor.transpose(o[:, P * c:P * c + P], YT[:, c, P * q:P * q + P], ident[:])
                    last.then_inc(done, 1)
                pe.wait_ge(ssq2_ok, 1)
                o, done = fill("rms_s")
                for q in range(WT):
                    last = nc.tensor.matmul(o[:], ones[:], wk2[:, 4 + q, :], start=(q == 0), stop=(q == WT - 1))
                last.then_inc(done, 1)

            for n, (s, c, wd, d) in enumerate(tiles):
                pe.wait_ge(w_in_slot[s % 2], 16 * (s // 2 + 1))
                if n >= 2:
                    pe.wait_ge(proj_got, n - 1)
                for k in range(NC):
                    last = nc.tensor.matmul(ps[n % 2][0:wd, :], ring[s % 2][:, k, c:c + wd], hT[:, k, :],
                                            start=(k == 0), stop=(k == NC - 1))
                last.then_inc(proj_ok, 1)
                if n == 3:
                    s5_setup()
                if 4 <= n < 12:
                    for p in (2 * n - 8, 2 * n - 7):
                        s5_in_mm(p)
                        if p:
                            s5_out_mm(p - 1)
                if n == 11:
                    s5_out_mm(NPAIR - 1)
                if n == 12:
                    s5_glu()
                if n == 14:
                    rms(U_RMS5, 0, wk2[:, 4:8, :])
                if n == 15:
                    lru_gates()
                if n == 18:
                    rms(U_RMSL, 1, wk[:, 0:4, :])
                if n == 23:
                    ssd_dt()
                if n == 25:
                    ssd_cs()
                if n == 26:
                    ssd_tokens()
                if n >= 28 and n % 2 == 0 and n < 28 + 2 * NSC:
                    ssd_chunk((n - 28) // 2)
                if n == 28 + 2 * NSC:
                    ssd_out()
            assert NT > 28 + 2 * NSC

            pe.wait_ge(lot_ok, 2)
            pe.wait_ge(lora_in, 48)
            for q in range(WT):
                for r, (k0, k1, t) in enumerate(((0, LW, 0), (LW, LW + LA, 0), (0, LG, 1))):
                    o, done = fill(("lora", q, r))
                    nc.tensor.matmul(o[:], loraW[k0:k1, t, P * q:P * q + P], LO[k0:k1, t, :], start=True, stop=True).then_inc(done, 1)
            pe.wait_ge(ksq_ok, 1)
            for q in range(WT):
                o, done = fill(("kn", q))
                nc.tensor.matmul(o[:], blk64[:], wprev[:, q, :], start=True, stop=True).then_inc(done, 1)
            pe.wait_ge(rk_ok, 1)
            for q in range(WT):
                o, done = fill(("bonus", q))
                nc.tensor.matmul(o[:], blk64[:], wcum[:, q, :], start=True, stop=True).then_inc(done, 1)
            pe.wait_ge(rw_ok, 5)
            pe.wait_ge(moved_in, 96)
            arr = [KR[:, 0], KR[:, 1], BH, K_, V_]

            def dims(a, h, c):
                cols = slice(RC * c, RC * c + RC)
                return arr[a][0:64, h // 2, cols] if h % 2 == 0 else moved[:, a, h // 2, cols]

            def dims2(h, c):
                cols = slice(RC * c, RC * c + RC)
                return KR[0:64, :, h // 2, cols] if h % 2 == 0 else moved[:, 0:2, h // 2, cols]

            lo = slice(0, 64)

            def hd(o, h):
                return o[lo, 64 * h:64 * h + 64]

            for c0 in range(0, NRC, 2):
                for c in (c0, c0 + 1):
                    for k, a in enumerate((2, 3, 4)):
                        o, done = fill(("tm", c, k))
                        for h in range(RH):
                            last = nc.tensor.transpose(hd(o, h), dims(a, h, c), ident[0:64, 0:64])
                        last.then_inc(done, 1)
                    for k in range(4):
                        o, done = fill(("gram", c, k))
                        for h in range(4 * (k % 2), 4 * (k % 2) + 4):
                            last = nc.tensor.matmul(o[lo, P * (h % 4):P * (h % 4) + P], dims(2 + k // 2, h, c), dims2(h, c), start=True, stop=True)
                        last.then_inc(done, 1)
                for lv in range(LEV):
                    for c in (c0, c0 + 1):
                        o, done = fill(("t", c, lv))
                        pe.wait_ge(of_ok, OC(c, lv))
                        if lv:
                            pe.wait_ge(x_ok, XC(c, lv))
                        for h in range(RH):
                            last = nc.tensor.matmul(hd(o, h), rb(c, 8)[:, h], rb(c, 5)[:, h] if lv else ident[0:64, 0:64], start=True, stop=True)
                        last.then_inc(done, 1)
                    for c in (c0, c0 + 1):
                        if lv:
                            b, i = at[("t", c, lv)]
                            pe.wait_ge(free[b], i + 1)
                        if lv and lv < LEV - 1:
                            o, done = fill(("u", c, lv))
                            for h in range(RH):
                                last = nc.tensor.matmul(hd(o, h), rb(c, 6)[:, h], rb(c, 7)[:, h], start=True, stop=True)
                            last.then_inc(done, 1)
                        if lv:
                            o, done = fill(("ut", c, lv))
                            for h in range(RH):
                                last = nc.tensor.matmul(hd(o, h), rb(c, 7)[:, h], rb(c, 6)[:, h], start=True, stop=True)
                            last.then_inc(done, 1)
                for c in (c0, c0 + 1):
                    Bt, Kt, Vt, G1, G2, XT = (rb(c, k) for k in (0, 1, 2, 3, 4, 6))
                    for k in range(3):
                        b, i = at[("tm", c, k)]
                        pe.wait_ge(free[b], i + 1)
                    pe.wait_ge(gram_ok, 4 * c + 4)
                    pe.wait_ge(x_ok, XC(c, LEV))
                    if c:
                        pe.wait_ge(rh_ok, c)
                    o, done = fill(("y", c))
                    for h in range(RH):
                        nc.tensor.matmul(hd(o, h), dims(0, h, c), RHs[:, h], start=True, stop=False)
                        last = nc.tensor.matmul(hd(o, h), G2[:, h, 0], Vt[:, h], start=False, stop=True)
                    last.then_inc(done, 1)
                    b, i = at[("y", c)]
                    pe.wait_ge(free[b], i + 1)
                    o, done = fill(("un", c))
                    for h in range(RH):
                        last = nc.tensor.matmul(hd(o, h), XT[:, h], RY[:, h], start=True, stop=True)
                    last.then_inc(done, 1)
                    b, i = at[("un", c)]
                    pe.wait_ge(free[b], i + 1)
                    o, done = fill(("h", c))
                    for h in range(RH):
                        nc.tensor.matmul(hd(o, h), Kt[:, h], Vt[:, h], start=True, stop=False)
                        last = nc.tensor.matmul(hd(o, h), Bt[:, h], RU[:, h], start=False, stop=True)
                    last.then_inc(done, 1)
                    o, done = fill(("o", c))
                    for h in range(RH):
                        nc.tensor.matmul(hd(o, h), RHs[:, h], dims(1, h, c), start=True, stop=False)
                        nc.tensor.matmul(hd(o, h), RU[:, h], G1[:, h, 1], start=False, stop=False)
                        last = nc.tensor.matmul(hd(o, h), Vt[:, h], G2[:, h, 1], start=False, stop=True)
                    last.then_inc(done, 1)
            pe.wait_ge(ro_ok, 2 * NRC)
            for q in range(WT):
                o, done = fill(("mean", q))
                nc.tensor.matmul(o[:], blk64[:], Ot[:, q, :], start=True, stop=True).then_inc(done, 1)
            for q in range(WT):
                pe.wait_ge(cen_ok, q + 1)
                o, done = fill(("var", q))
                nc.tensor.matmul(o[:], blk64[:], wk[:, 4 + q, :], start=True, stop=True).then_inc(done, 1)

            pe.wait_ge(rwy_ok, WT)
            pe.wait_ge(mix_ok, 12)
            for n in range(4 * NTT):
                ncol, i = divmod(n, NTT)
                pe.wait_ge(wo_in[ncol % 2], 16 * (ncol // 2 + 1))
                o, done = fill(("out", n))
                for c in range(NC):
                    last = nc.tensor.matmul(o[:], mixed[c][:, P * i:P * i + P], woslab[ncol % 2][:, c, :], start=(c == 0), stop=(c == NC - 1))
                last.then_inc(done, 1)
            for m in range(4 * NTT):
                i, c4 = divmod(m, 4)
                pe.wait_ge(h2_ok, i + 1)
                o, done = fill(("h2", m))
                for j in range(4):
                    c = 4 * c4 + j
                    last = nc.tensor.transpose(o[:, P * j:P * j + P], h2p[i][:, P * c:P * c + P], ident[:])
                last.then_inc(done, 1)
            pe.wait_ge(wr_in, 32)
            for b in range(2, 6):
                pe.wait_ge(free[b], max(i for bb, i in at.values() if bb == b) + 1)
            o, done = fill("logit")
            for i in range(NTT):
                for c in range(NC):
                    last = nc.tensor.matmul(o[:, (NG + NE) * i:(NG + NE) * (i + 1)], h2T[:, c, P * i:P * i + P], wr[:, c, :],
                                            start=(c == 0), stop=(c == NC - 1))
            last.then_inc(done, 1)
            pe.wait_ge(oh_ok, 1)
            o, done = fill("cum")
            ohs = rv(12, NTT, NE)
            for i in range(NTT):
                oi = o[:, NE * i:NE * i + NE]
                nc.tensor.matmul(oi, tris[:], ohs[:, i, :], start=True, stop=(i == 0))
                for j in range(i):
                    nc.tensor.matmul(oi, ones[:], ohs[:, j, :], start=False, stop=(j == i - 1))
            for j in range(NTT):
                last = nc.tensor.matmul(o[:, NTT * NE:NTT * NE + NE], ones[:], ohs[:, j, :], start=(j == 0), stop=(j == NTT - 1))
            last.then_inc(done, 1)
            pe.wait_ge(bl_ok, 1)
            o, done = fill("row")
            nc.tensor.matmul(o[0:1, 0:P], rv(3, 320)[:, 2:3], ident[:], start=True, stop=True).then_inc(done, 1)
            pe.wait_ge(tabf_ok, 1)
            o, done = fill("tab")
            nc.tensor.transpose(o[0:B, 0:NBLK], tabf, ident[0:NBLK, 0:NBLK]).then_inc(done, 1)

            pe.wait_ge(idx_ok, 1)
            pe.wait_ge(rowi_ok, 1)
            pe.wait_ge(spill, 16 * 2 * NTT)
            npairs = pe.value_load(rowi[0:1, P:P + 1], min_val=1, max_val=NBLK // 2)

            def turn(r, k, first):
                pe.wait_ge(xg_in[k], 16 * (r + 1))
                if first:
                    pe.wait_ge(xz_ok, k + 1)
                for h in range(2):
                    if not (first and k == 0):
                        pe.wait_ge((xT_ok, xT2_ok)[h], 2 * r + k)
                    pe.sem_inc(passed, 1)
                    for j in range(8):
                        c = 8 * h + j
                        last = nc.tensor.transpose(ps[h][:, B * j:B * j + B], xg[k][:, P * c:P * c + P], ident[0:B, 0:B])
                    last.then_inc(xtp_ok, 1)

            def up(r, k, first):
                pe.wait_ge(w1_in[k], 32 * (r + 1))
                pe.wait_ge(xT_ok, 2 * r + k + 1)
                pe.wait_ge(xT2_ok, 2 * r + k + 1)
                if not first:
                    pe.wait_ge(hid_ok, 2 * r + k - 1)
                for w in range(2):
                    for m in range(FC):
                        o = ps[2 + k][:, B * (FC * w + m):B * (FC * w + m) + B]
                        for c in range(NC):
                            last = nc.tensor.matmul(o, W13[k][w][:, c, P * m:P * m + P], xT[k][:, c, :], start=(c == 0), stop=(c == NC - 1))
                last.then_inc(up_ok, 1)

            def down(r, k, first):
                pe.wait_ge(hid_ok, 2 * r + k + 1)
                pe.wait_ge(w2_in[k], 16 * (r + 1))
                for n in range(4):
                    if k == 1:
                        pe.wait_ge(y_ok[0], 4 * r + 4) if n == 0 else None
                    elif not first and n == 0:
                        pe.wait_ge(y_ok[1], 4 * r)
                    for c in range(FC):
                        last = nc.tensor.matmul(ps[4 + n][0:B, :], hid[k][:, c, :], W2[k][:, c, 512 * n:512 * n + 512],
                                                start=(c == 0), stop=(c == FC - 1))
                    last.then_inc(down_ok, 1)

            def pair(r, first):
                up(r, 0, first)
                turn(r, 1, first)
                down(r, 0, first)
                up(r, 1, first)
                turn(r + 1, 0, False)
                down(r, 1, first)

            turn(0, 0, True)
            pair(0, True)
            with pe.Fori(1, NBLK // 2) as r:
                with pe.If(r < npairs):
                    pair(r, False)


def kernel(**inputs):
    import numpy as _np
    import concourse.bacc as _bacc
    from concourse import mybir as _mybir
    from concourse.bass_utils import run_bass_kernel_spmd as _run

    nc = _bacc.Bacc("TRN2", target_bir_lowering=False, num_devices=1)
    arrays, aps = {}, {}
    for name, value in inputs.items():
        a = _np.ascontiguousarray(value)
        arrays[f"in_{name}"] = a
        aps[name] = nc.dram_tensor(f"in_{name}", a.shape, _mybir.dt.from_np(a.dtype), kind="ExternalInput").ap()
    dt = _mybir.dt.float32
    out = nc.dram_tensor("out_0", (1, 512, 2048), dt, kind="ExternalOutput").ap()
    build(nc, aps, out)
    r = _run(nc, [arrays], core_ids=[0])
    return r.results[0]["out_0"]
```

```python
from contextlib import ExitStack

import concourse.bass as bass
from concourse import mybir

P = 128
F32 = mybir.dt.float32
I32 = mybir.dt.int32
ALU = mybir.AluOpType
ACT = mybir.ActivationFunctionType
AX = mybir.AxisListType.X

T = 512
D = 2048
NC = D // P
NTT = T // P
W = D // 4
WT = W // P
EPS = 1e-6
MAGIC = 1.5 * 2.0 ** 23

S5_G, S5_N, S5_H = 32, 64, 16
NPAIR = S5_G // 2
FINE, COARSE = 32, 16
RH, RD = 8, 64
LW, LA, LG = 32, 32, 96
RC = 64
NRC = T // RC
INV_SQRT_E = 0.6065306597126334
SH, SN, SC = 8, 128, 128
DTW = LG + SH
NSC = T // SC
NG, NPG, NE, FF = 8, 8, 64, 384
B = 64
NBLK = (2 * T + NE * (B - 1)) // B + 1
NROW = 4096
FC = FF // P

C_S5, C_XL, C_GL, C_R = 0, 512, 1024, 1536
C_LORA = C_R + 3 * W
C_XG = C_LORA + LW + LA
C_Z = C_XG + LG
C_XBC = C_Z + W
C_DT = C_XBC + 1024
IN_COLS = C_DT + SH


class Steps:

    def __init__(self, eng, sem):
        self.eng, self.sem, self.n = eng, sem, 0
        self.last = None

    def do(self, ins):
        ins.then_inc(self.sem, 1)
        self.n += 1
        self.last = (self.sem, self.n)

    def tell(self, ins, sem, value):
        ins.then_inc(sem, 1)
        self.last = (sem, value)

    def settle(self):
        self.eng.wait_ge(*self.last)


def param_rows():
    a, b = {}, {}
    n = 0
    for name, rows in (("s5_d", 4), ("s5_b_glu", 4), ("s5_gain", 4), ("lru_conv_w", 16), ("lru_conv_b", 4),
                       ("lru_ba", 4), ("lru_bx", 4), ("lru_a_param", 4), ("lru_gain", 4), ("rw_mu", 12),
                       ("rw_w0", 4), ("rw_a0", 4), ("rw_k_k", 4), ("rw_k_a", 4), ("rw_r_k", 4),
                       ("rw_ln_w", 4), ("rw_ln_b", 4), ("ssd_norm_w", 4)):
        a[name] = (n, rows)
        n += rows
    n = 0
    for name, rows in (("ssd_conv_w", 32), ("ssd_conv_b", 8), ("norm_mix", 16)):
        b[name] = (n, rows)
        n += rows
    return a, b


PA, PB = param_rows()
MU_LORA = 56


def build(nc, I, out):
    with ExitStack() as ctx:
        def sb(name, shape, dt=F32):
            return ctx.enter_context(nc.sbuf_tensor(name, shape, dt))

        def sem(name):
            return ctx.enter_context(nc.semaphore(name))

        big = sb("big", [P, 96, 512])
        hT = big[:, 0:16, :]
        ring = [big[:, 16 + 8 * i:24 + 8 * i, :].rearrange("p a n -> p (a n)").rearrange("p (k n) -> p k n", k=NC)
                for i in range(2)]
        proj = big[:, 32:70, :]
        U5, XL, GL = proj[:, 0:4, :], proj[:, 4:8, :], proj[:, 8:12, :]
        R_, K_, V_ = proj[:, 12:16, :], proj[:, 16:20, :], proj[:, 20:24, :]
        LO = proj[:, 24:26, :]
        Z_, XBC = proj[:, 26:30, :], proj[:, 30:38, :]
        xs = proj[:, 22:38, :].rearrange("p a n -> p (a n)").rearrange("p (i d) -> p i d", i=NTT)
        s5tab = proj[:, 20:24, :]
        rawB = proj[:, 16, :].rearrange("p (r g h) -> p r g h", r=2, g=NPAIR)
        dupC = proj[:, 18:20, :].rearrange("p r (q u n) -> p r q u n", q=WT, u=2)
        Gin = [proj[:, 12:16, :], big[:, 78:82, :]]
        ptmp = proj[:, 24:26, :]
        wk2 = big[:, 88:96, :]
        wk = big[:, 70:78, :]
        wglu = big[:, 78:82, :]
        lruW = big[:, 82:84, :].rearrange("p a (t c) -> p a t c", t=WT)
        loraW = big[:, 84:86, :]
        s5C = big[:, 86:88, :].rearrange("p r (g c) -> p r g c", g=NPAIR)
        s5G = big[:, 88:96, :].rearrange("p a n -> p (a n)").rearrange("p (r g c) -> p r g c", r=2, g=NPAIR)

        ident = sb("ident", [P, P])
        ones = sb("ones", [P, P])
        prmA, prmB, prmC = proj[:, 8, 0:P], proj[:, 8, P:2 * P], proj[0:48, 8, 2 * P:3 * P]
        colA = sb("colA", [P, P])
        colB = sb("colB", [P, P])
        colC = sb("colC", [P, 48])
        ldt = sb("ldt", [NPAIR, 2])
        st = sb("st", [P, 64])
        eps64 = sb("eps64", [P, 1])
        s5v = sb("s5v", [P, 16, NPAIR])
        misc = sb("misc", [P, 16])
        zero = sb("zero", [P, 1])
        halfpi = sb("halfpi", [P, 1])
        epsb = sb("epsb", [P, 1])
        tk = sb("tk", [P, FINE + COARSE])
        cosF, sinF = (proj[:, i:i + 2, :].rearrange("p a n -> p (a n)")[:, 0:NPAIR * (FINE + COARSE)]
                      .rearrange("p (g k) -> p g k", g=NPAIR) for i in (26, 28))
        lsp = sb("lsp", [P, 6, WT])
        ssdt = sb("ssdt", [P, NSC, SH])

        ps = [ctx.enter_context(nc.psum_tensor(f"ps{i}", [P, 512], F32)) for i in range(8)]

        def A(name, i=0):
            r, _ = PA[name]
            return colA[:, r + i:r + i + 1]

        def Bc(name, i=0):
            r, _ = PB[name]
            return colB[:, r + i:r + i + 1]

        KR = big[:, 40:48, :].rearrange("p (a j) n -> p a j n", a=2)
        XT_, XD, YT, XE = wk2[:, 0:4, :], wk2[:, 4:8, :], wk[:, 4:8, :], wk[:, 0:4, :]
        BT = big[:, 82:84, :].rearrange("p a n -> p (a n)").rearrange("p (c g n) -> p c g n", c=NSC, g=2)
        DM = big[:, 40:44, :].rearrange("p (u a) n -> p u (a n)", u=2).rearrange("p u (h l) -> p u h l", h=SH)
        SH_ = big[:, 86:88, :]
        Gt, BV, Ot = big[:, 92:96, :], big[:, 88:92, :], big[:, 20:24, :]
        BK_ = big[:, 78:86, :].rearrange("p a n -> p (a n)").rearrange("p (j c a t) -> p j c a t", j=WT, c=NRC, a=2)
        movedBK = big[0:64, 8:16, :].rearrange("p a n -> p (a n)").rearrange("p (j c a t) -> p j c a t", j=WT, c=NRC, a=2)
        moved = big[0:64, 0:20, :].rearrange("p (a j) n -> p a j n", a=5)

        def OF(c, lv):
            i = (57 if c % 2 else 56) if lv % 2 else (77 if c % 2 else 31)
            return big[0:64, i, :].rearrange("p (h t) -> p h t", h=RH)

        def rb(c, k):
            i, n, parts = {"BK": (0, 1, P), "UV": (1, 1, P), "G": (2, 2, P), "XT": (4, 2, 64), "X": (6, 1, 64)}[k]
            i += 70 if c % 2 else 24
            flat_ = big[0:parts, i:i + n, :].rearrange("p a n -> p (a n)")
            if n == 2:
                return flat_.rearrange("p (h a t) -> p h a t", h=RH, a=2)
            return flat_.rearrange("p (h t) -> p h t", h=RH)

        RHS = [big[0:64, i, :].rearrange("p (h t) -> p h t", h=RH) for i in (68, 86)]
        RY = big[0:64, 69, :].rearrange("p (h t) -> p h t", h=RH)
        cbc = sb("cbc", [P, 4, SH])
        tri = sb("tri", [P, P])
        tris = sb("tris", [P, P])
        maskneg = sb("maskneg", [P, P])
        sds = sb("sds", [P, 8, NSC * SH])
        blk64 = sb("blk64", [P, P])
        rmask = sb("rmask", [P, 2, 64])
        emask = proj[0:64, 17, 0:448].rearrange("p (i t) -> p i t", i=7)
        lvm = sb("lvm", [64, 6, 64])
        wce = sb("wce", [P, WT, NRC])
        wco = sb("wco", [64, WT, NRC])

        sg, ra, kk, cum, cumx, wcum, winv, wprev = (big[:, 4 * i:4 * i + 4, :] for i in range(8))
        knr = wk[:, 4:8, :]
        zroot = big[:, 87, :]
        mixd = big[:, 78:82, :]

        mixed = [U5[:, q, :] for q in range(WT)] + [XL[:, q, :] for q in range(WT)] + [V_[:, q, :] for q in range(WT)] \
            + [Z_[:, q, :] for q in range(WT)]

        def wide(i, n=4):
            return big[:, i:i + n, :].rearrange("p a n -> p (a n)")

        x2 = [wide(16 + 4 * i) for i in range(NTT)]
        woslab = [big[:, 0:16, :], big[:, 62:78, :]]
        h2p = [wide(78 + 4 * i) for i in range(NTT)]
        gffn = wide(44)
        h2T = big[:, 0:16, :]
        wr = wide(40)[:, 0:NC * (NG + NE)].rearrange("p (c n) -> p c n", c=NC)
        W13 = [[wide(36 * k + 12 * r, 12).rearrange("p (c f) -> p c f", c=NC) for r in range(2)] for k in range(2)]
        W2 = [wide(36 * k + 24, 12).rearrange("p (c n) -> p c n", c=FC) for k in range(2)]
        xg = [wide(80 + 4 * k)[0:B, :] for k in range(2)]
        yb = [wide(72 + 4 * k)[0:B, :] for k in range(2)]
        xT = [wide(88 + 2 * k, 2).rearrange("p (c t) -> p c t", c=NC) for k in range(2)]
        hid = [big[:, 92 + k, 0:FC * B].rearrange("p (c t) -> p c t", c=FC) for k in range(2)]
        sil = [big[:, 92 + k, 256:256 + FC * B] for k in range(2)]
        rt = wide(62, 12)

        hd = nc.dram_tensor("h_rows", (T, D), F32, kind="Internal").ap()
        x2d = nc.dram_tensor("x2_rows", (T, D), F32, kind="Internal").ap()
        yd = nc.dram_tensor("y_rows", (2 * T, D), F32, kind="Internal").ap()
        tokd = nc.dram_tensor("tok_rows", (NBLK * B, 1), I32, kind="Internal").ap()

        def rv(i, *shape):
            n = 1
            for z in shape:
                n *= z
            v_ = rt[:, 320 * i:320 * i + n]
            names = "abc"[:len(shape)]
            return v_ if len(shape) == 1 else v_.rearrange("p (" + " ".join(names) + ") -> p " + " ".join(names),
                                                            **{k: z for k, z in zip(names, shape)})

        tokv = rt[:, 5700:5708].bitcast(I32).rearrange("p (k i) -> p k i", k=2)
        desti = rt[:, 5720:5728].bitcast(I32).rearrange("p (k i) -> p k i", k=2)
        tini = rt[0:NBLK, 5760:5760 + B].bitcast(I32)
        tabi = rt[0:NBLK, 5840:5840 + B].bitcast(I32)
        tabf = rt[0:NBLK, 5920:5920 + B]
        gate = sb("gate", [P, 2, NTT])
        idxg = sb("idxg", [B, NBLK + 2], I32)
        idxs = sb("idxs", [B, NBLK + 2], I32)
        rowi = sb("rowi", [1, P + 2], I32)
        gix, six = ([sb(f"{n}{k}", [B, 1], I32) for k in range(2)] for n in ("gix", "six"))

        fills, at = {}, {}

        def plan(name, bank):
            at[name] = (bank, fills.get(bank, 0))
            fills[bank] = fills.get(bank, 0) + 1

        plan("dt", 6)
        plan("cs", 7)
        for i in range(NTT):
            plan(("xt", i), 2 + i)
        for i in range(2):
            plan(("bt", i), 6 + i)
        for c in range(NSC):
            plan(("row", c, 0), 2)
            plan(("row", c, 1), 3)
            plan(("score", c), 4)
            plan(("state", c), 7)
            if c:
                plan(("off", c), 6)
            plan(("diag", c), 5)
        for q in range(WT):
            plan(("yt", q), 2 + q)
        plan("rms_s", 6)
        for q in range(WT):
            for r in range(3):
                plan(("lora", q, r), 2 + (3 * q + r) % 6)
        for q in range(WT):
            plan(("kn", q), 2 + q)
        for q in range(WT):
            plan(("bonus", q), 2 + (q + 4) % 6)
        LEV = 6
        for c0 in range(0, NRC, 2):
            for c in (c0, c0 + 1):
                for k in range(2):
                    plan(("tm", c, k), k)
                for k in range(2):
                    plan(("gram", c, k), 3 + k)
            for lv in range(LEV):
                for c in (c0, c0 + 1):
                    plan(("t", c, lv), 3 * (c % 2))
                for c in (c0, c0 + 1):
                    if lv:
                        for k in range(2):
                            plan(("u", c, lv, k), 3 * (c % 2) + 1 + k)
            for c in (c0, c0 + 1):
                plan(("y", c), 6)
                plan(("un", c), 7)
                plan(("h", c), 0)
                plan(("o", c), 1)
        for q in range(WT):
            plan(("mean", q), 2 + q)
        for q in range(WT):
            plan(("var", q), 2 + q)

        for n in range(4 * NTT):
            plan(("out", n), n % 2)
        for m in range(4 * NTT):
            plan(("h2", m), 2 + m % 4)
        plan("logit", 6)
        plan("cum", 7)
        plan("row", 0)
        plan("tab", 1)

        x2_in, x2_ok, ssx_ok, msx_ok, rsx_ok = (sem(n) for n in ("x2_in", "x2_ok", "ssx_ok", "msx_ok", "rsx_ok"))
        wo_in = [sem("wo0_in"), sem("wo1_in")]
        gain_in, h2_ok, wr_in, spill = sem("gain_in"), sem("h2_ok"), sem("wr_in"), sem("spill")
        ri_ok, re_ok, oh_ok, bl_ok, dest_ok, rowi_ok = (sem(n) for n in ("ri_ok", "re_ok", "oh_ok", "bl_ok", "dest_ok", "rowi_ok"))
        tab_io, tabf_ok, idx_ok = (sem(n) for n in ("tab_io", "tabf_ok", "idx_ok"))
        w1_in, w2_in, xg_in, y_out = ([sem(f"{n}{k}") for k in range(2)] for n in ("w13_in", "w2_in", "xg_in", "y_out"))
        gcp_ok, y_ok = ([sem(f"{n}{k}") for k in range(2)] for n in ("gcp_ok", "y_ok"))
        xT_ok, xT2_ok, up_ok, down_ok, sil_ok, hid_ok, xz_ok = (
            sem(n) for n in ("xT_ok", "xT2_ok", "up_ok", "down_ok", "sil_ok", "hid_ok", "xz_ok"))
        fin_ok, fss_ok, frs_ok, fsum_ok, out_ok = (
            sem(n) for n in ("fin_ok", "fss_ok", "frs_ok", "fsum_ok", "out_ok"))
        full = [sem(f"bank{i}_full") for i in range(8)]
        free = [sem(f"bank{i}_free") for i in range(8)]
        cbc_in, dtx_ok, dte_ok, adt_ok = sem("cbc_in"), sem("dtx_ok"), sem("dte_ok"), sem("adt_ok")
        csd_ok, cse_ok = sem("csd_ok"), sem("cse_ok")
        sconv_ok, silu_ok, z_ok = sem("sconv_ok"), sem("silu_ok"), sem("z_ok")
        xe_ok, seg_ok, segx_ok = (sem(n) for n in ("xe_ok", "seg_ok", "segx_ok"))
        ssq2_ok = sem("ssq2_ok")
        mask_ok = sem("mask_ok")
        lo_ok, lot_ok, ksq_ok, kn_ok, knr_ok = (sem(n) for n in ("lo_ok", "lot_ok", "ksq_ok", "kn_ok", "knr_ok"))
        cum_ok, dec_ok, rk_ok, rw_ok, moved_in = (sem(n) for n in ("cum_ok", "dec_ok", "rk_ok", "rw_ok", "moved_in"))
        of_ok = sem("of_ok")
        rh_ok, ro_ok, cen_ok = (sem(n) for n in ("rh_ok", "ro_ok", "cen_ok"))
        var_ok, rwy_ok = sem("var_ok"), sem("rwy_ok")
        x_in = [sem(f"x_in{i}") for i in range(NTT)]
        prm_in = sem("prm_in")
        s5_in = sem("s5_in")
        w_in_slot = [sem("slab0_in"), sem("slab1_in")]
        wdt_in = sem("wdt_in")
        wglu_in, lruw_in, lora_in = sem("wglu_in"), sem("lruw_in"), sem("lora_in")
        dve_s, act_s, pool_s = sem("dve_step"), sem("act_step"), sem("pool_step")
        const_ok = sem("const_ok")
        zero_ok = sem("zero_ok")
        ssq_ok = sem("ssq_ok")
        ms_ok, rs_ok = sem("ms_ok"), sem("rs_ok")
        h_ok = sem("h_ok")
        tr_ok, tr_used = sem("tr_ok"), sem("tr_used")
        prm_tr, prm_col = sem("prm_tr"), sem("prm_col")
        gin_zero, bbar_ok, gin_ok = sem("gin_zero"), sem("bbar_ok"), sem("gin_ok")
        g_tr, g_got = sem("g_tr"), sem("g_got")
        ldt_in, ldt_ok, s5_col = sem("ldt_in"), sem("ldt_ok"), sem("s5_col")
        dt_ok, lrdt_ok, mag_ok = sem("dt_ok"), sem("lrdt_ok"), sem("mag_ok")
        phase_ok, trig_ok = sem("phase_ok"), sem("trig_ok")
        tab_ok, tab_used = sem("tab_ok"), sem("tab_used")
        bu_ok, bu_used, st_ok, st_used = sem("bu_ok"), sem("bu_used"), sem("st_ok"), sem("st_used")
        y_used, gelu_ok = sem("y_used"), sem("gelu_ok")
        mm_ok, mm_used = sem("mm_ok"), sem("mm_used")
        sq_ok = sem("sq_ok")
        conv_ok, spa_ok, spe_ok = sem("conv_ok"), sem("spa_ok"), sem("spe_ok")
        sp_ok, ta_ok, m2_ok, m_ok = sem("sp_ok"), sem("ta_ok"), sem("m2_ok"), sem("m_ok")
        mix_ok = sem("mix_ok")
        proj_ok, proj_got = sem("proj_ok"), sem("proj_got")

        SW = 256
        slabs = [(C_S5 + SW * i, SW) for i in range(C_R // SW)] + [(C_Z + SW * i, SW) for i in range((C_DT - C_Z) // SW)] \
            + [(C_LORA, LW + LA + LG)] + [(C_R + SW * i, SW) for i in range(3 * W // SW)]
        tiles = []
        for s, (c0, wd) in enumerate(slabs):
            parts = [(0, P), (P, P)] if wd == SW else [(0, LW + LA), (LW + LA, LG + SH)]
            for j, (c, w) in enumerate(parts):
                dest = c0 // P if c0 < C_LORA else (24 if c0 < C_Z else 26 + (c0 - C_Z) // P)
                tiles.append((s, c, w, dest + j))
        NT = len(tiles)
        proj_at = {d: n + 1 for n, (_, _, _, d) in enumerate(tiles)}

        U_GLU, U_RMS5, U_LRU, U_RMSL = 0, 4, 5, 13

        def ph(k):
            return wk[:, 2 * k:2 * k + 2, :].rearrange("p a n -> p (a n)")[:, 0:NPAIR * (FINE + COARSE)]\
                .rearrange("p (g k) -> p g k", g=NPAIR)

        def flat(x):
            return x.rearrange("p h t -> p (h t)")

        xtp_ok = sem("xtp_ok")
        passed = sem("passed")
        rbias = wide(94, 1)[:, 0:NG + NE]

        def wait_y_out(eng, r, k):
            if not isinstance(r, int) or r > 0:
                eng.wait_ge(y_out[k], 16 * r)

        def fbuf(i, j):
            return wide(4 * i) if j == 0 else wide(16 + 8 * i + 4 * (j - 1))

        gfin = wide(48)

        def OC(c, lv):
            return LEV * (c - c % 2) + 2 * lv + c % 2 + 1

        block = ctx.enter_context(nc.Block())

        @block.sync
        def _(sp):
            for i in range(NTT):
                sp.dma_start(xs[:, i, :], I["x"][0, P * i:P * (i + 1), :]).then_inc(x_in[i], 16)
            wv = I["w_in"][0].rearrange("(c p) n -> p c n", p=P)
            for s, (c0, wd) in enumerate(slabs):
                if s == 0:
                    sp.wait_ge(zero_ok, 1)
                    for tab, dst in ((PA, prmA), (PB, prmB)):
                        for name, (r, n) in tab.items():
                            src = I[name]
                            flat = src.rearrange(" ".join("abcd"[:len(src.shape)]) + " -> (" + " ".join("abcd"[:len(src.shape)]) + ")")
                            if name == "rw_mu":
                                flat = flat[0:3 * W]
                            sp.dma_start(dst[r:r + n, :], flat.rearrange("(r c) -> r c", c=P)).then_inc(prm_in, 16)
                    mu = I["rw_mu"]
                    sp.dma_start(prmB[MU_LORA:MU_LORA + 1, 0:LW + LA], mu[:, 3 * W:3 * W + LW + LA]).then_inc(prm_in, 16)
                    sp.dma_start(prmB[MU_LORA + 1:MU_LORA + 2, 0:LG], mu[:, 3 * W + LW + LA:]).then_inc(prm_in, 16)
                if s == 5:
                    sp.wait_ge(g_tr, 8)
                    sp.dma_start(wglu, I["s5_w_glu"][0].rearrange("(k p) n -> p k n", p=P)).then_inc(wglu_in, 16)
                if s >= 2:
                    sp.wait_ge(proj_ok, max(n + 1 for n, t in enumerate(tiles) if t[0] == s - 2))
                sp.dma_start(ring[s % 2][:, :, 0:wd], wv[:, :, c0:c0 + wd]).then_inc(w_in_slot[s % 2], 16)
                if wd != SW:
                    sp.dma_start(ring[s % 2][:, :, wd:wd + SH], wv[:, :, C_DT:]).then_inc(wdt_in, 16)
            for to, src, there in ((moved[:, 4], V_, 1), (moved[:, 0], KR[:, 0], 2), (movedBK, BK_, 4), (moved[:, 1], KR[:, 1], 5)):
                sp.wait_ge(rw_ok, there)
                sp.dma_start(to, src[64:128]).then_inc(moved_in, 16)
            sp.dma_start(wco[:], wce[64:128]).then_inc(moved_in, 16)
            sp.wait_ge(mask_ok, 1)
            sp.dma_start(rmask[64:128], rmask[0:64]).then_inc(moved_in, 16)
            sp.wait_ge(ro_ok, 2 * NRC)
            wov = I["w_out"][0].rearrange("(c p) n -> p c n", p=P)
            for n in range(4):
                if n == 1:
                    sp.wait_ge(rwy_ok, WT)
                    for i in range(NTT):
                        sp.dma_start(x2[i], I["x"][0, P * i:P * (i + 1), :]).then_inc(x2_in, 16)
                if n >= 2:
                    b, i = at[("out", NTT * (n - 2) + 3)]
                    sp.wait_ge(full[b], i + 1)
                sp.dma_start(woslab[n % 2], wov[:, :, 512 * n:512 * n + 512]).then_inc(wo_in[n % 2], 16)
            for w, o in (("moe_w_group", 0), ("moe_w_expert", NG)):
                v_ = I[w][0].rearrange("(p c) n -> p c n", c=NC)
                sp.dma_start(wr[:, :, o:o + v_.shape[2]], v_).then_inc(wr_in, 16)
            for i in range(NTT):
                sp.wait_ge(x2_ok, 4 * NTT)
                sp.dma_start(x2d[P * i:P * i + P, :], x2[i]).then_inc(spill, 16)
                sp.wait_ge(h2_ok, i + 1)
                sp.dma_start(hd[P * i:P * i + P, :], h2p[i]).then_inc(spill, 16)
            sp.wait_ge(spill, 16 * 2 * NTT)
            sp.wait_ge(rowi_ok, 1)
            npairs = sp.value_load(rowi[0:1, P:P + 1], min_val=1, max_val=NBLK // 2)

            def load(r, k, first):
                e = sp.value_load(rowi[0:1, bass.ds(2 * r + k, 1)], min_val=0, max_val=NE - 1)
                if not first:
                    sp.wait_ge(up_ok, 2 * r + k - 1)
                for w, name in enumerate(("moe_w1", "moe_w3")):
                    if first and k == 0 and w == 1:
                        sp.wait_ge(tab_io, 16 * (2 * NTT + 2))
                    sp.dma_start(W13[k][w], I[name][0][bass.ds(e, 1)].rearrange("e (p c) f -> p (e c) f", c=NC)).then_inc(w1_in[k], 16)
                if not first:
                    sp.wait_ge(down_ok, 8 * r + 4 * k - 4)
                if first and k == 0:
                    sp.wait_ge(xg_in[0], 16)
                sp.dma_start(W2[k], I["moe_w2"][0][bass.ds(e, 1)].rearrange("e (c p) n -> p (e c) n", p=P)).then_inc(w2_in[k], 16)

            load(0, 0, True)
            sp.wait_ge(idx_ok, 1)
            load(0, 1, True)
            with sp.Fori(1, NBLK // 2) as r:
                with sp.If(r < npairs):
                    load(r, 0, False)
                    load(r, 1, False)
            sp.wait_ge(up_ok, npairs * 2)
            for i in range(NTT):
                sp.dma_start(fbuf(i, 0), x2d[P * i:P * i + P, :]).then_inc(x_in[i], 16)
            sp.dma_start(gfin, I["norm_final"].rearrange("(a d) -> a d", a=1).to_broadcast([P, D])).then_inc(gain_in, 16)
            sp.wait_ge(y_out[0], npairs * 16)
            sp.wait_ge(y_out[1], npairs * 16)
            for i in range(NTT):
                for k in range(2):
                    sp.dma_start(fbuf(i, 1 + k), yd[T * k + P * i:T * k + P * i + P, :]).then_inc(x_in[i], 16)
            for i in range(NTT):
                sp.wait_ge(fin_ok, i + 1)
                sp.dma_start(out[0, P * i:P * i + P, :], fbuf(i, 0)).then_inc(out_ok, 16)
            sp.wait_ge(out_ok, 16 * NTT)

        @block.gpsimd
        def _(pool):
            g = Steps(pool, pool_s)
            g.do(nc.gpsimd.memset(ident[:], 0.0))
            nc.gpsimd.memset(ones[:], 1.0)
            nc.gpsimd.memset(zero[:], 0.0)
            nc.gpsimd.memset(halfpi[:], 1.5707963267948966)
            nc.gpsimd.memset(misc[:, :], 0.0)
            nc.gpsimd.memset(prmA, 0.0)
            nc.gpsimd.memset(prmB, 0.0).then_inc(zero_ok, 1)
            nc.gpsimd.memset(lruW, 0.0).then_inc(zero_ok, 1)
            nc.gpsimd.memset(epsb[:], EPS)
            nc.gpsimd.memset(eps64[:], 64e-5)
            nc.gpsimd.iota(tk[:, 0:FINE], pattern=[[1, FINE]], base=0, channel_multiplier=0,
                           allow_small_or_imprecise_dtypes=True)
            nc.gpsimd.iota(tk[:, FINE:], pattern=[[FINE, COARSE]], base=0, channel_multiplier=0,
                           allow_small_or_imprecise_dtypes=True)
            nc.gpsimd.memset(s5C, 0.0)
            nc.gpsimd.memset(Gin[0], 0.0)
            nc.gpsimd.memset(Gin[1], 0.0).then_inc(gin_zero, 1)
            pool.wait_ge(gin_zero, 1)
            nc.gpsimd.affine_select(out=ident[:], in_=ident[:], compare_op=ALU.not_equal, fill=1.0, base=0,
                                    pattern=[[-1, P]], channel_multiplier=1).then_inc(const_ok, 1)
            nc.gpsimd.memset(tri[:], 1.0)
            nc.gpsimd.memset(maskneg[:], 0.0)
            nc.gpsimd.memset(rmask[0:64], 1.0)
            nc.gpsimd.memset(emask[:], 1.0)
            nc.gpsimd.memset(blk64[:], 0.0)
            g.do(nc.gpsimd.memset(misc[:, :], 0.0))
            g.settle()
            ge = ALU.is_ge
            g.do(nc.gpsimd.affine_select(out=tri[:], in_=tri[:], compare_op=ge, fill=0.0, base=0, pattern=[[1, P]], channel_multiplier=-1))
            g.do(nc.gpsimd.affine_select(out=maskneg[:], in_=maskneg[:], compare_op=ge, fill=-1e9, base=0, pattern=[[1, P]], channel_multiplier=-1))
            g.do(nc.gpsimd.affine_select(out=rmask[0:64, 0], in_=rmask[0:64, 0], compare_op=ge, fill=0.0, base=-1, pattern=[[1, 64]], channel_multiplier=-1))
            g.do(nc.gpsimd.affine_select(out=rmask[0:64, 1], in_=rmask[0:64, 1], compare_op=ge, fill=0.0, base=0, pattern=[[1, 64]], channel_multiplier=-1))
            g.do(nc.gpsimd.memset(blk64[0:64, 0:64], 1.0))
            g.settle()
            g.do(nc.gpsimd.memset(blk64[64:128, 64:128], 1.0))
            g.settle()
            for i in range(7):
                m = 2 ** i
                e = emask[:, i].rearrange("p (b m) -> p b m", m=m)
                g.do(nc.gpsimd.affine_select(out=e, in_=e, compare_op=ge, fill=0.0, base=0, pattern=[[-m, 64 // m], [0, m]], channel_multiplier=1))
                g.settle()
                g.do(nc.gpsimd.affine_select(out=e, in_=e, compare_op=ge, fill=0.0, base=m - 1, pattern=[[m, 64 // m], [0, m]], channel_multiplier=-1))
                g.settle()
            g.do(nc.gpsimd.tensor_tensor(tris[:], tri[:], ident[:], ALU.subtract))
            g.do(nc.gpsimd.tensor_tensor(lvm[:], emask[:, 1:7], emask[:, 0:6], ALU.subtract))
            g.settle()
            g.tell(nc.gpsimd.tensor_tensor(lvm[:], lvm[:], rmask[0:64, 0:1].to_broadcast([64, 6, 64]), ALU.mult), mask_ok, 1)
            g.settle()
            pool.wait_ge(bbar_ok, 1)
            for r in range(2):
                gv = Gin[r].rearrange("p a (b c) -> p a b c", b=4)
                bb = wk[:, r, 0:256].rearrange("p (a b h) -> p a b h", a=WT, b=4)
                for b in range(4):
                    for u in range(2):
                        last = nc.gpsimd.tensor_copy(gv[64 * u:64 * u + 64, :, b, 32 * b + 16 * u:32 * b + 16 * u + 16],
                                                     bb[64 * u:64 * u + 64, :, b, :])
            last.then_inc(gin_ok, 1)
            pool.wait_ge(gin_ok, 1)
            pool.wait_ge(trig_ok, 1)
            pool.wait_ge(tr_ok, NTT * 4)
            for p in range(NPAIR):
                fine = [m[:, p, 0:FINE].unsqueeze(1).to_broadcast([P, COARSE, FINE]) for m in (cosF, sinF)]
                coarse = [m[:, p, FINE:].unsqueeze(2).to_broadcast([P, COARSE, FINE]) for m in (cosF, sinF)]
                cosT, sinT = (s5tab[:, 2 * (p % 2) + r, :].rearrange("p (a b) -> p a b", a=COARSE) for r in range(2))
                t0, t1 = (ptmp[:, r, :].rearrange("p (a b) -> p a b", a=COARSE) for r in range(2))
                if p >= 2:
                    pool.wait_ge(tab_used, p - 1)
                g.do(nc.gpsimd.tensor_tensor(t0, coarse[0], fine[0], ALU.mult))
                g.do(nc.gpsimd.tensor_tensor(t1, coarse[1], fine[1], ALU.mult))
                g.settle()
                g.do(nc.gpsimd.tensor_tensor(cosT, t0, t1, ALU.subtract))
                g.settle()
                g.do(nc.gpsimd.tensor_tensor(t0, coarse[1], fine[0], ALU.mult))
                g.do(nc.gpsimd.tensor_tensor(t1, coarse[0], fine[1], ALU.mult))
                g.settle()
                g.tell(nc.gpsimd.tensor_tensor(sinT, t0, t1, ALU.add), tab_ok, p + 1)
                g.settle()
            for c0 in range(0, NRC, 2):
                for lv in range(LEV):
                    for c in (c0, c0 + 1):
                        if lv == 0:
                            for k in range(2):
                                b, i = at[("gram", c, k)]
                                pool.wait_ge(free[b], i + 1)
                            if c >= 2:
                                pool.wait_ge(ro_ok, 2 * (c - 1))
                        elif lv > 1:
                            b, i = at[("t", c, lv - 2)]
                            pool.wait_ge(free[b], i + 1)
                        g.tell(nc.gpsimd.tensor_tensor(OF(c, lv), rb(c, "G")[0:64, :, 0, :], lvm[:, lv:lv + 1, :].to_broadcast([64, RH, 64]),
                                                       ALU.mult), of_ok, OC(c, lv))
                        if lv == 1:
                            g.settle()
                            g.do(nc.gpsimd.memset(rb(c, "UV")[0:64].rearrange("p h t -> p (h t)"), 0.0))
                            g.settle()

            b, i = at[("out", 4 * NTT - 1)]
            pool.wait_ge(free[b], i + 1)
            pool.wait_ge(full[at["logit"][0]], at["logit"][1] + 1)
            fl = dict(allow_small_or_imprecise_dtypes=True)
            nc.gpsimd.iota(rv(0, 8), pattern=[[1, 8]], base=0, channel_multiplier=0, **fl)
            nc.gpsimd.iota(rv(1, NE), pattern=[[1, NE]], base=0, channel_multiplier=0, **fl)
            nc.gpsimd.iota(rv(2, 8), pattern=[[B, 8]], base=0, channel_multiplier=0, **fl)
            nc.gpsimd.iota(rv(3, 1), pattern=[[0, 1]], base=0, channel_multiplier=1, **fl)
            nc.gpsimd.iota(tokv, pattern=[[T, 2], [P, NTT]], base=0, channel_multiplier=1)
            nc.gpsimd.memset(tini, NROW)
            g.tell(nc.gpsimd.memset(rv(0, 320)[:, 8:9], 0.0), ri_ok, 1)
            g.settle()
            pool.dma_start(tokd.rearrange("(b r) o -> b (r o)", r=B), tini).then_inc(tab_io, 16)
            pool.wait_ge(dest_ok, 1)
            pool.wait_ge(tab_io, 16)
            for k in range(2):
                for i in range(NTT):
                    nc.gpsimd.indirect_dma_start(tokd, bass.IndirectOffsetOnAxis(ap=desti[:, k, i:i + 1], axis=0),
                                                 tokv[:, k, i:i + 1], None).then_inc(tab_io, 16)
            pool.wait_ge(spill, 16 * 2 * NTT)
            for k in range(2):
                g.tell(nc.gpsimd.memset(xg[k], 0.0), xz_ok, k + 1)
            g.settle()
            pool.wait_ge(tab_io, 16 * (2 * NTT + 1))
            pool.dma_start(tabi, tokd.rearrange("(b r) o -> b (r o)", r=B)).then_inc(tab_io, 16)
            pool.wait_ge(idx_ok, 1)
            pool.wait_ge(rowi_ok, 1)
            npairs = pool.value_load(rowi[0:1, P:P + 1], min_val=1, max_val=NBLK // 2)

            def gather(r, k, first):
                if not first:
                    pool.wait_ge(xtp_ok, 4 * (r - 1) + 2 * k + 2)
                    pool.sem_inc(passed, 1)
                nc.gpsimd.tensor_copy(gix[k][:], idxg[:, bass.ds(2 * r + k, 1)]).then_inc(gcp_ok[k], 1)
                pool.wait_ge(gcp_ok[k], 1 if first else 2 * r)
                pool.sem_inc(passed, 1)
                nc.gpsimd.indirect_dma_start(xg[k], None, hd, bass.IndirectOffsetOnAxis(ap=gix[k][:, 0:1], axis=0),
                                             bounds_check=T - 1, oob_is_err=False).then_inc(xg_in[k], 16)

            def scatter(r, k):
                pool.wait_ge(y_ok[k], 4 * r + 4)
                pool.sem_inc(passed, 1)
                nc.gpsimd.tensor_copy(six[k][:], idxs[:, bass.ds(2 * r + k, 1)]).then_inc(gcp_ok[k], 1)
                pool.wait_ge(gcp_ok[k], 2 * r + 3)
                pool.sem_inc(passed, 1)
                nc.gpsimd.indirect_dma_start(yd, bass.IndirectOffsetOnAxis(ap=six[k][:, 0:1], axis=0), yb[k], None,
                                             bounds_check=2 * T - 1, oob_is_err=False).then_inc(y_out[k], 16)

            gather(0, 0, True)
            gather(0, 1, True)

            def pair(r):
                for k in range(2):
                    gather(r + 1, k, False)
                    scatter(r, k)

            pair(0)
            with pool.Fori(1, NBLK // 2) as r:
                with pool.If(r < npairs):
                    pair(r)

        @block.scalar
        def _(act):
            a = Steps(act, act_s)
            act.wait_ge(zero_ok, 1)
            act.dma_start(ldt[:], I["s5_log_dt"][0].rearrange("(g u) -> g u", u=2)).then_inc(ldt_in, 16)
            act.dma_start(prmC[16:32, :], I["s5_lambda_re"][0].rearrange("(g u) n -> g (u n)", u=2)).then_inc(s5_in, 16)
            act.dma_start(prmC[32:48, :], I["s5_lambda_im"][0].rearrange("(g u) n -> g (u n)", u=2)).then_inc(s5_in, 16)
            for r, w in enumerate(("s5_b_re", "s5_b_im")):
                act.dma_start(rawB[:, r], I[w][0].rearrange("(g u) n h -> (u n) g h", u=2)).then_inc(s5_in, 16)
            for r, w in enumerate(("s5_c_re", "s5_c_im")):
                for u in range(2):
                    act.dma_start(dupC[:, r, :, u, :], I[w][0].rearrange("(q g) h n -> (g h) q n", q=WT)).then_inc(s5_in, 16)
            for i in range(NTT):
                act.wait_ge(x_in[i], 16)
                nc.scalar.activation(hT[:, 0:4, :].rearrange("p a n -> p (a n)"), xs[:, i, :], ACT.Square,
                                     accum_out=st[:, i:i + 1]).then_inc(ssq_ok, 1)
                act.wait_ge(ssq_ok, i + 1)
            for k, w in enumerate(("ssd_dt_bias", "ssd_a_log", "ssd_d")):
                act.dma_start(cbc[:, k, :], I[w].to_broadcast([P, SH])).then_inc(cbc_in, 16)
            act.dma_start(loraW[0:LW, 0, :], I["rw_w2"][0]).then_inc(lora_in, 16)
            act.dma_start(loraW[LW:LW + LA, 0, :], I["rw_a2"][0]).then_inc(lora_in, 16)
            act.dma_start(loraW[0:LG, 1, :], I["rw_g2"][0]).then_inc(lora_in, 16)
            act.wait_ge(zero_ok, 2)
            for r, w in enumerate(("lru_wa", "lru_wx")):
                wv = I[w][0].rearrange("(t u) i j -> u i t j", u=2)
                for u in range(2):
                    act.dma_start(lruW[64 * u:64 * u + 64, r, :, 64 * u:64 * u + 64], wv[u]).then_inc(lruw_in, 16)
            act.wait_ge(ms_ok, 1)
            nc.scalar.activation(st[:, 8:12], st[:, 4:8], ACT.Sqrt).then_inc(rs_ok, 1)
            act.wait_ge(s5_col, 1)
            nc.scalar.activation(s5v[:, 0, :], colC[:, 0:16], ACT.Exp).then_inc(dt_ok, 1)
            act.wait_ge(lrdt_ok, 1)
            nc.scalar.activation(s5v[:, 2, :], s5v[:, 1, :], ACT.Exp).then_inc(mag_ok, 1)
            act.wait_ge(phase_ok, 2)
            nc.scalar.activation(sinF, ph(2), ACT.Sin, scale=6.283185)
            nc.scalar.activation(cosF, ph(3), ACT.Sin, scale=6.283185).then_inc(trig_ok, 1)
            act.wait_ge(spa_ok, 1)
            nc.scalar.activation(lsp[:, 1, :], lsp[:, 0, :], ACT.Exp, scale=-1.0).then_inc(spe_ok, 1)
            def s5_setup():
                for n in range(8):
                    act.wait_ge(g_tr, n + 1)
                    nc.scalar.activation(s5G.rearrange("p r g c -> p (r g c)")[:, 512 * n:512 * n + 512], ps[2 + n % 4][:], ACT.Copy).then_inc(g_got, 1)
                for r in range(2):
                    act.wait_ge(g_tr, 9 + r)
                    for u in range(2):
                        src = ps[2 + r][64 * u:64 * u + 64, :].rearrange("p (g u h) -> p g u h", u=2, h=S5_H)[:, :, u, :]
                        last = nc.scalar.activation(s5C[64 * u:64 * u + 64, r, :, 16 * u:16 * u + 16], src, ACT.Copy,
                                                    scale=1.0 - 2.0 * r)
                    last.then_inc(g_got, 1)

            def proj_out(n):
                s, c, wd, d = tiles[n]
                act.wait_ge(proj_ok, n + 1)
                nc.scalar.activation(proj[0:wd, d, :], ps[n % 2][0:wd, :], ACT.Copy).then_inc(proj_got, 1)

            def use(u, out, func, **kw):
                act.wait_ge(mm_ok, u + 1)
                nc.scalar.activation(out, ps[2 + u % 4][:], func, **kw).then_inc(mm_used, 1)

            def s5_gelu():
                act.wait_ge(y_used, WT)
                nc.scalar.activation(U5, U5, ACT.Gelu_apprx_tanh).then_inc(gelu_ok, 1)

            def s5_glu():
                for q in range(WT):
                    use(U_GLU + q, wk2[:, q, :], ACT.Sigmoid, bias=A("s5_b_glu", q))

            def lru_gates():
                for q in range(WT):
                    use(U_LRU + 2 * q, XL[:, q, :], ACT.Sigmoid, bias=A("lru_ba", q))
                    use(U_LRU + 2 * q + 1, wk[:, 4 + q, :], ACT.Sigmoid, bias=A("lru_bx", q))
                act.wait_ge(sp_ok, 1)
                act.wait_ge(mm_used, U_LRU + 8)
                for q in range(WT):
                    nc.scalar.activation(wk2[:, 4 + q, :], XL[:, q, :], ACT.Tanh, scale=lsp[:, 4, q:q + 1]).then_inc(ta_ok, 1)
                act.wait_ge(ta_ok, 4)
                for q in range(WT):
                    nc.scalar.activation(XL[:, q, :], XL[:, q, :], ACT.Exp, scale=lsp[:, 5, q:q + 1]).then_inc(ta_ok, 1)
                act.wait_ge(m2_ok, 1)
                nc.scalar.activation(wk2[:, 4:8, :], wk2[:, 4:8, :], ACT.Sqrt).then_inc(m_ok, 1)
                nc.scalar.activation(GL, GL, ACT.Gelu_apprx_tanh).then_inc(m_ok, 1)

            def rms(u, scratch):
                use(u, scratch, ACT.Sqrt, bias=epsb[:], scale=1.0 / W)

            def take(name, out, func=ACT.Copy, part=slice(0, P), cols=slice(0, 512), **kw):
                b, i = at[name]
                act.wait_ge(full[b], i + 1)
                nc.scalar.activation(out, ps[b][part, cols], func, **kw).then_inc(free[b], 1)

            def ssd_small():
                act.wait_ge(dtx_ok, 1)
                nc.scalar.activation(sds[:, 1, :], sds[:, 0, :], ACT.Exp, scale=-1.0).then_inc(dte_ok, 1)
                act.wait_ge(cbc_in, 48)
                nc.scalar.activation(cbc[:, 3, :], cbc[:, 1, :], ACT.Exp).then_inc(dte_ok, 1)
                act.wait_ge(csd_ok, 1)
                nc.scalar.activation(sds[:, 4:7, :], sds[:, 4:7, :], ACT.Exp).then_inc(cse_ok, 1)

            def ssd_silu():
                for j in range(8):
                    act.wait_ge(sconv_ok, j + 1)
                    nc.scalar.activation(XBC[:, j, :], wk[:, j % 4, :], ACT.Silu).then_inc(silu_ok, 1)
                nc.scalar.activation(Z_, Z_, ACT.Silu).then_inc(z_ok, 1)

            def ssd_tokens():
                for i in range(NTT):
                    take(("xt", i), XT_[:, i, :])
                for i in range(2):
                    take(("bt", i), BT.rearrange("p c g n -> p (c g n)")[:, 512 * i:512 * i + 512])

            def ssd_exp(c):
                act.wait_ge(seg_ok, c + 1)
                nc.scalar.activation(DM[:, c % 2], DM[:, c % 2], ACT.Exp).then_inc(segx_ok, 1)

            for n in range(NT):
                proj_out(n)
                if n == 3:
                    s5_setup()
                if n == 13:
                    s5_gelu()
                if n == 14:
                    s5_glu()
                if n == 15:
                    rms(U_RMS5, wk2[:, 0, :])
                if n == 16:
                    lru_gates()
                if n == 19:
                    rms(U_RMSL, wk2[:, 0, :])
                if n == 24:
                    ssd_silu()
                if n == 26:
                    ssd_small()
                if n == 27:
                    ssd_tokens()
                if n >= 28 and n % 2 == 0 and n < 28 + 2 * NSC:
                    ssd_exp((n - 28) // 2)
                if n == NT - 2:
                    act.wait_ge(lo_ok, 1)
                    nc.scalar.activation(LO[0:LW, 0, :], LO[0:LW, 0, :], ACT.Tanh).then_inc(lot_ok, 1)
                    nc.scalar.activation(LO[0:LG, 1, :], LO[0:LG, 1, :], ACT.Sigmoid).then_inc(lot_ok, 1)
            b, i = at["rms_s"]
            act.wait_ge(full[b], i + 1)
            nc.scalar.activation(zroot, ps[b][:], ACT.Sqrt, bias=epsb[:], scale=1.0 / W).then_inc(free[b], 1)

            for q in range(WT):
                take(("lora", q, 0), sg[:, q, :], ACT.Sigmoid, bias=A("rw_w0", q))
                take(("lora", q, 1), ra[:, q, :], ACT.Sigmoid, bias=A("rw_a0", q))
                take(("lora", q, 2), Gt[:, q, :])
            KAP = INV_SQRT_E
            act.wait_ge(cum_ok, 1)
            nc.scalar.activation(wcum, cum, ACT.Exp, scale=-KAP).then_inc(dec_ok, 1)
            nc.scalar.activation(winv, cum, ACT.Exp, scale=KAP).then_inc(dec_ok, 1)
            nc.scalar.activation(wprev, cumx, ACT.Exp, scale=-KAP).then_inc(dec_ok, 1)
            act.wait_ge(kn_ok, 1)
            nc.scalar.activation(knr, knr, ACT.Ln).then_inc(knr_ok, 1)
            act.wait_ge(knr_ok, 1)
            nc.scalar.activation(knr, knr, ACT.Exp, scale=-0.5).then_inc(knr_ok, 1)
            lo = slice(0, 64)

            def flat(x):
                return x.rearrange("p h t -> p (h t)")

            for c0 in range(0, NRC, 2):
                for c in (c0, c0 + 1):
                    if c >= 2:
                        act.wait_ge(ro_ok, 2 * (c - 1))
                    take(("tm", c, 0), flat(rb(c, "BK")))
                    b, i = at[("tm", c, 1)]
                    act.wait_ge(full[b], i + 1)
                    nc.scalar.activation(flat(rb(c, "UV")[64:128]), ps[b][lo, :], ACT.Copy).then_inc(free[b], 1)
                for lv in range(1, LEV):
                    for c in (c0, c0 + 1):
                        b, i = at[("t", c, lv)]
                        act.wait_ge(full[b], i + 1)
                        nc.scalar.activation(rb(c, "XT")[:, :, 1, :], ps[b][lo, :].rearrange("p (h t) -> p h t", h=RH),
                                             ACT.Copy).then_inc(free[b], 1)
                for c in (c0, c0 + 1):
                    take(("y", c), flat(RY), part=lo)
                    take(("un", c), flat(rb(c, "UV")[0:64]), part=lo, scale=-1.0)
                    b, i = at[("o", c)]
                    act.wait_ge(full[b], i + 1)
                    pv = ps[b][lo, :].rearrange("p (j o t) -> p o j t", o=2, t=RC)
                    nc.scalar.activation(Ot[0:64, :, RC * c:RC * c + RC], pv[:, 0], ACT.Copy).then_inc(ro_ok, 1)
                    nc.scalar.activation(Ot[64:128, :, RC * c:RC * c + RC], pv[:, 1], ACT.Copy).then_inc(free[b], 1)
                    act.wait_ge(free[b], i + 1)
                    nc.scalar.activation(misc[:, 4:5], misc[:, 5:6], ACT.Copy).then_inc(ro_ok, 1)
            for q in range(WT):
                take(("var", q), wk[:, q, :], ACT.Ln, bias=eps64[:], scale=1.0 / RD)
            for q in range(WT):
                b, i = at[("var", q)]
                act.wait_ge(free[b], i + 1)
                nc.scalar.activation(wk[:, q, :], wk[:, q, :], ACT.Exp, scale=-0.5).then_inc(var_ok, 1)
            act.dma_start(gffn, I["norm_ffn"].to_broadcast([P, D])).then_inc(gain_in, 16)
            for n in range(4 * NTT):
                ncol, i = divmod(n, NTT)
                cols = slice(512 * ncol, 512 * ncol + 512)
                act.wait_ge(x2_ok, n + 1)
                nc.scalar.activation(h2p[i][:, cols], x2[i][:, cols], ACT.Square,
                                     accum_out=st[:, 48 + 4 * i + ncol:49 + 4 * i + ncol]).then_inc(ssx_ok, 1)
            act.wait_ge(msx_ok, 1)
            nc.scalar.activation(st[:, 24:28], st[:, 20:24], ACT.Sqrt).then_inc(rsx_ok, 1)
            for m in range(4 * NTT):
                i, c4 = divmod(m, 4)
                b, n = at[("h2", m)]
                act.wait_ge(full[b], n + 1)
                nc.scalar.activation(h2T[:, 4 * c4:4 * c4 + 4, P * i:P * i + P], ps[b][:].rearrange("p (a n) -> p a n", a=4),
                                     ACT.Copy).then_inc(free[b], 1)
            act.dma_start(rbias[:, 0:NG], I["moe_b_group"].to_broadcast([P, NG])).then_inc(cbc_in, 16)
            act.dma_start(rbias[:, NG:], I["moe_b_expert"].to_broadcast([P, NE])).then_inc(cbc_in, 16)
            act.wait_ge(re_ok, 1)
            nc.scalar.activation(rv(6, NTT, NG), rv(6, NTT, NG), ACT.Exp).then_inc(re_ok, 1)
            act.wait_ge(re_ok, 3)
            nc.scalar.activation(gate[:, 1, :], gate[:, 1, :], ACT.Exp).then_inc(re_ok, 1)
            act.wait_ge(idx_ok, 1)
            act.wait_ge(rowi_ok, 1)
            act.wait_ge(spill, 16 * 2 * NTT)
            npairs = act.value_load(rowi[0:1, P:P + 1], min_val=1, max_val=NBLK // 2)

            def columns(r, k):
                act.wait_ge(xtp_ok, 4 * r + 2 * k + 1)
                nc.scalar.activation(xT[k][:, 0:8, :].rearrange("p c t -> p (c t)"), ps[0][:], ACT.Copy).then_inc(xT_ok, 1)

            def block_(r, k, nr, nk):
                act.wait_ge(up_ok, 2 * r + k + 1)
                nc.scalar.activation(sil[k], ps[2 + k][:, 0:FC * B], ACT.Silu).then_inc(sil_ok, 1)
                columns(nr, nk)
                for n in (0, 2):
                    act.wait_ge(down_ok, 8 * r + 4 * k + n + 1)
                    if n == 0 and k is not None:
                        wait_y_out(act, r, k)
                    nc.scalar.activation(yb[k][:, 512 * n:512 * n + 512], ps[4 + n][0:B, :], ACT.Copy).then_inc(y_ok[k], 1)

            columns(0, 0)
            block_(0, 0, 0, 1)
            block_(0, 1, 1, 0)
            with act.Fori(1, NBLK // 2) as r:
                with act.If(r < npairs):
                    block_(r, 0, r, 1)
                    block_(r, 1, r + 1, 0)
            for i in range(NTT):
                act.wait_ge(fsum_ok, i + 1)
                nc.scalar.activation(fbuf(i, 1), fbuf(i, 0), ACT.Square, accum_out=st[:, 32 + i:33 + i]).then_inc(fss_ok, 1)
                act.wait_ge(fss_ok, i + 1)
                nc.scalar.activation(st[:, 36 + i:37 + i], st[:, 32 + i:33 + i], ACT.Sqrt, bias=epsb[:], scale=1.0 / D).then_inc(frs_ok, 1)

        NPRM = 16 * (len(PA) + len(PB) + 2)

        @block.vector
        def _(dve):
            v = Steps(dve, dve_s)
            dve.wait_ge(ssq_ok, NTT)
            v.do(nc.vector.tensor_scalar(st[:, 12:16], st[:, 0:4], 1.0 / D, EPS, ALU.mult, ALU.add))
            v.settle()
            v.tell(nc.vector.reciprocal(st[:, 4:8], st[:, 12:16]), ms_ok, 1)
            dve.wait_ge(rs_ok, 1)
            for i in range(NTT):
                v.tell(nc.vector.tensor_scalar(xs[:, i, :], xs[:, i, :], st[:, 8 + i:9 + i], None, ALU.mult), h_ok, i + 1)
            dve.wait_ge(prm_tr, 1)
            nc.vector.tensor_copy(colA[:], ps[6][:, 0:128])
            nc.vector.tensor_copy(colB[:], ps[6][:, 128:256]).then_inc(prm_col, 1)
            dve.wait_ge(prm_col, 1)
            dve.wait_ge(ldt_in, 16)
            v.tell(nc.vector.tensor_copy(prmC[0:16, :].rearrange("p (u n) -> p u n", u=2),
                                         ldt[:].unsqueeze(2).to_broadcast([NPAIR, 2, S5_N])), ldt_ok, 1)
            dve.wait_ge(prm_tr, 2)
            v.tell(nc.vector.tensor_copy(colC[:], ps[7][:, 0:48]), s5_col, 1)
            v.settle()
            lr, li = colC[:, 16:32], colC[:, 32:48]
            ap4 = colA[:, PA["lru_a_param"][0]:PA["lru_a_param"][0] + WT]
            v.do(nc.vector.tensor_scalar(lsp[:, 2, :], ap4, -1.0, None, ALU.mult))
            v.settle()
            v.tell(nc.vector.tensor_tensor(lsp[:, 0, :], ap4, lsp[:, 2, :], ALU.max), spa_ok, 1)
            for m in range(NTT * 4):
                i, c4 = divmod(m, 4)
                dve.wait_ge(tr_ok, m + 1)
                g0 = PB["norm_mix"][0] + 4 * c4
                nc.vector.tensor_tensor(
                    hT[:, 4 * c4:4 * c4 + 4, P * i:P * (i + 1)], ps[2 + m % 4][:].rearrange("p (a n) -> p a n", a=4),
                    colB[:, g0:g0 + 4].to_broadcast([P, 4, P]), ALU.mult).then_inc(tr_used, 1)

            def op(out, a, b, o):
                v.do(nc.vector.tensor_tensor(out, a, b, o))

            def sc(out, a, s1, s2=None, o0=ALU.mult, o1=None):
                if s2 is None:
                    v.do(nc.vector.tensor_scalar(out, a, s1, None, o0))
                else:
                    v.do(nc.vector.tensor_scalar(out, a, s1, s2, o0, o1))

            MUL, ADD, SUB = ALU.mult, ALU.add, ALU.subtract
            S = [s5v[:, i, :] for i in range(16)]
            dve.wait_ge(dt_ok, 1)
            op(S[3], li, S[0], MUL)
            v.tell(nc.vector.tensor_tensor(S[1], lr, S[0], MUL), lrdt_ok, 1)
            v.settle()
            sc(S[4], S[3], 0.15915494309189535)
            v.settle()
            sc(S[5], S[4], MAGIC, MAGIC, ADD, SUB)
            v.settle()
            op(S[4], S[4], S[5], SUB)
            v.settle()
            sc(S[5], S[4], 16384.0, MAGIC, MUL, ADD)
            v.settle()
            sc(S[6], S[5], MAGIC, 1.0 / 16384.0, SUB, MUL)
            v.settle()
            op(S[7], S[4], S[6], SUB)
            v.settle()
            shp = [P, NPAIR, FINE + COARSE]
            tkb = tk[:].unsqueeze(1).to_broadcast(shp)
            op(ph(0), tkb, S[6].unsqueeze(2).to_broadcast(shp), MUL)
            op(ph(2), tkb, S[7].unsqueeze(2).to_broadcast(shp), MUL)
            v.settle()
            sc(ph(1), ph(0), MAGIC, MAGIC, ADD, SUB)
            v.settle()
            op(ph(0), ph(0), ph(1), SUB)
            v.settle()
            op(ph(0), ph(0), ph(2), ADD)
            v.settle()
            sc(ph(1), ph(0), MAGIC, MAGIC, ADD, SUB)
            v.settle()
            v.tell(nc.vector.tensor_tensor(ph(2), ph(0), ph(1), SUB), phase_ok, 1)
            v.settle()
            sc(ph(0), ph(0), 0.25, None, ADD)
            v.settle()
            sc(ph(1), ph(0), MAGIC, MAGIC, ADD, SUB)
            v.settle()
            v.tell(nc.vector.tensor_tensor(ph(3), ph(0), ph(1), SUB), phase_ok, 2)
            dve.wait_ge(trig_ok, 1)
            dve.wait_ge(mag_ok, 1)
            op(S[8], S[2], cosF[:, :, 1], MUL)
            op(S[9], S[2], sinF[:, :, 1], MUL)
            op(S[10], lr, lr, MUL)
            op(S[11], li, li, MUL)
            v.settle()
            sc(S[8], S[8], -1.0, None, ADD)
            op(S[10], S[10], S[11], ADD)
            v.settle()
            v.do(nc.vector.reciprocal(S[10], S[10]))
            op(S[11], S[8], lr, MUL)
            op(S[12], S[9], li, MUL)
            op(S[13], S[9], lr, MUL)
            op(S[14], S[8], li, MUL)
            v.settle()
            op(S[11], S[11], S[12], ADD)
            op(S[13], S[13], S[14], SUB)
            v.settle()
            op(S[11], S[11], S[10], MUL)
            op(S[13], S[13], S[10], MUL)
            v.settle()
            dve.wait_ge(s5_in, 16 * 8)
            w4 = [wk[:, r, 0:256].rearrange("p (g h) -> p g h", g=NPAIR) for r in range(4)]
            qre, qim = (S[i].unsqueeze(2).to_broadcast([P, NPAIR, S5_H]) for i in (11, 13))
            op(w4[0], rawB[:, 0], qre, MUL)
            op(w4[2], rawB[:, 1], qim, MUL)
            op(w4[1], rawB[:, 1], qre, MUL)
            op(w4[3], rawB[:, 0], qim, MUL)
            v.settle()
            op(w4[0], w4[0], w4[2], SUB)
            v.tell(nc.vector.tensor_tensor(w4[1], w4[1], w4[3], ADD), bbar_ok, 1)
            dve.wait_ge(spe_ok, 1)

            def log1p(out, e, s, s2):
                sc(out, e, 2.0, None, ADD)
                v.settle()
                v.do(nc.vector.reciprocal(out, out))
                v.settle()
                op(s, e, out, MUL)
                v.settle()
                op(s2, s, s, MUL)
                v.settle()
                sc(out, s2, 2.0 / 17, 2.0 / 15, MUL, ADD)
                for k in (13, 11, 9, 7, 5, 3, 1):
                    v.settle()
                    op(out, out, s2, MUL)
                    v.settle()
                    sc(out, out, 2.0 / k, None, ADD)
                v.settle()
                op(out, out, s, MUL)
                v.settle()

            log1p(lsp[:, 3, :], lsp[:, 1, :], lsp[:, 4, :], lsp[:, 5, :])
            v.do(nc.vector.scalar_tensor_tensor(out=lsp[:, 0, :], in0=lsp[:, 2, :], scalar=0.0, in1=lsp[:, 3, :],
                                                op0=ALU.max, op1=ALU.add))
            v.settle()
            sc(lsp[:, 4, :], lsp[:, 0, :], 8.0)
            v.tell(nc.vector.tensor_scalar(lsp[:, 5, :], lsp[:, 0, :], -8.0, None, MUL), sp_ok, 1)
            dve.wait_ge(gin_ok, 1)

            def s5_pair(p):
                bre, bim = ps[2 + 2 * (p % 2)][:], ps[3 + 2 * (p % 2)][:]
                cosT, sinT = s5tab[:, 2 * (p % 2), :], s5tab[:, 2 * (p % 2) + 1, :]
                k = [wk[:, i, :] for i in range(4)]
                xr, xi = wk[:, 4 + 2 * (p % 2), :], wk[:, 5 + 2 * (p % 2), :]
                dve.wait_ge(bu_ok, p + 1)
                dve.wait_ge(tab_ok, p + 1)
                v.settle()
                op(k[0], bre, cosT, MUL)
                op(k[1], bim, sinT, MUL)
                op(k[2], bim, cosT, MUL)
                v.tell(nc.vector.tensor_tensor(k[3], bre, sinT, MUL), bu_used, p + 1)
                v.settle()
                op(k[0], k[0], k[1], ADD)
                op(k[2], k[2], k[3], SUB)
                v.settle()
                mag = s5v[:, 2, p:p + 1].to_broadcast([P, T])
                v.do(nc.vector.tensor_tensor_scan(k[1], mag, k[0], 0.0, MUL, ADD))
                v.do(nc.vector.tensor_tensor_scan(k[3], mag, k[2], 0.0, MUL, ADD))
                v.settle()
                op(k[0], cosT, k[1], MUL)
                op(k[2], sinT, k[3], MUL)
                v.settle()
                if p >= 2:
                    dve.wait_ge(st_used, p - 1)
                op(xr, k[0], k[2], SUB)
                v.settle()
                op(k[0], sinT, k[1], MUL)
                v.tell(nc.vector.tensor_tensor(k[2], cosT, k[3], MUL), tab_used, p + 1)
                v.settle()
                v.tell(nc.vector.tensor_tensor(xi, k[0], k[2], ADD), st_ok, p + 1)

            def s5_y(q):
                dve.wait_ge(st_used, 4 * q + 4)
                v.tell(nc.vector.scalar_tensor_tensor(out=U5[:, q, :], in0=U5[:, q, :], scalar=A("s5_d", q),
                                                      in1=ps[6][:], op0=MUL, op1=ADD), y_used, q + 1)

            for p in range(NPAIR):
                s5_pair(p)
                if p % 4 == 1 and p > 1:
                    s5_y(p // 4 - 1)
            s5_y(WT - 1)
            v.settle()
            dve.wait_ge(proj_got, proj_at[7])

            def conv(out, src, name, q, rows, at):
                conv_to(conv_ok, out, src, name, q, rows, at)

            def conv_to(done, out, src, name, q, rows, at):
                col = (A if name == "lru" else Bc)
                v.do(nc.vector.tensor_scalar(out, src, col(name + "_conv_w", 3 * rows + q), col(name + "_conv_b", q), MUL, ADD))
                for sh in (1, 2, 3):
                    v.settle()
                    ins = nc.vector.scalar_tensor_tensor(out=out[:, sh:], in0=src[:, 0:T - sh],
                                                         scalar=col(name + "_conv_w", (3 - sh) * rows + q),
                                                         in1=out[:, sh:], op0=MUL, op1=ADD)
                    if sh < 3:
                        v.do(ins)
                    else:
                        v.tell(ins, done, at)

            dve.wait_ge(st_used, NPAIR)
            for q in range(WT):
                conv(wk[:, q, :], XL[:, q, :], "lru", q, WT, q + 1)
            v.settle()

            def rms(x, sq, scratch, u, k, gain):
                v.tell(nc.vector.tensor_tensor(sq, x, x, MUL), sq_ok, k + 1)
                dve.wait_ge(mm_used, u + 1)
                v.do(nc.vector.reciprocal(scratch, scratch))
                v.settle()
                for q in range(WT):
                    v.tell(nc.vector.scalar_tensor_tensor(out=x[:, q, :], in0=x[:, q, :], scalar=gain(q), in1=scratch,
                                                          op0=MUL, op1=MUL), mix_ok, WT * k + q + 1)

            dve.wait_ge(mm_used, U_GLU + WT)
            op(U5, U5, wk2[:, 0:4, :], MUL)
            v.settle()
            rms(U5, wk2[:, 4:8, :], wk2[:, 0, :], U_RMS5, 0, lambda q: A("s5_gain", q))
            v.settle()
            dve.wait_ge(mm_used, U_LRU + 8)
            op(wk[:, 0:4, :], wk[:, 0:4, :], wk[:, 4:8, :], MUL)
            v.settle()
            dve.wait_ge(ta_ok, 4)
            sc(wk[:, 4:8, :], wk2[:, 4:8, :], 1.0, None, ADD)
            v.settle()
            v.do(nc.vector.reciprocal(wk[:, 4:8, :], wk[:, 4:8, :]))
            v.settle()
            v.tell(nc.vector.scalar_tensor_tensor(out=wk2[:, 4:8, :], in0=wk2[:, 4:8, :], scalar=2.0, in1=wk[:, 4:8, :],
                                                  op0=MUL, op1=MUL), m2_ok, 1)
            dve.wait_ge(m_ok, 1)
            op(wk[:, 0:4, :], wk[:, 0:4, :], wk2[:, 4:8, :], MUL)
            v.settle()
            dve.wait_ge(ta_ok, 8)
            for q in range(WT):
                v.do(nc.vector.tensor_tensor_scan(wk[:, 4 + q, :], XL[:, q, :], wk[:, q, :], 0.0, MUL, ADD))
            v.settle()
            dve.wait_ge(m_ok, 2)
            op(XL, wk[:, 4:8, :], GL, MUL)
            v.settle()
            rms(XL, wk[:, 0:4, :], wk2[:, 0, :], U_RMSL, 1, lambda q: A("lru_gain", q))
            v.settle()

            def got(name):
                b, i = at[name]
                dve.wait_ge(full[b], i + 1)
                return ps[b], (free[b], i + 1)

            def shift(x, d, mus):
                n = x.shape[1]
                op(d[:, :, 1:], x[:, :, 0:T - 1], x[:, :, 1:], SUB)
                sc(d[:, :, 0:1], x[:, :, 0:1], -1.0)
                v.settle()
                for k in range(n):
                    v.do(nc.vector.scalar_tensor_tensor(out=x[:, k, :], in0=d[:, k, :], scalar=mus(k), in1=x[:, k, :], op0=MUL, op1=ADD))
                v.settle()

            def rw_mix(step):
                if step == 0:
                    for k, rows in enumerate((LW + LA, LG)):
                        dve.wait_ge(proj_got, proj_at[24 + k])
                        shift(LO[0:rows, k:k + 1, :], mixd[0:rows, k:k + 1, :], lambda _: colB[0:rows, MU_LORA + k:MU_LORA + k + 1])
                    v.tell(nc.vector.tensor_copy(misc[:, 6:7], misc[:, 7:8]), lo_ok, 1)
                else:
                    x = (R_, K_)[step - 1]
                    dve.wait_ge(proj_got, proj_at[12 + 4 * step - 1])
                    shift(x, mixd, lambda k: A("rw_mu", 4 * (step - 1) + k))

            for j in range(8):
                dve.wait_ge(proj_got, proj_at[30 + j])
                if j >= 4:
                    dve.wait_ge(silu_ok, j - 3)
                v.settle()
                conv_to(sconv_ok, wk[:, j % 4, :], XBC[:, j, :], "ssd", j, 8, j + 1)
            dve.wait_ge(cbc_in, 48)
            bias4, a4, d4 = (cbc[:, k:k + 1, :].to_broadcast([P, NSC, SH]) for k in (0, 3, 2))
            sd = [sds[:, k, :].rearrange("p (c h) -> p c h", h=SH) for k in range(8)]
            src, done = got("dt")
            v.tell(nc.vector.tensor_tensor(sd[2], src[:, 0:NSC * DTW].rearrange("p (c h) -> p c h", h=DTW)[:, :, LG:], bias4, ADD), *done)
            v.settle()
            sc(sd[3], sd[2], -1.0)
            v.settle()
            v.tell(nc.vector.tensor_tensor(sd[0], sd[2], sd[3], ALU.max), dtx_ok, 1)
            dve.wait_ge(dte_ok, 2)
            log1p(sds[:, 3, :], sds[:, 1, :], sds[:, 4, :], sds[:, 5, :])
            v.do(nc.vector.scalar_tensor_tensor(out=sds[:, 2, :], in0=sds[:, 2, :], scalar=0.0, in1=sds[:, 3, :], op0=ALU.max, op1=ADD))
            v.settle()
            op(sd[3], sd[2], a4, MUL)
            v.settle()
            v.tell(nc.vector.tensor_scalar(sds[:, 3, :], sds[:, 3, :], -1.0, None, MUL), adt_ok, 1)
            src, done = got("cs")
            v.settle()
            v.do(nc.vector.tensor_copy(sds[:, 7, :], src[:, 0:32]))
            v.do(nc.vector.tensor_copy(sds[:, 6, :], src[:, 32:64]))
            v.tell(nc.vector.tensor_copy(sds[:, 4, :], src[:, 0:32]), *done)
            v.settle()
            v.tell(nc.vector.tensor_tensor(sds[:, 5, :], sds[:, 6, :], sds[:, 7, :], SUB), csd_ok, 1)
            dve.wait_ge(cse_ok, 1)
            hs = [P, NSC, SH, 64]

            def heads(x):
                return x.rearrange("p c (h d) -> p c h d", h=SH)

            b, i = at[("xt", 3)]
            dve.wait_ge(free[b], i + 1)
            for c in range(NSC):
                op(XD[:, c, :].rearrange("p (h d) -> p h d", h=SH), XT_[:, c, :].rearrange("p (h d) -> p h d", h=SH),
                   sd[2][:, c].unsqueeze(2).to_broadcast([P, SH, 64]), MUL)
            v.settle()
            dve.wait_ge(silu_ok, 8)
            for c in range(NSC):
                v.tell(nc.vector.tensor_tensor(XE[:, c, :].rearrange("p (h d) -> p h d", h=SH), XD[:, c, :].rearrange("p (h d) -> p h d", h=SH),
                                               sd[5][:, c].unsqueeze(2).to_broadcast([P, SH, 64]), MUL), xe_ok, c + 1)
            for c in range(NSC):
                dm = DM[:, c % 2]
                if c >= 2:
                    b, i = at[("diag", c - 2)]
                    dve.wait_ge(full[b], i + 1)
                for k in range(2):
                    src, done = got(("row", c, k))
                    v.tell(nc.vector.tensor_tensor(dm[:, 4 * k:4 * k + 4], src[:].rearrange("p (h l) -> p h l", h=4),
                                                   sd[7][:, c, 4 * k:4 * k + 4].unsqueeze(2).to_broadcast([P, 4, P]), SUB), *done)
                    v.settle()
                v.tell(nc.vector.tensor_copy(misc[:, 6:7], misc[:, 7:8]), seg_ok, c + 1)
                src, done = got(("state", c))
                if c == 0:
                    v.tell(nc.vector.tensor_copy(SH_[:, 0, :], src[:]), *done)
                    v.settle()
                elif c < NSC - 1:
                    op(SH_[:, c % 2, :].rearrange("p (h d) -> p h d", h=SH), SH_[:, (c - 1) % 2, :].rearrange("p (h d) -> p h d", h=SH),
                       sd[6][:, c].unsqueeze(2).to_broadcast([P, SH, 64]), MUL)
                    v.settle()
                    v.tell(nc.vector.tensor_tensor(SH_[:, c % 2, :], SH_[:, c % 2, :], src[:], ADD), *done)
                    v.settle()
                else:
                    v.tell(nc.vector.tensor_copy(misc[:, 8:9], src[:, 0:1]), *done)
                    v.settle()
                dve.wait_ge(segx_ok, c + 1)
                src, done = got(("score", c))
                for k in range(2):
                    x = nc.vector.tensor_tensor(dm[:, 4 * k:4 * k + 4], dm[:, 4 * k:4 * k + 4],
                                                src[:, 128 * k:128 * k + 128].unsqueeze(1).to_broadcast([P, 4, P]), MUL)
                    if k:
                        v.tell(x, *done)
                v.settle()
                yt = YT[:, c, :].rearrange("p (h d) -> p h d", h=SH)
                op(yt, XT_[:, c, :].rearrange("p (h d) -> p h d", h=SH), cbc[:, 2, :].unsqueeze(2).to_broadcast([P, SH, 64]), MUL)
                v.settle()
                if c:
                    src, done = got(("off", c))
                    v.tell(nc.vector.tensor_tensor(XD[:, c - 1, :].rearrange("p (h d) -> p h d", h=SH), src[:].rearrange("p (h d) -> p h d", h=SH),
                                                   sd[4][:, c].unsqueeze(2).to_broadcast([P, SH, 64]), MUL), *done)
                    v.settle()
                    op(YT[:, c, :], YT[:, c, :], XD[:, c - 1, :], ADD)
                    v.settle()
                src, done = got(("diag", c))
                v.tell(nc.vector.tensor_tensor(YT[:, c, :], YT[:, c, :], src[:], ADD), *done)
                v.settle()
                if c:
                    rw_mix(c - 1)
                    v.settle()
            dve.wait_ge(z_ok, 1)
            for q in range(WT):
                src, done = got(("yt", q))
                v.tell(nc.vector.tensor_tensor(Z_[:, q, :], Z_[:, q, :], src[:], MUL), *done)
                v.settle()
            v.tell(nc.vector.tensor_tensor(wk2[:, 4:8, :], Z_, Z_, MUL), ssq2_ok, 1)

            dve.wait_ge(proj_got, NT)
            v.settle()

            dve.wait_ge(proj_ok, NT)
            for q in range(WT):
                sc(kk[:, q, :], K_[:, q, :], A("rw_k_k", q))
            v.settle()
            v.tell(nc.vector.tensor_tensor(knr, kk, kk, MUL), ksq_ok, 1)
            v.settle()
            v.do(nc.vector.memset(wk[:, 0, :], 1.0))
            v.settle()
            v.do(nc.vector.memset(wk[:, 0, :].rearrange("p (c t) -> p c t", t=RC)[:, :, 0:1], 0.0))
            for q in range(WT):
                b, i = at[("lora", q, 0)]
                dve.wait_ge(free[b], i + 1)
                v.settle()
                v.do(nc.vector.tensor_tensor_scan(cum[:, q, :], wk[:, 0, :], sg[:, q, :], 0.0, MUL, ADD))
            v.settle()
            v.tell(nc.vector.tensor_tensor(cumx, cum, sg, SUB), cum_ok, 1)
            b, i = at[("lora", 3, 1)]
            dve.wait_ge(free[b], i + 1)
            v.settle()
            for q in range(WT):
                sc(BV[:, q, :], ra[:, q, :], -1.0, A("rw_k_a", q), ADD, MUL)
            v.settle()
            v.do(nc.vector.scalar_tensor_tensor(out=K_, in0=BV, scalar=1.0, in1=K_, op0=ADD, op1=MUL))
            v.settle()
            for q in range(WT):
                v.tell(nc.vector.scalar_tensor_tensor(out=mixd[:, q, :], in0=R_[:, q, :], scalar=A("rw_r_k", q), in1=K_[:, q, :], op0=MUL, op1=MUL),
                       rk_ok, q + 1)
            v.settle()
            for q in range(WT):
                src, done = got(("kn", q))
                v.tell(nc.vector.tensor_scalar(knr[:, q, :], src[:], 1e-24, None, ALU.max), *done)
                v.settle()
            v.tell(nc.vector.tensor_copy(misc[:, 6:7], misc[:, 7:8]), kn_ok, 1)
            shift(V_, wk[:, 0:4, :], lambda k: A("rw_mu", 8 + k))
            dve.wait_ge(knr_ok, 2)
            op(kk, kk, knr, MUL)
            v.settle()
            op(ra, ra, kk, MUL)
            dve.wait_ge(dec_ok, 3)
            v.tell(nc.vector.tensor_copy(wce[:], wcum.rearrange("p j (c t) -> p j c t", t=RC)[:, :, :, RC - 1]), rw_ok, 1)
            v.settle()
            v.tell(nc.vector.tensor_tensor(KR[:, 0], kk, wprev, MUL), rw_ok, 2)
            for q in range(WT):
                b, i = at[("bonus", q)]
                dve.wait_ge(full[b], i + 1)
            for a, x in enumerate((ra, K_)):
                for j in range(WT):
                    ins = nc.vector.tensor_tensor(BK_[:, j, :, a, :], *(y[:, j, :].rearrange("p (c t) -> p c t", t=RC) for y in (x, winv)), MUL)
                    if j < WT - 1:
                        v.do(ins)
                v.tell(ins, rw_ok, 3 + a)
            v.tell(nc.vector.tensor_tensor(R_, R_, wcum, MUL), rw_ok, 5)
            v.settle()
            for q in range(WT):
                src, done = got(("bonus", q))
                v.tell(nc.vector.tensor_tensor(BV[:, q, :], V_[:, q, :], src[:], MUL), *done)
                v.settle()
            v.settle()
            v.do(nc.vector.memset(flat(RHS[0]), 0.0))
            b, i = at["rms_s"]
            dve.wait_ge(free[b], i + 1)
            v.do(nc.vector.reciprocal(zroot, zroot))
            v.settle()
            for q in range(WT):
                v.tell(nc.vector.scalar_tensor_tensor(out=Z_[:, q, :], in0=Z_[:, q, :], scalar=A("ssd_norm_w", q), in1=zroot,
                                                      op0=MUL, op1=MUL), mix_ok, 9 + q)
            v.settle()
            lo = slice(0, 64)
            I8 = ident[0:64, 0:64].unsqueeze(1).to_broadcast([64, RH, 64])
            dve.wait_ge(moved_in, 96)
            for c0 in range(0, NRC, 2):
                for c in (c0, c0 + 1):
                    if c >= 2:
                        dve.wait_ge(ro_ok, 2 * (c - 1))
                    for k in range(2):
                        src, done = got(("gram", c, k))
                        v.tell(nc.vector.tensor_tensor(rb(c, "G")[:, 4 * k:4 * k + 4].rearrange("p h a t -> p h (a t)"),
                                                       src[:].rearrange("p (h u) -> p h u", h=4),
                                                       rmask[:].rearrange("p a t -> p (a t)").unsqueeze(1).to_broadcast([P, 4, P]), MUL), *done)
                        v.settle()
                for lv in range(LEV):
                    for c in (c0, c0 + 1):
                        X, XT = rb(c, "X"), rb(c, "XT")[:, :, 0, :]
                        if lv == 0:
                            dve.wait_ge(of_ok, OC(c, 0))
                            op(XT, I8, OF(c, 0), SUB)
                            v.settle()
                            src, done = got(("t", c, 0))
                            v.tell(nc.vector.tensor_tensor(X, I8, src[lo, :].rearrange("p (h t) -> p h t", h=RH), SUB), *done)
                            v.settle()
                        else:
                            for k in range(2):
                                src, done = got(("u", c, lv, k))
                                g4 = slice(4 * k, 4 * k + 4)
                                u4 = src[:].rearrange("p (h a t) -> p h a t", h=4, a=2)
                                if lv < LEV - 1:
                                    op(X[:, g4], X[:, g4], u4[0:64, :, 1, :], SUB)
                                v.tell(nc.vector.tensor_tensor(XT[:, g4], XT[:, g4], u4[64:128, :, 0, :], SUB), *done)
                                v.settle()
                for c in (c0, c0 + 1):
                    src, done = got(("h", c))
                    now = RHS[(c + 1) % 2]
                    v.tell(nc.vector.tensor_tensor(flat(now), flat(RHS[c % 2]), src[lo, :], ADD), *done)
                    v.settle()
                    hv = now.rearrange("p (j o) v -> p o j v", o=2)
                    v.do(nc.vector.tensor_tensor(hv[:, 0], hv[:, 0], wce[0:64, :, c].unsqueeze(2).to_broadcast([64, WT, 64]), MUL))
                    v.tell(nc.vector.tensor_tensor(hv[:, 1], hv[:, 1], wco[:, :, c].unsqueeze(2).to_broadcast([64, WT, 64]), MUL), rh_ok, c + 1)
                    v.settle()
            dve.wait_ge(ro_ok, 2 * NRC)
            for q in range(WT):
                src, done = got(("mean", q))
                v.tell(nc.vector.scalar_tensor_tensor(out=Ot[:, q, :], in0=src[:], scalar=-1.0 / RD, in1=Ot[:, q, :], op0=MUL, op1=ADD), *done)
                v.settle()
                v.tell(nc.vector.tensor_tensor(wk[:, 4 + q, :], Ot[:, q, :], Ot[:, q, :], MUL), cen_ok, q + 1)
                v.settle()
            dve.wait_ge(var_ok, WT)
            for q in range(WT):
                v.do(nc.vector.scalar_tensor_tensor(out=Ot[:, q, :], in0=Ot[:, q, :], scalar=A("rw_ln_w", q), in1=wk[:, q, :], op0=MUL, op1=MUL))
            v.settle()
            for q in range(WT):
                v.do(nc.vector.scalar_tensor_tensor(out=Ot[:, q, :], in0=Ot[:, q, :], scalar=A("rw_ln_b", q), in1=BV[:, q, :], op0=ADD, op1=ADD))
            v.settle()
            for q in range(WT):
                v.tell(nc.vector.tensor_tensor(V_[:, q, :], Ot[:, q, :], Gt[:, q, :], MUL), rwy_ok, q + 1)

            for n in range(4 * NTT):
                ncol, i = divmod(n, NTT)
                src, done = got(("out", n))
                dve.wait_ge(x2_in, 16 * NTT)
                xc = x2[i][:, 512 * ncol:512 * ncol + 512]
                v.tell(nc.vector.tensor_tensor(xc, xc, src[:], ADD), *done)
                v.settle()
                v.tell(nc.vector.tensor_copy(misc[:, 6:7], misc[:, 7:8]), x2_ok, n + 1)
                v.settle()
            dve.wait_ge(ssx_ok, 4 * NTT)
            v.do(nc.vector.tensor_reduce(out=st[:, 16:20], in_=st[:, 48:64].rearrange("p (i n) -> p i n", i=NTT), op=ADD, axis=AX))
            v.settle()
            sc(st[:, 28:32], st[:, 16:20], 1.0 / D, EPS, MUL, ADD)
            v.settle()
            v.tell(nc.vector.reciprocal(st[:, 20:24], st[:, 28:32]), msx_ok, 1)
            dve.wait_ge(rsx_ok, 1)
            dve.wait_ge(gain_in, 16)
            v.settle()
            for i in range(NTT):
                v.tell(nc.vector.scalar_tensor_tensor(
                    out=h2p[i].rearrange("t (c p) -> t p c", p=P), in0=x2[i].rearrange("t (p c) -> t p c", c=NC),
                    scalar=st[:, 24 + i:25 + i], in1=gffn.rearrange("t (p c) -> t p c", c=NC), op0=MUL, op1=MUL), h2_ok, i + 1)

            def red(out, x, o):
                v.do(nc.vector.tensor_reduce(out=out, in_=x, op=o, axis=AX))

            def bc(x, n):
                return x.unsqueeze(2).to_broadcast([P, NTT, n])

            def first(idx, x, m, t):
                op(t, x, bc(m, 8), ALU.is_equal)
                v.settle()
                sc(t, t, -8.0, 8.0, MUL, ADD)
                v.settle()
                op(t, t, i8, ADD)
                v.settle()
                red(idx, t, ALU.min)
                v.settle()

            src, done = got("logit")
            dve.wait_ge(cbc_in, 80)
            dve.wait_ge(ri_ok, 1)
            L = rv(4, NTT, NG + NE)
            v.tell(nc.vector.tensor_tensor(L, src[:, 0:NTT * (NG + NE)].rearrange("p (i n) -> p i n", i=NTT),
                                           rbias.unsqueeze(1).to_broadcast([P, NTT, NG + NE]), ADD), *done)
            v.settle()
            i8 = rv(0, 8).unsqueeze(1).to_broadcast([P, NTT, 8])
            gl, el = L[:, :, 0:NG], L[:, :, NG:]
            t8, es, oh = rv(5, NTT, 8), rv(7, NTT, 8), rv(8, NTT, 8)
            sm = [rt[:, 5600 + 4 * j:5604 + 4 * j] for j in range(12)]
            gm, gi, gs, m1, i1, m2, i2, e1, e2 = sm[:9]
            red(gm, gl, ALU.max)
            v.settle()
            v.tell(nc.vector.tensor_tensor(rv(6, NTT, NG), gl, bc(gm, 8), SUB), re_ok, 1)
            first(gi, gl, gm, t8)
            dve.wait_ge(re_ok, 2)
            red(gs, rv(6, NTT, NG), ADD)
            v.settle()
            v.do(nc.vector.reciprocal(gs, gs))
            op(oh, i8, bc(gi, 8), ALU.is_equal)
            v.settle()
            sel = rv(9, NTT, NG, NPG)
            for i in range(NTT):
                op(sel[:, i], el[:, i].rearrange("p (g j) -> p g j", g=NG), oh[:, i].unsqueeze(2).to_broadcast([P, NG, NPG]), MUL)
            v.settle()
            for i in range(NTT):
                red(es[:, i], sel[:, i].rearrange("p g j -> p j g"), ADD)
            v.settle()
            red(m1, es, ALU.max)
            v.settle()
            first(i1, es, m1, t8)
            op(oh, i8, bc(i1, 8), ALU.is_equal)
            v.settle()
            v.do(nc.vector.scalar_tensor_tensor(out=es, in0=oh, scalar=-1e30, in1=es, op0=MUL, op1=ADD))
            v.settle()
            red(m2, es, ALU.max)
            v.settle()
            first(i2, es, m2, t8)
            v.tell(nc.vector.tensor_tensor(gate[:, 1, :], m2, m1, SUB), re_ok, 3)
            v.do(nc.vector.scalar_tensor_tensor(out=e1, in0=gi, scalar=8.0, in1=i1, op0=MUL, op1=ADD))
            v.do(nc.vector.scalar_tensor_tensor(out=e2, in0=gi, scalar=8.0, in1=i2, op0=MUL, op1=ADD))
            v.settle()
            i64 = rv(1, NE).unsqueeze(1).to_broadcast([P, NTT, NE])
            op(rv(10, NTT, NE), i64, bc(e1, NE), ALU.is_equal)
            op(rv(11, NTT, NE), i64, bc(e2, NE), ALU.is_equal)
            v.settle()
            v.tell(nc.vector.tensor_tensor(rv(12, NTT, NE), rv(10, NTT, NE), rv(11, NTT, NE), ADD), oh_ok, 1)
            dve.wait_ge(re_ok, 4)
            sc(gate[:, 0, :], gate[:, 1, :], 1.0, None, ADD)
            v.settle()
            v.do(nc.vector.reciprocal(gate[:, 0, :], gate[:, 0, :]))
            v.settle()
            op(gate[:, 0, :], gate[:, 0, :], gs, MUL)
            v.settle()
            op(gate[:, 1, :], gate[:, 1, :], gate[:, 0, :], MUL)
            src, done = got("cum")
            v.settle()
            v.do(nc.vector.tensor_copy(rv(13, 320), src[:, 0:320]))
            v.settle()
            cnt = rv(13, 320)[:, 256:320]
            c8 = rt[:, 320 * 14:320 * 14 + 512].rearrange("p (e j) -> p e j", e=NE)
            op(c8, cnt.unsqueeze(2).to_broadcast([P, NE, 8]), rv(2, 8).unsqueeze(1).to_broadcast([P, NE, 8]), ALU.is_gt)
            v.settle()
            nb, pend, pst = (rv(7, 320)[:, 32 + 64 * j:96 + 64 * j] for j in range(3))
            red(nb, c8, ADD)
            v.do(nc.vector.memset(rv(8, 320)[:, 64:128], 1.0))
            v.settle()
            v.do(nc.vector.tensor_tensor_scan(pend, rv(8, 320)[:, 64:128], nb, 0.0, MUL, ADD))
            v.settle()
            op(pst, pend, nb, SUB)
            sc(rv(9, NE), pend, rv(3, 1), None, ALU.is_le)
            v.settle()
            red(rv(3, 320)[:, 1:2], rv(9, NE), ADD)
            sc(pst, pst, float(B))
            v.settle()
            sc(rv(3, 320)[:, 1:2], rv(3, 320)[:, 1:2], float(NE - 1), None, ALU.min)
            v.settle()
            v.tell(nc.vector.tensor_copy(rv(3, 320)[:, 2:3], rv(3, 320)[:, 1:2]), bl_ok, 1)
            place = rv(13, 320)[:, 0:256].rearrange("p (i e) -> p i e", i=NTT)
            op(place, place, pst.unsqueeze(1).to_broadcast([P, NTT, NE]), ADD)
            v.settle()
            for k in range(2):
                op(rv(10 + k, NTT, NE), rv(10 + k, NTT, NE), place, MUL)
                v.settle()
                red(sm[9 + k], rv(10 + k, NTT, NE), ADD)
                v.settle()
                v.do(nc.vector.tensor_copy(desti[:, k, :], sm[9 + k]))
            v.settle()
            v.tell(nc.vector.tensor_copy(misc[:, 6:7], misc[:, 7:8]), dest_ok, 1)
            v.settle()
            src, done = got("row")
            v.do(nc.vector.tensor_copy(rowi[0:1, 0:P], src[0:1, 0:P]))
            v.settle()
            v.tell(nc.vector.tensor_copy(misc[:, 6:7], misc[:, 7:8]), *done)
            sc(sm[11][0:1, 0:1], pend[0:1, NE - 1:NE], 0.5, 0.25, MUL, ADD)
            v.settle()
            sc(sm[11][0:1, 1:2], sm[11][0:1, 0:1], MAGIC, MAGIC, ADD, SUB)
            v.settle()
            v.tell(nc.vector.tensor_copy(rowi[0:1, P:P + 1], sm[11][0:1, 1:2]), rowi_ok, 1)
            dve.wait_ge(tab_io, 16 * (2 * NTT + 2))
            v.tell(nc.vector.tensor_copy(tabf, tabi), tabf_ok, 1)
            src, done = got("tab")
            v.settle()
            v.do(nc.vector.memset(idxg[:, NBLK:NBLK + 2], NROW))
            v.do(nc.vector.tensor_copy(idxs[:, 0:NBLK], src[0:B, 0:NBLK]))
            sc(rt[0:B, 320:320 + NBLK], src[0:B, 0:NBLK], T - 0.5, -float(T), ALU.is_gt, MUL)
            v.settle()
            v.tell(nc.vector.tensor_tensor(rt[0:B, 640:640 + NBLK], rt[0:B, 320:320 + NBLK], src[0:B, 0:NBLK], ADD), *done)
            v.settle()
            v.tell(nc.vector.tensor_copy(idxg[:, 0:NBLK], rt[0:B, 640:640 + NBLK]), idx_ok, 1)
            v.settle()

            dve.wait_ge(spill, 16 * 2 * NTT)
            dve.wait_ge(rowi_ok, 1)
            npairs = dve.value_load(rowi[0:1, P:P + 1], min_val=1, max_val=NBLK // 2)

            def columns(r, k):
                dve.wait_ge(xtp_ok, 4 * r + 2 * k + 2)
                nc.vector.tensor_copy(xT[k][:, 8:16, :].rearrange("p c t -> p (c t)"), ps[1][:]).then_inc(xT2_ok, 1)

            def block_(r, k, nr, nk):
                dve.wait_ge(sil_ok, 2 * r + k + 1)
                nc.vector.tensor_tensor(hid[k].rearrange("p c t -> p (c t)"), sil[k], ps[2 + k][:, FC * B:2 * FC * B], MUL).then_inc(hid_ok, 1)
                columns(nr, nk)
                for n in (1, 3):
                    dve.wait_ge(down_ok, 8 * r + 4 * k + n + 1)
                    if n == 1:
                        wait_y_out(dve, r, k)
                    nc.vector.tensor_copy(yb[k][:, 512 * n:512 * n + 512], ps[4 + n][0:B, :]).then_inc(y_ok[k], 1)

            columns(0, 0)
            block_(0, 0, 0, 1)
            block_(0, 1, 1, 0)
            with dve.Fori(1, NBLK // 2) as r:
                with dve.If(r < npairs):
                    block_(r, 0, r, 1)
                    block_(r, 1, r + 1, 0)
            dve.wait_ge(gain_in, 32)
            for i in range(NTT + 1):
                if i < NTT:
                    xf, y0, y1 = (fbuf(i, j) for j in range(3))
                    dve.wait_ge(x_in[i], 64)
                    v.settle()
                    v.do(nc.vector.scalar_tensor_tensor(out=xf, in0=y0, scalar=gate[:, 0, i:i + 1], in1=xf, op0=MUL, op1=ADD))
                    v.settle()
                    v.tell(nc.vector.scalar_tensor_tensor(out=xf, in0=y1, scalar=gate[:, 1, i:i + 1], in1=xf, op0=MUL, op1=ADD), fsum_ok, i + 1)
                if i:
                    dve.wait_ge(frs_ok, i)
                    xf = fbuf(i - 1, 0)
                    v.do(nc.vector.reciprocal(st[:, 39 + i:40 + i], st[:, 35 + i:36 + i]))
                    v.settle()
                    v.tell(nc.vector.scalar_tensor_tensor(out=xf, in0=xf, scalar=st[:, 39 + i:40 + i], in1=gfin, op0=MUL, op1=MUL), fin_ok, i)

        @block.tensor
        def _(pe):
            pe.wait_ge(const_ok, 1)
            pe.wait_ge(prm_in, NPRM)
            nc.tensor.transpose(ps[6][:, 0:128], prmA, ident[:])
            nc.tensor.transpose(ps[6][:, 128:256], prmB, ident[:]).then_inc(prm_tr, 1)
            pe.wait_ge(ldt_ok, 1)
            pe.wait_ge(s5_in, 16 * 8)
            nc.tensor.transpose(ps[7][:, 0:48], prmC, ident[0:48, 0:48]).then_inc(prm_tr, 1)
            for m in range(NTT * 4):
                i, c4 = divmod(m, 4)
                if c4 == 0:
                    pe.wait_ge(h_ok, i + 1)
                if m >= 4:
                    pe.wait_ge(tr_used, m - 3)
                for j in range(4):
                    c = 4 * c4 + j
                    last = nc.tensor.transpose(ps[2 + m % 4][:, P * j:P * (j + 1)], xs[:, i, P * c:P * (c + 1)], ident[:])
                last.then_inc(tr_ok, 1)
            pe.wait_ge(tr_used, NTT * 4)

            def s5_setup():
                pe.wait_ge(gin_ok, 1)
                for n in range(8):
                    if n >= 4:
                        pe.wait_ge(g_got, n - 3)
                    for j in range(4):
                        last = nc.tensor.transpose(ps[2 + n % 4][:, P * j:P * j + P],
                                                   Gin[n // 4][:, n % 4, P * j:P * j + P], ident[:])
                    last.then_inc(g_tr, 1)
                for r in range(2):
                    pe.wait_ge(g_got, 5 + r)
                    for q in range(WT):
                        last = nc.tensor.transpose(ps[2 + r][:, P * q:P * q + P],
                                                   dupC[:, r, q].rearrange("p u n -> p (u n)"), ident[:])
                    last.then_inc(g_tr, 1)
                pe.wait_ge(g_got, 10)

            def s5_in_mm(p):
                if p >= 2:
                    pe.wait_ge(bu_used, p - 1)
                if p % 4 == 0:
                    pe.wait_ge(proj_got, p // 4 + 1)
                for r in range(2):
                    last = nc.tensor.matmul(ps[2 + 2 * (p % 2) + r][:], s5G[:, r, p, :], U5[:, p // 4, :], start=True, stop=True)
                last.then_inc(bu_ok, 1)

            def s5_out_mm(p):
                pe.wait_ge(st_ok, p + 1)
                if p % 4 == 0 and p:
                    pe.wait_ge(y_used, p // 4)
                o = ps[6][32 * (p % 4):32 * (p % 4) + 32, :]
                for r in range(2):
                    last = nc.tensor.matmul(o, s5C[:, r, p, :], wk[:, 4 + 2 * (p % 2) + r, :], start=(r == 0), stop=(r == 1))
                last.then_inc(st_used, 1)

            def s5_step(p):
                if 0 <= p < NPAIR:
                    s5_in_mm(p)
                if 2 <= p < NPAIR + 2:
                    s5_out_mm(p - 2)

            def bank(u):
                if u >= 4:
                    pe.wait_ge(mm_used, u - 3)
                return ps[2 + u % 4][:]

            def s5_glu():
                pe.wait_ge(gelu_ok, 1)
                pe.wait_ge(wglu_in, 16)
                for q in range(WT):
                    o = bank(U_GLU + q)
                    for k in range(WT):
                        last = nc.tensor.matmul(o, wglu[:, k, P * q:P * q + P], U5[:, k, :], start=(k == 0), stop=(k == WT - 1))
                    last.then_inc(mm_ok, 1)

            def rms(u, k, sq):
                pe.wait_ge(sq_ok, k + 1)
                o = bank(u)
                for q in range(WT):
                    last = nc.tensor.matmul(o, ones[:], sq[:, q, :], start=(q == 0), stop=(q == WT - 1))
                last.then_inc(mm_ok, 1)

            def lru_gates():
                pe.wait_ge(conv_ok, WT)
                pe.wait_ge(lruw_in, 64)
                for q in range(WT):
                    for r in range(2):
                        o = bank(U_LRU + 2 * q + r)
                        nc.tensor.matmul(o, lruW[:, r, q, :], wk[:, q, :], start=True, stop=True).then_inc(mm_ok, 1)

            def fill(name):
                b, i = at[name]
                if i:
                    pe.wait_ge(free[b], i)
                return ps[b], full[b]

            def ssd_dt():
                pe.wait_ge(proj_got, proj_at[25])
                pe.wait_ge(mm_used, U_RMSL + 1)
                o, done = fill("dt")
                for i in range(NTT):
                    last = nc.tensor.transpose(o[:, DTW * i:DTW * (i + 1)], LO[0:DTW, 1, P * i:P * (i + 1)], ident[0:DTW, 0:DTW])
                last.then_inc(done, 1)

            def ssd_cs():
                pe.wait_ge(adt_ok, 1)
                pe.wait_ge(mask_ok, 1)
                o, done = fill("cs")
                nc.tensor.matmul(o[:, 0:32], tri[:], sds[:, 3, :], start=True, stop=True)
                nc.tensor.matmul(o[:, 32:64], ones[:], sds[:, 3, :], start=True, stop=True).then_inc(done, 1)

            def ssd_tokens():
                pe.wait_ge(silu_ok, 8)
                for i in range(NTT):
                    o, done = fill(("xt", i))
                    for q in range(WT):
                        last = nc.tensor.transpose(o[:, P * q:P * q + P], XBC[:, q, P * i:P * i + P], ident[:])
                    last.then_inc(done, 1)
                for i in range(2):
                    o, done = fill(("bt", i))
                    for j in range(4):
                        c, g = 2 * i + j // 2, j % 2
                        last = nc.tensor.transpose(o[:, P * j:P * j + P], XBC[:, 4 + g, P * c:P * c + P], ident[:])
                    last.then_inc(done, 1)

            def ssd_chunk(c):
                cols = slice(P * c, P * c + P)
                for k in range(2):
                    o, done = fill(("row", c, k))
                    for j in range(4):
                        h = 4 * k + j
                        nc.tensor.matmul(o[:, P * j:P * j + P], sds[:, 3, SH * c + h:SH * c + h + 1].to_broadcast([P, P]), tri[:],
                                         start=True, stop=False)
                        last = nc.tensor.matmul(o[:, P * j:P * j + P], ident[:], maskneg[:], start=False, stop=True)
                    last.then_inc(done, 1)
                o, done = fill(("score", c))
                for g in range(2):
                    last = nc.tensor.matmul(o[:, P * g:P * g + P], XBC[:, 4 + g, cols], XBC[:, 6 + g, cols], start=True, stop=True)
                last.then_inc(done, 1)
                pe.wait_ge(xe_ok, c + 1)
                for i in range(2):
                    b, n = at[("bt", i)]
                    pe.wait_ge(free[b], n + 1)
                o, done = fill(("state", c))
                for g in range(2):
                    last = nc.tensor.matmul(o[:, 256 * g:256 * g + 256], BT[:, c, g, :], XE[:, c, 256 * g:256 * g + 256], start=True, stop=True)
                last.then_inc(done, 1)
                if c:
                    b, n = at[("state", c - 1)]
                    pe.wait_ge(free[b], n + 1)
                    o, done = fill(("off", c))
                    for g in range(2):
                        last = nc.tensor.matmul(o[:, 256 * g:256 * g + 256], XBC[:, 6 + g, cols], SH_[:, (c - 1) % 2, 256 * g:256 * g + 256],
                                                start=True, stop=True)
                    last.then_inc(done, 1)

            def ssd_diag(c):
                b, n = at[("score", c)]
                pe.wait_ge(free[b], n + 1)
                o, done = fill(("diag", c))
                for h in range(SH):
                    last = nc.tensor.matmul(o[:, 64 * h:64 * h + 64], DM[:, c % 2, h, :], XD[:, c, 64 * h:64 * h + 64], start=True, stop=True)
                last.then_inc(done, 1)

            def ssd_out():
                b, n = at[("diag", NSC - 1)]
                pe.wait_ge(free[b], n + 1)
                for q in range(WT):
                    o, done = fill(("yt", q))
                    for c in range(NSC):
                        last = nc.tensor.transpose(o[:, P * c:P * c + P], YT[:, c, P * q:P * q + P], ident[:])
                    last.then_inc(done, 1)

            for n, (s, c, wd, d) in enumerate(tiles):
                pe.wait_ge(w_in_slot[s % 2], 16 * (s // 2 + 1))
                if n >= 2:
                    pe.wait_ge(proj_got, n - 1)
                if n == 25:
                    pe.wait_ge(wdt_in, 16)
                for k in range(NC):
                    last = nc.tensor.matmul(ps[n % 2][0:wd, :], ring[s % 2][:, k, c:c + wd], hT[:, k, :],
                                            start=(k == 0), stop=(k == NC - 1))
                    if k == NC // 2 - 1:
                        s5_step(2 * n - 8)
                last.then_inc(proj_ok, 1)
                if n == 3:
                    s5_setup()
                s5_step(2 * n - 7)
                if n == 14:
                    s5_glu()
                if n == 15:
                    rms(U_RMS5, 0, wk2[:, 4:8, :])
                if n == 16:
                    lru_gates()
                if n == 19:
                    rms(U_RMSL, 1, wk[:, 0:4, :])
                if n == 26:
                    ssd_dt()
                if n == 27:
                    ssd_cs()
                    ssd_tokens()
                if n >= 28 and n % 2 == 0 and n < 28 + 2 * NSC:
                    ssd_chunk((n - 28) // 2)
                if n >= 29 and n % 2 and n < 29 + 2 * NSC:
                    ssd_diag((n - 29) // 2)
                if n == 28 + 2 * NSC:
                    ssd_out()
            assert NT > 28 + 2 * NSC

            pe.wait_ge(ssq2_ok, 1)
            o, done = fill("rms_s")
            for q in range(WT):
                last = nc.tensor.matmul(o[:], ones[:], wk2[:, 4 + q, :], start=(q == 0), stop=(q == WT - 1))
            last.then_inc(done, 1)

            pe.wait_ge(lot_ok, 2)
            pe.wait_ge(lora_in, 48)
            for q in range(WT):
                for r, (k0, k1, t) in enumerate(((0, LW, 0), (LW, LW + LA, 0), (0, LG, 1))):
                    o, done = fill(("lora", q, r))
                    nc.tensor.matmul(o[:], loraW[k0:k1, t, P * q:P * q + P], LO[k0:k1, t, :], start=True, stop=True).then_inc(done, 1)
            pe.wait_ge(ksq_ok, 1)
            for q in range(WT):
                o, done = fill(("kn", q))
                nc.tensor.matmul(o[:], blk64[:], knr[:, q, :], start=True, stop=True).then_inc(done, 1)
            for q in range(WT):
                pe.wait_ge(rk_ok, q + 1)
                o, done = fill(("bonus", q))
                nc.tensor.matmul(o[:], blk64[:], mixd[:, q, :], start=True, stop=True).then_inc(done, 1)
            pe.wait_ge(rw_ok, 5)
            pe.wait_ge(moved_in, 96)
            arr = {0: KR[:, 0], 1: KR[:, 1], 4: V_}

            def dims(a, h, c):
                cols = slice(RC * c, RC * c + RC)
                return arr[a][0:64, h // 2, cols] if h % 2 == 0 else moved[:, a, h // 2, cols]

            def dimsBK(h, c):
                return (BK_[0:64] if h % 2 == 0 else movedBK)[:, h // 2, c].rearrange("p a t -> p (a t)")

            def dims2(h, c):
                cols = slice(RC * c, RC * c + RC)
                return KR[0:64, :, h // 2, cols] if h % 2 == 0 else moved[:, 0:2, h // 2, cols]

            lo = slice(0, 64)

            def hd(o, h):
                return o[lo, 64 * h:64 * h + 64]

            for c0 in range(0, NRC, 2):
                for c in (c0, c0 + 1):
                    o, done = fill(("tm", c, 0))
                    for h in range(RH):
                        last = nc.tensor.transpose(o[:, 64 * h:64 * h + 64], dimsBK(h, c), ident[0:64, 0:64])
                    last.then_inc(done, 1)
                    o, done = fill(("tm", c, 1))
                    for h in range(RH):
                        last = nc.tensor.transpose(hd(o, h), dims(4, h, c), ident[0:64, 0:64])
                    last.then_inc(done, 1)
                    for k in range(2):
                        o, done = fill(("gram", c, k))
                        for h in range(4 * k, 4 * k + 4):
                            last = nc.tensor.matmul(o[:, P * (h % 4):P * (h % 4) + P], dimsBK(h, c), dims2(h, c), start=True, stop=True)
                        last.then_inc(done, 1)
                for lv in range(LEV):
                    for c in (c0, c0 + 1):
                        o, done = fill(("t", c, lv))
                        pe.wait_ge(of_ok, OC(c, lv))
                        if lv > 1:
                            for k in range(2):
                                b, i = at[("u", c, lv - 1, k)]
                                pe.wait_ge(free[b], i + 1)
                        for h in range(RH):
                            last = nc.tensor.matmul(hd(o, h), OF(c, lv)[:, h], rb(c, "X")[:, h] if lv else ident[0:64, 0:64], start=True, stop=True)
                        last.then_inc(done, 1)
                    for c in (c0, c0 + 1):
                        if lv:
                            b, i = at[("t", c, lv)]
                            pe.wait_ge(free[b], i + 1)
                            for k in range(2):
                                o, done = fill(("u", c, lv, k))
                                for h in range(4 * k, 4 * k + 4):
                                    both = rb(c, "XT")[:, h].rearrange("p a t -> p (a t)")
                                    last = nc.tensor.matmul(o[:, P * (h % 4):P * (h % 4) + P], both, both, start=True, stop=True)
                                last.then_inc(done, 1)
                for c in (c0, c0 + 1):
                    BK, UV, G, XT = (rb(c, k) for k in ("BK", "UV", "G", "XT"))
                    RHs = RHS[c % 2]
                    for k in range(2):
                        for name in (("tm", c, k), ("gram", c, k), ("u", c, LEV - 1, k)):
                            b, i = at[name]
                            pe.wait_ge(free[b], i + 1)
                    if c:
                        pe.wait_ge(rh_ok, c)
                    o, done = fill(("y", c))
                    for h in range(RH):
                        nc.tensor.matmul(hd(o, h), dims(0, h, c), RHs[:, h], start=True, stop=False)
                        last = nc.tensor.matmul(hd(o, h), G[:, h, 0], UV[:, h], start=False, stop=True)
                    last.then_inc(done, 1)
                    b, i = at[("y", c)]
                    pe.wait_ge(free[b], i + 1)
                    o, done = fill(("un", c))
                    for h in range(RH):
                        last = nc.tensor.matmul(hd(o, h), XT[:, h, 0], RY[:, h], start=True, stop=True)
                    last.then_inc(done, 1)
                    b, i = at[("un", c)]
                    pe.wait_ge(free[b], i + 1)
                    o, done = fill(("h", c))
                    for h in range(RH):
                        last = nc.tensor.matmul(hd(o, h), BK[:, h], UV[:, h], start=True, stop=True)
                    last.then_inc(done, 1)
                    o, done = fill(("o", c))
                    for h in range(RH):
                        nc.tensor.matmul(hd(o, h), RHs[:, h], dims(1, h, c), start=True, stop=False)
                        last = nc.tensor.matmul(hd(o, h), UV[:, h], G[:, h, 1], start=False, stop=True)
                    last.then_inc(done, 1)
            pe.wait_ge(ro_ok, 2 * NRC)
            for q in range(WT):
                o, done = fill(("mean", q))
                nc.tensor.matmul(o[:], blk64[:], Ot[:, q, :], start=True, stop=True).then_inc(done, 1)
            for q in range(WT):
                pe.wait_ge(cen_ok, q + 1)
                o, done = fill(("var", q))
                nc.tensor.matmul(o[:], blk64[:], wk[:, 4 + q, :], start=True, stop=True).then_inc(done, 1)

            pe.wait_ge(rwy_ok, WT)
            pe.wait_ge(mix_ok, 12)
            for n in range(4 * NTT):
                ncol, i = divmod(n, NTT)
                pe.wait_ge(wo_in[ncol % 2], 16 * (ncol // 2 + 1))
                o, done = fill(("out", n))
                for c in range(NC):
                    last = nc.tensor.matmul(o[:], mixed[c][:, P * i:P * i + P], woslab[ncol % 2][:, c, :], start=(c == 0), stop=(c == NC - 1))
                last.then_inc(done, 1)
            for m in range(4 * NTT):
                i, c4 = divmod(m, 4)
                pe.wait_ge(h2_ok, i + 1)
                o, done = fill(("h2", m))
                for j in range(4):
                    c = 4 * c4 + j
                    last = nc.tensor.transpose(o[:, P * j:P * j + P], h2p[i][:, P * c:P * c + P], ident[:])
                last.then_inc(done, 1)
            pe.wait_ge(wr_in, 32)
            for b in range(2, 6):
                pe.wait_ge(free[b], max(i for bb, i in at.values() if bb == b) + 1)
            o, done = fill("logit")
            for i in range(NTT):
                for c in range(NC):
                    last = nc.tensor.matmul(o[:, (NG + NE) * i:(NG + NE) * (i + 1)], h2T[:, c, P * i:P * i + P], wr[:, c, :],
                                            start=(c == 0), stop=(c == NC - 1))
            last.then_inc(done, 1)
            pe.wait_ge(oh_ok, 1)
            o, done = fill("cum")
            ohs = rv(12, NTT, NE)
            for i in range(NTT):
                oi = o[:, NE * i:NE * i + NE]
                nc.tensor.matmul(oi, tris[:], ohs[:, i, :], start=True, stop=(i == 0))
                for j in range(i):
                    nc.tensor.matmul(oi, ones[:], ohs[:, j, :], start=False, stop=(j == i - 1))
            for j in range(NTT):
                last = nc.tensor.matmul(o[:, NTT * NE:NTT * NE + NE], ones[:], ohs[:, j, :], start=(j == 0), stop=(j == NTT - 1))
            last.then_inc(done, 1)
            pe.wait_ge(bl_ok, 1)
            o, done = fill("row")
            nc.tensor.matmul(o[0:1, 0:P], rv(3, 320)[:, 2:3], ident[:], start=True, stop=True).then_inc(done, 1)
            pe.wait_ge(tabf_ok, 1)
            o, done = fill("tab")
            nc.tensor.transpose(o[0:B, 0:NBLK], tabf, ident[0:NBLK, 0:NBLK]).then_inc(done, 1)

            def keep_busy(times):
                for _ in range(times):
                    nc.tensor.matmul(ps[7][:, 0:P], ones[:], ones[:], start=True, stop=True)

            keep_busy(16)

            pe.wait_ge(idx_ok, 1)
            pe.wait_ge(rowi_ok, 1)
            pe.wait_ge(spill, 16 * 2 * NTT)
            npairs = pe.value_load(rowi[0:1, P:P + 1], min_val=1, max_val=NBLK // 2)

            def turn(r, k, first):
                pe.wait_ge(xg_in[k], 16 * (r + 1))
                if first:
                    pe.wait_ge(xz_ok, k + 1)
                for h in range(2):
                    if not (first and k == 0):
                        pe.wait_ge((xT_ok, xT2_ok)[h], 2 * r + k)
                    pe.sem_inc(passed, 1)
                    for j in range(8):
                        c = 8 * h + j
                        last = nc.tensor.transpose(ps[h][:, B * j:B * j + B], xg[k][:, P * c:P * c + P], ident[0:B, 0:B])
                    last.then_inc(xtp_ok, 1)

            def up(r, k, first):
                pe.wait_ge(w1_in[k], 32 * (r + 1))
                pe.wait_ge(xT_ok, 2 * r + k + 1)
                pe.wait_ge(xT2_ok, 2 * r + k + 1)
                if not first:
                    pe.wait_ge(hid_ok, 2 * r + k - 1)
                for w in range(2):
                    for m in range(FC):
                        o = ps[2 + k][:, B * (FC * w + m):B * (FC * w + m) + B]
                        for c in range(NC):
                            last = nc.tensor.matmul(o, W13[k][w][:, c, P * m:P * m + P], xT[k][:, c, :], start=(c == 0), stop=(c == NC - 1))
                last.then_inc(up_ok, 1)

            def down(r, k, first):
                pe.wait_ge(hid_ok, 2 * r + k + 1)
                pe.wait_ge(w2_in[k], 16 * (r + 1))
                for n in range(4):
                    if k == 1:
                        pe.wait_ge(y_ok[0], 4 * r + 4) if n == 0 else None
                    elif not first and n == 0:
                        pe.wait_ge(y_ok[1], 4 * r)
                    for c in range(FC):
                        last = nc.tensor.matmul(ps[4 + n][0:B, :], hid[k][:, c, :], W2[k][:, c, 512 * n:512 * n + 512],
                                                start=(c == 0), stop=(c == FC - 1))
                    last.then_inc(down_ok, 1)

            def pair(r, first):
                up(r, 0, first)
                turn(r, 1, first)
                down(r, 0, first)
                up(r, 1, first)
                turn(r + 1, 0, False)
                down(r, 1, first)

            turn(0, 0, True)
            keep_busy(8)
            pair(0, True)
            with pe.Fori(1, NBLK // 2) as r:
                with pe.If(r < npairs):
                    pair(r, False)


def kernel(**inputs):
    import numpy as _np
    import concourse.bacc as _bacc
    from concourse import mybir as _mybir
    from concourse.bass_utils import run_bass_kernel_spmd as _run

    nc = _bacc.Bacc("TRN2", target_bir_lowering=False, num_devices=1)
    arrays, aps = {}, {}
    for name, value in inputs.items():
        a = _np.ascontiguousarray(value)
        arrays[f"in_{name}"] = a
        aps[name] = nc.dram_tensor(f"in_{name}", a.shape, _mybir.dt.from_np(a.dtype), kind="ExternalInput").ap()
    dt = _mybir.dt.float32
    out = nc.dram_tensor("out_0", (1, 512, 2048), dt, kind="ExternalOutput").ap()
    build(nc, aps, out)
    r = _run(nc, [arrays], core_ids=[0])
    return r.results[0]["out_0"]
```
